# Optimizing a Trainium2 kernel written in Bass

```python
import jax
import jax.numpy as jnp
from jax import lax
import numpy as np

D_MODEL = 1024
BATCH = 1
SEQ = 1024
DEPTH = 2
DEC_BATCH = 8
DEC_SEQ = 4
PAST_LEN = 2048
PAGE_SIZE = 128

HEAD_DIM = 64
A_HEADS = 8
A_WIDTH = A_HEADS * HEAD_DIM
A_PATTERNS = ((128, 1), (512, 4), (2048, 16))
A_WIN_MAX = 2048
B_HEADS = 4
B_DK = 64
B_DV = 128
B_WIDTH = B_HEADS * B_DV
B_CHUNK = 128
ROPE_BASE = 10000.0
GN_EPS = 1e-5
C_HEADS = 16
C_KV_HEADS = 2
C_WIDTH = C_HEADS * HEAD_DIM
C_KV_WIDTH = C_KV_HEADS * HEAD_DIM
CMP_LEN = 32
CMP_STRIDE = 16
CMP_HIDDEN = 256
SEL_BLOCK = 64
SEL_TOPK = 16
SEL_FORCE = 1e9
C_WINDOW = 512
Q_BLOCK = 128
N_EVEN = (DEPTH + 1) // 2
N_ODD = DEPTH // 2
EVEN_SPLITS = (A_WIDTH, A_WIDTH, A_WIDTH, A_WIDTH, B_HEADS * B_DK, B_HEADS * B_DK, B_WIDTH, B_WIDTH)
D_IN_EVEN = 4 * A_WIDTH + 2 * B_HEADS * B_DK + 2 * B_WIDTH
D_MIX_EVEN = A_WIDTH + B_WIDTH
ODD_SPLITS = (C_WIDTH, C_KV_WIDTH, C_KV_WIDTH, C_KV_WIDTH, C_KV_WIDTH, C_KV_WIDTH, C_KV_WIDTH, 3 * C_HEADS, C_WIDTH)
D_IN_ODD = 2 * C_WIDTH + 6 * C_KV_WIDTH + 3 * C_HEADS
D_MIX_ODD = C_WIDTH
RMS_EPS = 1e-6
NEG_INF = -1e30

kernel_name = 'hybrid_dilated_retention_nsa_step'

def rmsnorm(x, g):
    xf = x.astype(jnp.float32)
    y = xf * lax.rsqrt(jnp.mean(xf * xf, axis=-1, keepdims=True) + RMS_EPS)
    return (y * g.astype(jnp.float32)).astype(x.dtype)

def split_cols(h, sizes):
    return jnp.split(h, np.cumsum(sizes)[:-1].tolist(), axis=-1)

def masked_softmax(s, mask):
    s = jnp.where(mask, s, NEG_INF)
    m = jnp.max(s, axis=-1, keepdims=True)
    p = jnp.where(mask, jnp.exp(s - m), 0.0)
    l = jnp.sum(p, axis=-1, keepdims=True)
    l = jnp.where(l > 0, l, 1.0)
    return p / l, (m + jnp.log(l))[..., 0]

def banded_attention(q, k, v, lookback):
    n, t, h, hd = q.shape
    g = k.shape[2]
    r = h // g
    blk = Q_BLOCK
    n_prev = -(-lookback // blk)
    t_pad = -(-t // blk) * blk
    span = (n_prev + 1) * blk
    q = jnp.pad(q, ((0, 0), (0, t_pad - t), (0, 0), (0, 0)))
    kv_pad = ((0, 0), (n_prev * blk, t_pad - t), (0, 0), (0, 0))
    k = jnp.pad(k, kv_pad)
    v = jnp.pad(v, kv_pad)
    scale = hd ** -0.5

    def one_block(start):
        qb = lax.dynamic_slice_in_dim(q, start, blk, axis=1).reshape(n, blk, g, r, hd)
        kb = lax.dynamic_slice_in_dim(k, start, span, axis=1)
        vb = lax.dynamic_slice_in_dim(v, start, span, axis=1)
        qpos = start + jnp.arange(blk)
        kpos = start - n_prev * blk + jnp.arange(span)
        dist = qpos[:, None] - kpos[None, :]
        mask = (kpos[None, :] >= 0) & (dist >= 0) & (dist <= lookback)
        s = jnp.einsum('nqgrd,nkgd->ngrqk', qb, kb, preferred_element_type=jnp.float32) * scale
        p, lse = masked_softmax(s, mask)
        o = jnp.einsum('ngrqk,nkgd->nqgrd', p, vb.astype(jnp.float32))
        return o.reshape(n, blk, h, hd), lse.transpose(0, 3, 1, 2).reshape(n, blk, h)

    o, lse = lax.map(one_block, jnp.arange(t_pad // blk) * blk)
    o = o.transpose(1, 0, 2, 3, 4).reshape(n, t_pad, h, hd)[:, :t]
    lse = lse.transpose(1, 0, 2, 3).reshape(n, t_pad, h)[:, :t]
    return o, lse

def gathered_window_attention(q, k_all, v_all, n_past, lookback, dilation):
    n, s_len, h, hd = q.shape
    g = k_all.shape[2]
    r = h // g
    n_keys = lookback // dilation + 1
    idx = n_past + np.arange(s_len)[:, None] - dilation * np.arange(n_keys)[None, :]
    valid = jnp.asarray(idx >= 0)
    idx = np.maximum(idx, 0)
    kg = k_all[:, idx]
    vg = v_all[:, idx]
    s = jnp.einsum('nqgrd,nqkgd->ngrqk', q.reshape(n, s_len, g, r, hd), kg,
                   preferred_element_type=jnp.float32) * hd ** -0.5
    p, lse = masked_softmax(s, valid)
    o = jnp.einsum('ngrqk,nqkgd->nqgrd', p, vg.astype(jnp.float32))
    return o.reshape(n, s_len, h, hd), lse.transpose(0, 3, 1, 2).reshape(n, s_len, h)

def merge_by_denominators(outs, lses):
    w = jax.nn.softmax(jnp.stack(lses, axis=0), axis=0)
    return jnp.einsum('pnth,pnthd->nthd', w, jnp.stack(outs, axis=0))

def dilated_attention_prompt(q, k, v):
    b, t, h, hd = q.shape
    outs, lses = [], []
    for window, dil in A_PATTERNS:
        n_sub = t // dil

        def to_residue(u):
            return u.reshape(b, n_sub, dil, h, hd).transpose(0, 2, 1, 3, 4).reshape(b * dil, n_sub, h, hd)

        o, lse = banded_attention(to_residue(q), to_residue(k), to_residue(v), window // dil)
        outs.append(o.reshape(b, dil, n_sub, h, hd).transpose(0, 2, 1, 3, 4).reshape(b, t, h, hd))
        lses.append(lse.reshape(b, dil, n_sub, h).transpose(0, 2, 1, 3).reshape(b, t, h))
    return merge_by_denominators(outs, lses)

def dilated_attention_sample(q, k_all, v_all, n_past):
    outs, lses = [], []
    for window, dil in A_PATTERNS:
        o, lse = gathered_window_attention(q, k_all, v_all, n_past, window, dil)
        outs.append(o)
        lses.append(lse)
    return merge_by_denominators(outs, lses)

def rotary(x, pos):
    half = x.shape[-1] // 2
    freqs = ROPE_BASE ** (-jnp.arange(half, dtype=jnp.float32) / half)
    ang = pos.astype(jnp.float32)[:, None] * freqs[None, :]
    cos = jnp.cos(ang)[None, :, None, :]
    sin = jnp.sin(ang)[None, :, None, :]
    xf = x.astype(jnp.float32)
    x1, x2 = xf[..., :half], xf[..., half:]
    return jnp.concatenate([x1 * cos - x2 * sin, x1 * sin + x2 * cos], axis=-1)

def retention(q, k, v, s0):
    n, t, h, dk = q.shape
    dv = v.shape[-1]
    c = B_CHUNK if t % B_CHUNK == 0 else t
    nc = t // c
    log_g = jnp.log1p(-jnp.exp2(-5.0 - jnp.arange(h, dtype=jnp.float32)))
    i = jnp.arange(c, dtype=jnp.float32)
    diff = i[:, None] - i[None, :]
    intra = jnp.where(diff >= 0, jnp.exp(log_g[:, None, None] * jnp.maximum(diff, 0.0)), 0.0)
    q_decay = jnp.exp(log_g[None, :] * (i[:, None] + 1.0))[None, :, :, None]
    k_decay = jnp.exp(log_g[None, :] * (c - 1.0 - i[:, None]))[None, :, :, None]
    chunk_decay = jnp.exp(log_g * c)[None, :, None, None]

    def to_chunks(u):
        return u.astype(jnp.float32).reshape(n, nc, c, h, u.shape[-1]).transpose(1, 0, 2, 3, 4)

    def step(state, inp):
        qc, kc, vc = inp
        scores = jnp.einsum('nqhd,nkhd->nhqk', qc, kc) * intra
        o = jnp.einsum('nhqk,nkhe->nqhe', scores, vc) + jnp.einsum('nqhd,nhde->nqhe', qc, state) * q_decay
        state = state * chunk_decay + jnp.einsum('nkhd,nkhe->nhde', kc * k_decay, vc)
        return state, o

    state, o = lax.scan(step, s0.astype(jnp.float32), (to_chunks(q), to_chunks(k), to_chunks(v)))
    return o.transpose(1, 0, 2, 3, 4).reshape(n, t, h, dv), state

def head_norm(o):
    mu = jnp.mean(o, axis=-1, keepdims=True)
    var = jnp.mean(jnp.square(o - mu), axis=-1, keepdims=True)
    return (o - mu) * lax.rsqrt(var + GN_EPS)

def layer_output(x, branches, w_out):
    mixed = jnp.concatenate(branches, axis=-1).astype(x.dtype)
    return x + mixed @ w_out

def even_project(x, norm_g, w_in):
    b, t, _ = x.shape
    qa, ka, va, za, qb, kb, vb, zb = split_cols(rmsnorm(x, norm_g) @ w_in, EVEN_SPLITS)
    a_heads = lambda u: u.reshape(b, t, A_HEADS, HEAD_DIM)
    b_heads = lambda u: u.reshape(b, t, B_HEADS, -1)
    return a_heads(qa), a_heads(ka), a_heads(va), za, b_heads(qb), b_heads(kb), b_heads(vb), zb

def even_output(x, oa, ob, za, zb, w_out):
    b, t, _ = x.shape
    ga = oa.reshape(b, t, A_WIDTH) * jax.nn.silu(za.astype(jnp.float32))
    gb = head_norm(ob).reshape(b, t, B_WIDTH) * jax.nn.silu(zb.astype(jnp.float32))
    return layer_output(x, [ga, gb], w_out)

def even_layer_prompt(x, norm_g, w_in, w_out):
    b, t, _ = x.shape
    qa, ka, va, za, qb, kb, vb, zb = even_project(x, norm_g, w_in)
    oa = dilated_attention_prompt(qa, ka, va)
    pos = jnp.arange(t)
    s0 = jnp.zeros((b, B_HEADS, B_DK, B_DV), jnp.float32)
    ob, s_fin = retention(rotary(qb, pos), rotary(kb, pos) * B_DK ** -0.5, vb, s0)
    keep = min(A_WIN_MAX, t)
    return even_output(x, oa, ob, za, zb, w_out), ka[:, t - keep:], va[:, t - keep:], s_fin

def even_layer_sample(x, cache_k, cache_v, state, norm_g, w_in, w_out):
    b, s_len, _ = x.shape
    qa, ka, va, za, qb, kb, vb, zb = even_project(x, norm_g, w_in)
    n_past = cache_k.shape[1]
    oa = dilated_attention_sample(qa, jnp.concatenate([cache_k, ka], axis=1),
                                  jnp.concatenate([cache_v, va], axis=1), n_past)
    pos = PAST_LEN + jnp.arange(s_len)
    ob, s_new = retention(rotary(qb, pos), rotary(kb, pos) * B_DK ** -0.5, vb, state)
    return even_output(x, oa, ob, za, zb, w_out), ka, va, s_new

def odd_project(x, norm_g, w_in):
    b, t, _ = x.shape
    q, kc, vc, ks, vs, kw, vw, gl, z = split_cols(rmsnorm(x, norm_g) @ w_in, ODD_SPLITS)
    kv = lambda u: u.reshape(b, t, C_KV_HEADS, HEAD_DIM)
    return q.reshape(b, t, C_HEADS, HEAD_DIM), kv(kc), kv(vc), kv(ks), kv(vs), kv(kw), kv(vw), gl, z

def odd_output(x, o_cmp, o_sel, o_win, gl, z, w_out):
    b, t, _ = x.shape
    gates = jax.nn.sigmoid(gl.astype(jnp.float32)).reshape(b, t, C_HEADS, 3, 1)
    o = gates[:, :, :, 0] * o_cmp + gates[:, :, :, 1] * o_sel + gates[:, :, :, 2] * o_win
    return layer_output(x, [o.reshape(b, t, C_WIDTH) * jax.nn.silu(z.astype(jnp.float32))], w_out)

def compress_blocks(kv, pos_emb, w1, w2):
    n, t, g, hd = kv.shape
    per = CMP_LEN // CMP_STRIDE
    n_cmp = (t - CMP_LEN) // CMP_STRIDE + 1
    pieces = kv[:, :CMP_STRIDE * (n_cmp + per - 1)].reshape(n, n_cmp + per - 1, CMP_STRIDE, g, hd)
    blocks = jnp.concatenate([pieces[:, j:j + n_cmp] for j in range(per)], axis=2)
    hid = jax.nn.silu(jnp.einsum('nilgd,ldf->nigf', blocks + pos_emb[None, None, :, None, :],
                                 w1.reshape(CMP_LEN, hd, CMP_HIDDEN)))
    return jnp.einsum('nigf,fd->nigd', hid, w2)

def select_blocks(kv):
    n, t, g, hd = kv.shape
    n_slc = -(-t // SEL_BLOCK)
    kv = jnp.pad(kv, ((0, 0), (0, n_slc * SEL_BLOCK - t), (0, 0), (0, 0)))
    return kv.reshape(n, n_slc, SEL_BLOCK, g, hd).transpose(0, 3, 1, 2, 4)

def nsa_compressed_selected(q, qpos, kc, vc, ks_b, vs_b):
    n, nq, h, hd = q.shape
    g = kc.shape[2]
    r = h // g
    n_cmp = kc.shape[1]
    n_slc = ks_b.shape[2]
    scale = hd ** -0.5
    qg = q.reshape(n, nq, g, r, hd)
    c_end = jnp.arange(n_cmp) * CMP_STRIDE + CMP_LEN - 1
    c_mask = c_end[None, :] <= qpos[:, None]
    s = jnp.einsum('nqgrd,ncgd->ngrqc', qg, kc, preferred_element_type=jnp.float32) * scale
    p, _ = masked_softmax(s, c_mask)
    o_cmp = jnp.einsum('ngrqc,ncgd->nqgrd', p, vc.astype(jnp.float32)).reshape(n, nq, h, hd)
    per = CMP_LEN // CMP_STRIDE
    ratio = SEL_BLOCK // CMP_STRIDE
    j_np = np.arange(n_slc)[:, None]
    i_np = ratio * j_np - (per - 1) + np.arange(ratio + per - 1)[None, :]
    overlap = (np.minimum(i_np * CMP_STRIDE + CMP_LEN, (j_np + 1) * SEL_BLOCK)
               - np.maximum(i_np * CMP_STRIDE, j_np * SEL_BLOCK))
    w_ov = np.where((i_np >= 0) & (i_np < n_cmp), np.clip(overlap, 0, None) / CMP_LEN, 0.0).astype(np.float32)
    imp = jnp.sum(p, axis=2)
    imp_g = jnp.take(imp, np.clip(i_np, 0, n_cmp - 1).reshape(-1), axis=-1).reshape(n, g, nq, n_slc, -1)
    p_slc = jnp.einsum('ngqjo,jo->ngqj', imp_g, w_ov)
    j = jnp.arange(n_slc)
    cur = qpos // SEL_BLOCK
    forced = (j[None, :] == 0) | (j[None, :] == cur[:, None]) | (j[None, :] == cur[:, None] - 1)
    causal = j[None, :] * SEL_BLOCK <= qpos[:, None]
    score = jnp.where(forced, SEL_FORCE, jnp.where(causal, p_slc, -SEL_FORCE))
    top_s, top_i = lax.top_k(score, min(SEL_TOPK, n_slc))
    n_sel = top_i.shape[-1]
    ni = jnp.arange(n)[:, None, None, None]
    gi = jnp.arange(g)[None, :, None, None]
    kg = ks_b[ni, gi, top_i].reshape(n, g, nq, n_sel * SEL_BLOCK, hd)
    vg = vs_b[ni, gi, top_i].reshape(n, g, nq, n_sel * SEL_BLOCK, hd)
    kpos = (top_i[..., None] * SEL_BLOCK + jnp.arange(SEL_BLOCK)).reshape(n, g, nq, n_sel * SEL_BLOCK)
    mask = jnp.repeat(top_s > -0.5 * SEL_FORCE, SEL_BLOCK, axis=-1) & (kpos <= qpos[None, None, :, None])
    s2 = jnp.einsum('nqgrd,ngqkd->ngrqk', qg, kg, preferred_element_type=jnp.float32) * scale
    p2, _ = masked_softmax(s2, mask[:, :, None])
    o_sel = jnp.einsum('ngrqk,ngqkd->nqgrd', p2, vg.astype(jnp.float32)).reshape(n, nq, h, hd)
    return o_cmp, o_sel

def odd_layer_prompt(x, norm_g, w_in, w_out, pos_k, w1_k, w2_k, pos_v, w1_v, w2_v):
    b, t, _ = x.shape
    q, kc, vc, ks, vs, kw, vw, gl, z = odd_project(x, norm_g, w_in)
    kcb = compress_blocks(kc, pos_k, w1_k, w2_k)
    vcb = compress_blocks(vc, pos_v, w1_v, w2_v)
    ksb = select_blocks(ks)
    vsb = select_blocks(vs)
    nb = t // Q_BLOCK
    q_blocks = q.reshape(b, nb, Q_BLOCK, C_HEADS, HEAD_DIM).transpose(1, 0, 2, 3, 4)
    pos_blocks = jnp.arange(t).reshape(nb, Q_BLOCK)
    o_cmp, o_sel = lax.map(lambda a: nsa_compressed_selected(a[0], a[1], kcb, vcb, ksb, vsb),
                           (q_blocks, pos_blocks))
    unblock = lambda o: o.transpose(1, 0, 2, 3, 4).reshape(b, t, C_HEADS, HEAD_DIM)
    o_win, _ = banded_attention(q, kw, vw, C_WINDOW)
    keep = min(C_WINDOW, t)
    y = odd_output(x, unblock(o_cmp), unblock(o_sel), o_win, gl, z, w_out)
    return y, kc, vc, ks, vs, kw[:, t - keep:], vw[:, t - keep:]

def odd_layer_sample(x, page_table, pool_kc, pool_vc, pool_ks, pool_vs, buf_kw, buf_vw,
                     norm_g, w_in, w_out, pos_k, w1_k, w2_k, pos_v, w1_v, w2_v):
    b, s_len, _ = x.shape
    q, kc, vc, ks, vs, kw, vw, gl, z = odd_project(x, norm_g, w_in)
    n_past = page_table.shape[1] * PAGE_SIZE

    def with_past(pool, new):
        past = pool[page_table].reshape(b, n_past, C_KV_HEADS, HEAD_DIM)
        return jnp.concatenate([past, new], axis=1)

    kcb = compress_blocks(with_past(pool_kc, kc), pos_k, w1_k, w2_k)
    vcb = compress_blocks(with_past(pool_vc, vc), pos_v, w1_v, w2_v)
    ksb = select_blocks(with_past(pool_ks, ks))
    vsb = select_blocks(with_past(pool_vs, vs))
    qpos = n_past + jnp.arange(s_len)
    o_cmp, o_sel = nsa_compressed_selected(q, qpos, kcb, vcb, ksb, vsb)
    o_win, _ = gathered_window_attention(q, jnp.concatenate([buf_kw, kw], axis=1),
                                         jnp.concatenate([buf_vw, vw], axis=1), buf_kw.shape[1], C_WINDOW, 1)
    y = odd_output(x, o_cmp, o_sel, o_win, gl, z, w_out)
    return y, kc, vc, ks, vs, kw, vw

def setup_inputs(seed: int = 0) -> dict:
    key = jax.random.key(seed)
    ks = jax.random.split(key, 25)
    f32 = jnp.float32
    n_pages = PAST_LEN // PAGE_SIZE
    n_used = DEC_BATCH * n_pages
    n_pool = n_used + n_used // 4
    a_buf = min(A_WIN_MAX, PAST_LEN)
    c_buf = min(C_WINDOW, PAST_LEN)

    def rnd(k, shape, scale):
        return scale * jax.random.normal(k, shape, f32)

    page_table = jax.random.permutation(ks[11], n_pool)[:n_used].reshape(DEC_BATCH, n_pages).astype(jnp.int32)
    kv_page = (N_ODD, n_pool, PAGE_SIZE, C_KV_HEADS, HEAD_DIM)
    a_shape = (N_EVEN, DEC_BATCH, a_buf, A_HEADS, HEAD_DIM)
    w_shape = (N_ODD, DEC_BATCH, c_buf, C_KV_HEADS, HEAD_DIM)
    return {
        'x_prompt': rnd(ks[0], (BATCH, SEQ, D_MODEL), 1.0),
        'x_sample': rnd(ks[1], (DEC_BATCH, DEC_SEQ, D_MODEL), 1.0),
        'cache_a_k': rnd(ks[2], a_shape, 1.0),
        'cache_a_v': rnd(ks[3], a_shape, 1.0),
        'state_ret': rnd(ks[4], (N_EVEN, DEC_BATCH, B_HEADS, B_DK, B_DV), 0.5),
        'cache_c_kcmp': rnd(ks[5], kv_page, 1.0),
        'cache_c_vcmp': rnd(ks[6], kv_page, 1.0),
        'cache_c_ksel': rnd(ks[7], kv_page, 1.0),
        'cache_c_vsel': rnd(ks[8], kv_page, 1.0),
        'cache_c_kwin': rnd(ks[9], w_shape, 1.0),
        'cache_c_vwin': rnd(ks[10], w_shape, 1.0),
        'page_table': page_table,
        'even_norm': 1.0 + rnd(ks[12], (N_EVEN, D_MODEL), 0.05),
        'even_w_in': rnd(ks[13], (N_EVEN, D_MODEL, D_IN_EVEN), D_MODEL ** -0.5),
        'even_w_out': rnd(ks[14], (N_EVEN, D_MIX_EVEN, D_MODEL), D_MIX_EVEN ** -0.5),
        'odd_norm': 1.0 + rnd(ks[15], (N_ODD, D_MODEL), 0.05),
        'odd_w_in': rnd(ks[16], (N_ODD, D_MODEL, D_IN_ODD), D_MODEL ** -0.5),
        'odd_w_out': rnd(ks[17], (N_ODD, D_MIX_ODD, D_MODEL), D_MIX_ODD ** -0.5),
        'cmp_pos_k': rnd(ks[18], (N_ODD, CMP_LEN, HEAD_DIM), 0.5),
        'cmp_w1_k': rnd(ks[19], (N_ODD, CMP_LEN * HEAD_DIM, CMP_HIDDEN), (CMP_LEN * HEAD_DIM) ** -0.5),
        'cmp_w2_k': rnd(ks[20], (N_ODD, CMP_HIDDEN, HEAD_DIM), CMP_HIDDEN ** -0.5),
        'cmp_pos_v': rnd(ks[21], (N_ODD, CMP_LEN, HEAD_DIM), 0.5),
        'cmp_w1_v': rnd(ks[22], (N_ODD, CMP_LEN * HEAD_DIM, CMP_HIDDEN), (CMP_LEN * HEAD_DIM) ** -0.5),
        'cmp_w2_v': rnd(ks[23], (N_ODD, CMP_HIDDEN, HEAD_DIM), CMP_HIDDEN ** -0.5),
        'final_norm': 1.0 + rnd(ks[24], (D_MODEL,), 0.05),
    }

def reference(x_prompt, x_sample, cache_a_k, cache_a_v, state_ret, cache_c_kcmp, cache_c_vcmp,
              cache_c_ksel, cache_c_vsel, cache_c_kwin, cache_c_vwin, page_table,
              even_norm, even_w_in, even_w_out, odd_norm, odd_w_in, odd_w_out,
              cmp_pos_k, cmp_w1_k, cmp_w2_k, cmp_pos_v, cmp_w1_v, cmp_w2_v, final_norm):
    hp, hs = x_prompt, x_sample
    ak_p, ak_s, av_p, av_s, ret_p, ret_s = [], [], [], [], [], []
    kc_p, kc_s, vc_p, vc_s, ks_p, ks_s, vs_p, vs_s, kw_p, kw_s, vw_p, vw_s = ([] for _ in range(12))
    for layer in range(DEPTH):
        i = layer // 2
        if layer % 2 == 0:
            hp, k_new, v_new, st = even_layer_prompt(hp, even_norm[i], even_w_in[i], even_w_out[i])
            ak_p.append(k_new)
            av_p.append(v_new)
            ret_p.append(st)
            hs, k_new, v_new, st = even_layer_sample(hs, cache_a_k[i], cache_a_v[i], state_ret[i],
                                                     even_norm[i], even_w_in[i], even_w_out[i])
            ak_s.append(k_new)
            av_s.append(v_new)
            ret_s.append(st)
        else:
            cmp_args = (cmp_pos_k[i], cmp_w1_k[i], cmp_w2_k[i], cmp_pos_v[i], cmp_w1_v[i], cmp_w2_v[i])
            hp, *rows = odd_layer_prompt(hp, odd_norm[i], odd_w_in[i], odd_w_out[i], *cmp_args)
            for lst, row in zip((kc_p, vc_p, ks_p, vs_p, kw_p, vw_p), rows):
                lst.append(row)
            hs, *rows = odd_layer_sample(hs, page_table, cache_c_kcmp[i], cache_c_vcmp[i], cache_c_ksel[i],
                                         cache_c_vsel[i], cache_c_kwin[i], cache_c_vwin[i],
                                         odd_norm[i], odd_w_in[i], odd_w_out[i], *cmp_args)
            for lst, row in zip((kc_s, vc_s, ks_s, vs_s, kw_s, vw_s), rows):
                lst.append(row)
    y_prompt = rmsnorm(hp, final_norm)
    y_sample = rmsnorm(hs, final_norm)
    stk = lambda lst: jnp.stack(lst, axis=0)
    return (y_prompt, y_sample, stk(ak_p), stk(ak_s), stk(av_p), stk(av_s), stk(ret_p), stk(ret_s),
            stk(kc_p), stk(kc_s), stk(vc_p), stk(vc_s), stk(ks_p), stk(ks_s), stk(vs_p), stk(vs_s),
            stk(kw_p), stk(kw_s), stk(vw_p), stk(vw_s))


_drawn_inputs = setup_inputs


def setup_inputs(seed=0):
    import zlib

    import numpy as np

    out = dict(_drawn_inputs(seed))
    spreads = {}
    factors = {'cache_c_kcmp': 3.879,
     'cache_c_vcmp': 3.137,
     'cache_c_ksel': 4.488,
     'cache_c_vsel': 3.605,
     'cache_c_kwin': 3.32,
     'cmp_pos_k': 8.0}
    for name, (base, spread) in spreads.items():
        noise = np.random.default_rng([zlib.crc32(name.encode()), seed]).standard_normal(out[name].shape)
        drawn = base * np.exp(spread * noise) if base else spread * noise
        out[name] = jnp.asarray(drawn.astype(out[name].dtype))
    for name, factor in factors.items():
        out[name] = (out[name] * factor).astype(out[name].dtype)
    return out
```

```python
import concourse.bass as bass
from concourse import mybir
import numpy as np
import math
from contextlib import ExitStack

F32 = mybir.dt.float32
BF16 = mybir.dt.bfloat16
I32 = mybir.dt.int32
ALU = mybir.AluOpType
ACT = mybir.ActivationFunctionType
AX = mybir.AxisListType.X

P = 128
D = 1024
T = 1024
NT = T // P
NB, NJ = 8, 4
NS = NB * NJ
ROWS = T + NS
HD = 64
PAST = 2048
PAGE = 128
NPOOL = 160
SCALE = HD ** -0.5
BIG = 1e30
EPS_RMS, EPS_GN = 1e-6, 1e-5
QA, KA, VA, ZA, QB, KB, VB, ZB, E_COLS = 0, 512, 1024, 1536, 2048, 2304, 2560, 3072, 3584
QC, KC, VC, KS, VS, KW, VW, GL, ZC, O_COLS = 0, 1024, 1152, 1280, 1408, 1536, 1664, 1792, 1840, 2864
KD = D // P
BH, BDV = 4, 128
NPC = T // 16
NCB = NPC - 1
NPS = PAST // 16
NCS = NPS - 1
NSL = 33
CH = 256
STR = 96
AK = 4 * P + 4 * STR + NJ


def _constants():
    cols, parts = {}, []

    def put(name, a):
        a = np.asarray(a, np.float64).reshape(np.asarray(a).shape[0], -1)
        full = np.zeros((P, a.shape[1]), np.float32)
        full[:a.shape[0]] = a
        at = sum(x.shape[1] for x in parts)
        parts.append(full)
        cols[name] = (at, at + a.shape[1])

    p = np.arange(P)[:, None]
    f = np.arange(P)[None, :]
    put("ident", np.eye(P))
    put("causal", np.where(f > p, BIG, 0.0))
    put("edge", np.where(f < p, BIG, 0.0))
    t, c = np.arange(NT)[None, :, None], np.arange(NCB)[None, None, :]
    put("cmask", np.where(16 * c + 31 > 128 * t + p[:, :, None], BIG, 0.0))

    def many(dist):
        n = ((dist <= 128).astype(int) + ((dist % 4 == 0) & (dist <= 512)) + ((dist % 16 == 0) & (dist <= 2048)))
        n = np.where(dist >= 0, n, 0)
        return np.where(n > 0, -np.log(np.maximum(n, 1)), BIG)

    put("abias", many(p + (NT - 1) * P - np.arange(NT * P)[None, :]))
    row = np.arange(32)[:, None]
    j = row % NJ
    win = PAST - 512 + 4 * np.arange(P)[None, :] + np.arange(4)[:, None]
    strided = 16 * np.arange(STR)[None, :] + np.arange(4)[:, None]
    new = PAST + np.arange(NJ)
    pos = np.concatenate([win.ravel(), strided.ravel(), new])[None, :]
    put("asbias", many(PAST + j - pos))
    put("adiag", np.repeat((row // NJ == np.arange(8)[None, :]).astype(float), HD, axis=1))
    row = np.arange(64)[:, None]
    j = row % NJ
    put("newmask", np.where(np.arange(NJ)[None, :] > j, BIG, 0.0))
    put("winmask", np.where((4 * np.arange(P)[None, :] + np.arange(4)[:, None]).ravel()[None, :] < j, BIG, 0.0))
    put("same", ((row // 32 == row.T // 32) & (row % NJ == row.T % NJ)).astype(float))
    c, b = np.arange(NCS)[:, None], np.arange(NSL)[None, :]
    over = np.minimum(16 * c + 32, 64 * b + 64) - np.maximum(16 * c, 64 * b)
    put("overlap", np.clip(over, 0, None) / 32.0)
    put("valid", (p >= 31).astype(float))
    put("sub", p % 8)
    lg = np.log1p(-np.exp2(-5.0 - np.arange(BH)))
    h = np.arange(BH)[None, :]
    k3, q3, h3 = np.arange(P)[:, None, None], np.arange(P)[None, None, :], np.arange(BH)[None, :, None]
    put("intra", np.where(q3 >= k3, np.exp(lg[h3] * np.maximum(q3 - k3, 0)), 0.0) * SCALE)
    put("qdec", np.exp(lg[h] * (p + 1.0)))
    put("kdec", np.exp(lg[h] * (P - 1.0 - p)) * SCALE)
    k3, q3 = np.arange(NS)[:, None, None], np.arange(NS)[None, None, :]
    put("intra_s", np.where((q3 >= k3) & (q3 // NJ == k3 // NJ), np.exp(lg[h3] * np.maximum(q3 - k3, 0)), 0.0) * SCALE)
    js = np.arange(NS)[:, None] % NJ
    put("qdec_s", np.exp(lg[h] * (js + 1.0)))
    put("kdec_s", np.exp(lg[h] * (NJ - 1.0 - js)) * SCALE)
    m3, t3 = np.arange(NB // 2)[None, :, None], np.arange(NS)[None, None, :]
    put("qmask_s", (t3 // NJ == 2 * m3 + p[:, :, None] // HD).astype(float))
    put("kmask_s", (np.arange(NS)[:, None] // NJ == np.arange(NB)[None, :]).astype(float))
    freqs = (10000.0 ** (-np.arange(32) / 32.0)).astype(np.float32)
    tok = np.concatenate([np.arange(T), np.zeros(P)]).reshape(NT + 1, P)
    tok[NT, :NS] = PAST + np.arange(NS) % NJ
    ang = (tok.astype(np.float32)[:, :, None] * freqs[None, None, :]).astype(np.float64)
    trig = np.stack([np.cos(ang), np.sin(ang)], axis=2).astype(np.float32)
    return np.concatenate(parts, axis=1), cols, trig, lg


CONST, COLS, TRIG, LOG_G = _constants()


def gemm_tiles():
    return [(t, P if t < NT else NS) for t in range(NT + 1)]


def next_round(nc, sems):
    nums = sorted(s.num for s in sems)
    first = nums[0]
    for at, num in enumerate(nums):
        if at + 1 == len(nums) or nums[at + 1] != num + 1:
            nc.sync.sem_clear(range(first, num + 1))
            first = nums[at + 1] if at + 1 < len(nums) else None
    nc.all_engine_barrier()


class Phase(ExitStack):

    def __init__(self, nc):
        super().__init__()
        self.nc, self.semaphores = nc, []

    def semaphore(self, name):
        s = self.enter_context(self.nc.semaphore(name))
        self.semaphores.append(s)
        return s

    def __exit__(self, *error):
        if error[0] is None:
            next_round(self.nc, self.semaphores)
        return super().__exit__(*error)


def project(nc, ident, kind, src, w, n_cols, dst, gain=None, gates=None, residual=None):
    chunk = next(c for c in range(512, 0, -2) if n_cols % c == 0)
    n_chunks = n_cols // chunk
    with Phase(nc) as ctx:
        def sb(name, shape, dt=F32):
            return ctx.enter_context(nc.sbuf_tensor(f"{dst[0].tensor.name}_{name}", shape, dt))

        def sem(name):
            return ctx.semaphore(f"{dst[0].tensor.name}_{name}")

        yT = sb("yT", [P, KD, (NT + 1) * P])
        wbuf = sb("w", [P, KD, 2, chunk])
        res = sb("res", [P, 3, chunk])
        outb = sb("out", [P, 3, chunk])
        x = sb("x", [P, 2, D])
        z = sb("z", [P, 2, D])
        y = sb("y", [P, 2, D])
        g = sb("g", [P, D])
        stat = sb("stat", [P, 2, 4])
        tps = [ctx.enter_context(nc.psum_tensor(f"{dst[0].tensor.name}_tps{b}", [P, KD, P], F32)) for b in range(2)]
        acc = [ctx.enter_context(nc.psum_tensor(f"{dst[0].tensor.name}_acc{b}", [P, 512], F32)) for b in range(3)]
        gain_in = sem("gain_in")
        loaded = [sem(f"loaded{b}") for b in range(2)]
        squares = [sem(f"squares{b}") for b in range(2)]
        means = [sem(f"means{b}") for b in range(2)]
        roots = [sem(f"roots{b}") for b in range(2)]
        inverses = [sem(f"inverses{b}") for b in range(2)]
        rows_ready = [sem(f"rows_ready{b}") for b in range(2)]
        turned = [sem(f"turned{b}") for b in range(2)]
        yT_written = [sem(f"yT_written{b}") for b in range(2)]
        w_in = sem("w_in")
        w_used = sem("w_used")
        pad_zero = sem("pad_zero")
        res_in = [sem(f"res_in{b}") for b in range(3)]
        product = [sem(f"product{b}") for b in range(3)]
        evacuated = [sem(f"evacuated{b}") for b in range(3)]
        stored = [sem(f"stored{b}") for b in range(3)]
        n_loads = 1 if kind == "norm" else 1 + len(gates)

        def all_tiles(e, step):
            with e.Fori(0, NT // 2) as i:
                for b in range(2):
                    step(i, b, lambda a: a[0][bass.ds((i * 2 + b) * P, P), :], P)
            step(NT // 2, 0, lambda a: a[1], NS)

        with nc.Block() as block:
            @block.sync
            def _(sp):
                for b in range(3):
                    sp.sem_inc(stored[b], 16)
                if kind == "norm":
                    sp.dma_start(g[:, :], gain.partition_broadcast(P)).then_inc(gain_in, 16)

                def load(u, b, rows, n):
                    sp.wait_ge(rows_ready[b], u + 1)
                    sp.dma_start(x[0:n, b, :], rows(src)).then_inc(loaded[b], 16)
                    if kind == "gate":
                        at = 0
                        for c0, c1 in gates[1:]:
                            sp.dma_start(z[0:n, b, at:at + c1 - c0], rows(gates[0])[:, c0:c1]).then_inc(loaded[b], 16)
                            at += c1 - c0
                all_tiles(sp, load)

                def store(i, t, n):
                    k = i * 3 + t // 3
                    sp.wait_ge(evacuated[t % 3], k + 2)
                    to = dst[0][t * P:t * P + n, :] if t < NT else dst[1]
                    sp.dma_start(to[:, bass.ds(i * chunk, chunk)], outb[0:n, t % 3, :]).then_inc(stored[t % 3], 16)
                def load_w(i):
                    sp.dma_start(wbuf[:, :, bass.ds(i % 2, 1), :].rearrange("p k a c -> p k (a c)"),
                                 w[:, bass.ds(i * chunk, chunk)].rearrange("(k p) c -> p k c", p=P)).then_inc(w_in, 16)
                load_w(0)
                with sp.Fori(0, n_chunks - 1) as i:
                    sp.wait_ge(w_used, i + 1)
                    load_w(i + 1)
                    for t, n in gemm_tiles():
                        store(i, t, n)
                for t, n in gemm_tiles():
                    store(n_chunks - 1, t, n)
                for b in range(3):
                    sp.wait_ge(stored[b], 16 * (3 * n_chunks + 1))

            @block.scalar
            def _(act):
                def stats(u, b, rows, n):
                    if kind == "gate":
                        act.wait_ge(loaded[b], (u + 1) * (16 * (len(gates))))
                        nc.scalar.activation(z[0:n, b, :], z[0:n, b, :], ACT.Silu).then_inc(squares[b], 1)
                    else:
                        act.wait_ge(loaded[b], (u + 1) * 16)
                        nc.scalar.activation(z[0:n, b, :], x[0:n, b, :], ACT.Square,
                                             accum_out=stat[0:n, b, 0:1]).then_inc(squares[b], 1)
                        act.wait_ge(means[b], u + 1)
                        nc.scalar.activation(stat[0:n, b, 2:3], stat[0:n, b, 1:2], ACT.Sqrt).then_inc(roots[b], 1)

                def evacuate(i, b, n, col):
                    act.wait_ge(turned[b], i + 2)
                    nc.scalar.copy(yT[:, :, col], tps[b][:, :, 0:n]).then_inc(yT_written[b], 1)
                for b in range(2):
                    act.sem_inc(yT_written[b], 1)
                with act.Fori(0, NT // 2) as i:
                    for b in range(2):
                        stats(i, b, None, P)
                    for b in range(2):
                        evacuate(i, b, P, bass.ds((i * 2 + b) * P, P))
                stats(NT // 2, 0, None, NS)
                evacuate(NT // 2, 0, NS, slice(T, T + NS))
                if residual is not None:
                    with act.Fori(0, n_chunks) as i:
                        for t, n in gemm_tiles():
                            act.wait_ge(evacuated[t % 3], i * 3 + t // 3 + 1)
                            fr = residual[0][t * P:t * P + n, :] if t < NT else residual[1]
                            act.dma_start(res[0:n, t % 3, :], fr[:, bass.ds(i * chunk, chunk)]).then_inc(res_in[t % 3], 16)

            @block.vector
            def _(dve):
                if kind == "norm":
                    dve.wait_ge(gain_in, 16)

                def rows_of(u, b, rows, n):
                    if kind == "gate":
                        dve.wait_ge(squares[b], u + 1)
                        dve.wait_ge(loaded[b], (u + 1) * (16 * (len(gates))))
                        dve.wait_ge(turned[b], u + 1)
                        nc.vector.tensor_tensor(y[0:n, b, :], x[0:n, b, :], z[0:n, b, :], ALU.mult).then_inc(rows_ready[b], 1)
                        return
                    dve.wait_ge(squares[b], u + 1)
                    nc.vector.tensor_scalar(stat[0:n, b, 1:2], stat[0:n, b, 0:1], 1.0 / D, EPS_RMS, ALU.mult, ALU.add).then_inc(means[b], 1)
                    dve.wait_ge(roots[b], u + 1)
                    nc.vector.reciprocal(stat[0:n, b, 3:4], stat[0:n, b, 2:3]).then_inc(inverses[b], 1)
                    dve.wait_ge(inverses[b], u + 1)
                    dve.wait_ge(turned[b], u + 1)
                    nc.vector.scalar_tensor_tensor(out=y[0:n, b, :], in0=x[0:n, b, :], scalar=stat[0:n, b, 3:4],
                                                   in1=g[0:n, :], op0=ALU.mult, op1=ALU.mult).then_inc(rows_ready[b], 1)
                for b in range(2):
                    dve.sem_inc(rows_ready[b], 1)
                for b in range(3):
                    dve.sem_inc(evacuated[b], 1)
                nc.vector.memset(yT[:, :, ROWS:], 0.0).then_inc(pad_zero, 1)
                all_tiles(dve, rows_of)
                with dve.Fori(0, n_chunks) as i:
                    for t, n in gemm_tiles():
                        k = i * 3 + t // 3
                        dve.wait_ge(product[t % 3], k + 1)
                        dve.wait_ge(stored[t % 3], (k + 1) * 16)
                        if residual is None:
                            nc.vector.tensor_copy(outb[0:n, t % 3, :], acc[t % 3][0:n, 0:chunk]).then_inc(evacuated[t % 3], 1)
                        else:
                            dve.wait_ge(res_in[t % 3], (k + 1) * 16)
                            nc.vector.tensor_tensor(outb[0:n, t % 3, :], acc[t % 3][0:n, 0:chunk], res[0:n, t % 3, :],
                                                    ALU.add).then_inc(evacuated[t % 3], 1)

            @block.tensor
            def _(pe):
                for b in range(2):
                    pe.sem_inc(turned[b], 1)

                def turn(u, b, rows, n):
                    pe.wait_ge(rows_ready[b], u + 2)
                    pe.wait_ge(yT_written[b], u + 1)
                    for k in range(KD):
                        last = nc.tensor.transpose(tps[b][:, k, 0:n], y[0:n, b, k * P:(k + 1) * P], ident[0:n, 0:n])
                    last.then_inc(turned[b], 1)
                all_tiles(pe, turn)
                pe.wait_ge(yT_written[0], NT // 2 + 2)
                pe.wait_ge(yT_written[1], NT // 2 + 1)
                pe.wait_ge(pad_zero, 1)
                with pe.Fori(0, n_chunks) as i:
                    pe.wait_ge(w_in, (i + 1) * 16)
                    for t, n in gemm_tiles():
                        pe.wait_ge(evacuated[t % 3], i * 3 + t // 3 + 1)
                        for k in range(KD):
                            last = nc.tensor.matmul(acc[t % 3][:, 0:chunk], yT[:, k, t * P:(t + 1) * P],
                                                    wbuf[:, k, bass.ds(i % 2, 1), :].rearrange("p a c -> p (a c)"),
                                                    start=(k == 0), stop=(k == KD - 1))
                            if t == 1 and k == 0:
                                last.then_inc(w_used, 1)
                        last.then_inc(product[t % 3], 1)


def final_norm(nc, src, gain, dst):
    with Phase(nc) as ctx:
        x = ctx.enter_context(nc.sbuf_tensor("fn_x", [P, NT + 1, D], F32))
        sq = ctx.enter_context(nc.sbuf_tensor("fn_sq", [P, D], F32))
        g = ctx.enter_context(nc.sbuf_tensor("fn_g", [P, D], F32))
        stat = ctx.enter_context(nc.sbuf_tensor("fn_stat", [P, 4, NT + 1], F32))
        loaded = [ctx.semaphore(f"fn_loaded{t}") for t in range(NT + 1)]
        gain_in = ctx.semaphore("fn_gain_in")
        squares = ctx.semaphore("fn_squares")
        means = ctx.semaphore("fn_means")
        roots = ctx.semaphore("fn_roots")
        inverses = ctx.semaphore("fn_inverses")
        normed = ctx.semaphore("fn_normed")
        stored = ctx.semaphore("fn_stored")
        cleared = ctx.semaphore("fn_cleared")
        with nc.Block() as block:
            @block.sync
            def _(sp):
                sp.dma_start(g[:, :], gain.partition_broadcast(P)).then_inc(gain_in, 16)
                for t, n in gemm_tiles():
                    fr = src[0][t * P:t * P + n, :] if t < NT else src[1]
                    sp.dma_start(x[0:n, t, :], fr).then_inc(loaded[t], 16)
                for t, n in gemm_tiles():
                    sp.wait_ge(normed, t + 1)
                    to = dst[0][t * P:t * P + n, :] if t < NT else dst[1]
                    sp.dma_start(to, x[0:n, t, :]).then_inc(stored, 16)
                sp.wait_ge(stored, 16 * (NT + 1))

            @block.scalar
            def _(act):
                act.wait_ge(cleared, 1)
                for t, n in gemm_tiles():
                    act.wait_ge(loaded[t], 16)
                    if t:
                        act.wait_ge(squares, t)
                    nc.scalar.activation(sq[0:n, :], x[0:n, t, :], ACT.Square, accum_out=stat[0:n, 0, t:t + 1]).then_inc(squares, 1)
                act.wait_ge(means, 1)
                nc.scalar.activation(stat[:, 2, :], stat[:, 1, :], ACT.Sqrt).then_inc(roots, 1)

            @block.vector
            def _(dve):
                nc.vector.memset(stat[:, 0, :], 1.0).then_inc(cleared, 1)
                dve.wait_ge(squares, NT + 1)
                nc.vector.tensor_scalar(stat[:, 1, :], stat[:, 0, :], 1.0 / D, EPS_RMS, ALU.mult, ALU.add).then_inc(means, 1)
                dve.wait_ge(roots, 1)
                nc.vector.reciprocal(stat[:, 3, :], stat[:, 2, :]).then_inc(inverses, 1)
                dve.wait_ge(inverses, 1)
                dve.wait_ge(gain_in, 16)
                for t, n in gemm_tiles():
                    nc.vector.scalar_tensor_tensor(out=x[0:n, t, :], in0=x[0:n, t, :], scalar=stat[0:n, 3, t:t + 1],
                                                   in1=g[0:n, :], op0=ALU.mult, op1=ALU.mult).then_inc(normed, 1)


def attend_prompt(nc, con, kind, h, mix, n_pairs, kcmp=None, vcmp=None):
    sparse = kind == "sparse"
    NBR = 3 if sparse else 1
    with Phase(nc) as ctx:
        def sb(name, shape, dt=F32):
            return ctx.enter_context(nc.sbuf_tensor(f"{kind}_{name}", shape, dt))

        def sem(name):
            s = ctx.semaphore(f"{kind}_{name}")
            sems.append(s)
            return s
        sems = []
        q_in = sb("q_in", [P, NT, P])
        n_kv = 2 if sparse else 1
        k_in = [sb(f"k_in{m}", [P, NT, 2, HD]) for m in range(n_kv)]
        v_in = [sb(f"v_in{m}", [P, NT, HD if sparse else P]) for m in range(n_kv)]
        v_sb = [sb(f"v{m}", [P, NT, HD if sparse else P]) for m in range(n_kv)]
        qT = sb("qT", [P, T])
        kT = [sb(f"kT{m}", [P, T]) for m in range(n_kv)]
        pr = [sb(f"pr{b}", [P, T]) for b in range(2)]
        prT = [sb(f"prT{b}", [P, 4 * P]) for b in range(2)]
        o_sb = sb("o", [P, NT, 2, HD])
        nmax = sb("nmax", [P, 2])
        lsum = sb("lsum", [P, 2, 2 * NBR])
        coef = sb("coef", [P, 2, 2 * NBR])
        part = sb("part", [P, 2 * NBR, HD])
        if sparse:
            gl_in = sb("gl_in", [P, NT, 6])
            gate_e = sb("gate_e", [P, NT, 6])
            gate_den = sb("gate_den", [P, NT, 6])
            kc = sb("kc", [P, NCB])
            vc = sb("vc", [NCB, HD])
            kc_in = sb("kc_in", [P, NCB])
            vc_in = sb("vc_in", [NCB, HD])
        sp_s = [ctx.enter_context(nc.psum_tensor(f"{kind}_scores{b}", [P, T], F32)) for b in range(2)]
        sp_t = [ctx.enter_context(nc.psum_tensor(f"{kind}_turn{b}", [P, 4 * P], F32)) for b in range(2)]
        sp_o = [ctx.enter_context(nc.psum_tensor(f"{kind}_o_acc{b}", [P, 512], F32)) for b in range(2)]
        first_load = ctx.semaphore(f"{kind}_first_load")
        loaded = sem("loaded")
        v_copied = sem("v_copied")
        prep_turned = sem("prep_turned")
        prep_copied = [sem("prep_copied_act"), sem("prep_copied_dve")]
        gate_exp = sem("gate_exp")
        gate_ready = sem("gate_ready")
        scores_ready = sem("scores_ready")
        max_ready = sem("max_ready")
        probs_ready = sem("probs_ready")
        turned = sem("turned")
        prT_ready = [sem("prT_ready_act"), sem("prT_ready_dve")]
        group_used = sem("group_used")
        dve_step = sem("dve_step")
        out_ready = sem("out_ready")
        stored = sem("stored")

        def load(sp, i, s):
            hp = h[0].rearrange("(t p) c -> p t c", p=P)
            g = i // 4
            todo = [(q_in[:, :, :], hp[:, :, bass.ds(i * P + (QC if sparse else QA), P)])]
            if sparse:
                for m, (kcol, vcol) in enumerate(((KS, VS), (KW, VW))):
                    for half in range(2):
                        todo.append((k_in[m][:, :, half, :], hp[:, :, bass.ds(g * HD + kcol, HD)]))
                    todo.append((v_in[m][:, :, :], hp[:, :, bass.ds(g * HD + vcol, HD)]))
                todo.append((gl_in[:, :, :], hp[:, :, bass.ds(i * 6 + GL, 6)]))
                for half in range(2):
                    todo.append((kc_in[half * HD:(half + 1) * HD, :], kcmp[bass.ds(g * HD, HD), :]))
                todo.append((vc_in[:, :], vcmp[:, bass.ds(g * HD, HD)]))
            else:
                todo.append((k_in[0][:, :, :, :].rearrange("p t e d -> p t (e d)"), hp[:, :, bass.ds(i * P + KA, P)]))
                todo.append((v_in[0][:, :, :], hp[:, :, bass.ds(i * P + VA, P)]))
            for out, in_ in todo:
                sp.dma_start(out, in_).then_inc(s, 16)
            return len(todo)

        jobs = []
        for t in range(NT):
            for e in range(2):
                if sparse:
                    jobs.append((t, e, 0, None))
                    jobs.append((t, e, 1, list(range(t + 1))))
                    jobs.append((t, e, 2, list(range(max(0, t - 4), t + 1))))
                else:
                    jobs.append((t, e, 0, list(range(t + 1))))
        width = [NCB if blocks is None else P * len(blocks) for _, _, _, blocks in jobs]
        groups = []
        of_job = []
        for n, w in enumerate(width):
            of_job.append([])
            for c0 in range(0, w, 4 * P):
                of_job[n].append(len(groups))
                groups.append((n, c0, min(4 * P, w - c0)))

        last_group = {t: of_job[n][-1] for n, (t, _, _, _) in enumerate(jobs)}

        with nc.Block() as block:
            @block.sync
            def _(sp):
                n = load(sp, 0, first_load)
                sp.wait_ge(first_load, 16 * n)

        with nc.Fori(0, n_pairs) as i:
            with nc.Block() as block:
                n_prep = 2 + 2 * n_kv

                @block.sync
                def _(sp):
                    sp.wait_ge(prep_copied[0], n_prep // 2)
                    sp.wait_ge(prep_copied[1], n_prep // 2)
                    sp.wait_ge(v_copied, 1)
                    if sparse:
                        sp.wait_ge(gate_exp, 1)
                    n = load(sp, (i + 1) % n_pairs, loaded)
                    for t in range(NT):
                        sp.wait_ge(out_ready, t + 1)
                        sp.dma_start(mix[t * P:(t + 1) * P, bass.ds(i * P, P)],
                                     o_sb[:, t, :, :].rearrange("p e d -> p (e d)")).then_inc(stored, 16)
                    sp.wait_ge(stored, 16 * NT)
                    sp.wait_ge(loaded, 16 * n)

                @block.gpsimd
                def _(pool):
                    if sparse:
                        nc.gpsimd.tensor_copy(kc[:, :], kc_in[:, :])
                        nc.gpsimd.tensor_copy(vc[:, :], vc_in[:, :])
                        nc.gpsimd.tensor_copy(v_sb[1][:, :, :], v_in[1][:, :, :])
                    nc.gpsimd.tensor_copy(v_sb[0][:, :, :], v_in[0][:, :, :]).then_inc(v_copied, 1)

                def prep_dst(g):
                    if g < 2:
                        return qT[:, g * 512:(g + 1) * 512]
                    return kT[(g - 2) // 2][:, (g % 2) * 512:(g % 2 + 1) * 512]

                def copy_group(eng, copy, g):
                    n, _, w = groups[g]
                    eng.wait_ge(turned, g + 1)
                    if g >= 2:
                        eng.wait_ge(group_used, g - 1)
                    if width[n] == NCB:
                        copy(prT[g % 2][0:NCB, 0:P], sp_t[g % 2][0:NCB, 0:P]).then_inc(prT_ready[g % 2], 1)
                    else:
                        copy(prT[g % 2][:, 0:w], sp_t[g % 2][:, 0:w]).then_inc(prT_ready[g % 2], 1)

                @block.scalar
                def _(act):
                    for g in range(0, n_prep, 2):
                        act.wait_ge(prep_turned, g + 1)
                        nc.scalar.activation(prep_dst(g), sp_t[0][:, :], ACT.Copy,
                                             scale=-SCALE if g < 2 else 1.0).then_inc(prep_copied[0], 1)
                    if sparse:
                        nc.scalar.activation(gate_e[:, :, :], gl_in[:, :, :], ACT.Exp, scale=-1.0).then_inc(gate_exp, 1)
                    for n, (t, e, br, _) in enumerate(jobs):
                        act.wait_ge(max_ready, n + 1)
                        if of_job[n][0] >= 1 and n >= 2:
                            act.wait_ge(turned, of_job[n - 2][-1] + 1)
                        if t >= 2:
                            act.wait_ge(out_ready, t - 1)
                        src = sp_s[n % 2] if sparse else pr[n % 2]
                        slot = e * NBR + br
                        nc.scalar.activation(pr[n % 2][:, 0:width[n]], src[:, 0:width[n]], ACT.Exp, scale=-1.0,
                                             bias=nmax[:, n % 2:n % 2 + 1],
                                             accum_out=lsum[:, t % 2, slot:slot + 1]).then_inc(probs_ready, 1)
                        for g in of_job[n]:
                            if g % 2 == 0:
                                copy_group(act, nc.scalar.copy, g)

                @block.vector
                def _(dve):
                    steps = 0
                    for g in range(1, n_prep, 2):
                        dve.wait_ge(prep_turned, g + 1)
                        nc.vector.tensor_scalar(prep_dst(g), sp_t[1][:, :], -SCALE if g < 2 else 1.0, None,
                                                ALU.mult).then_inc(prep_copied[1], 1)
                    if sparse:
                        dve.wait_ge(gate_exp, 1)
                        nc.vector.tensor_scalar(gate_den[:, :, :], gate_e[:, :, :], 1.0, None, ALU.add).then_inc(gate_ready, 1)
                        dve.wait_ge(gate_ready, 1)

                    def maximum(n):
                        t = jobs[n][0]
                        dve.wait_ge(scores_ready, n + 1)
                        if n >= 2:
                            dve.wait_ge(probs_ready, n - 1)
                        if sparse:
                            nc.vector.tensor_reduce(nmax[:, n % 2:n % 2 + 1], sp_s[n % 2][:, 0:width[n]], AX,
                                                    ALU.min).then_inc(max_ready, 1)
                        else:
                            if n >= 2:
                                dve.wait_ge(turned, of_job[n - 2][-1] + 1)
                            nc.vector.tensor_tensor_reduce(
                                out=pr[n % 2][:, 0:width[n]], in0=sp_s[n % 2][:, 0:width[n]],
                                in1=con("abias")[:, (NT - 1 - t) * P:], scale=1.0, scalar=3e38, op0=ALU.add, op1=ALU.min,
                                accum_out=nmax[:, n % 2:n % 2 + 1]).then_inc(max_ready, 1)

                    def finish(t):
                        nonlocal steps
                        dve.wait_ge(group_used, last_group[t] + 1)
                        l, c = lsum[:, t % 2, :], coef[:, t % 2, :]
                        o = sp_o[t % 2][:, 0:2 * NBR * HD].rearrange("p (s d) -> p s d", d=HD)
                        if sparse:
                            nc.vector.tensor_tensor(c, l, gate_den[:, t, :], ALU.mult).then_inc(dve_step, 1)
                            steps += 1
                            dve.wait_ge(dve_step, steps)
                            nc.vector.reciprocal(c, c).then_inc(dve_step, 1)
                            steps += 1
                            dve.wait_ge(dve_step, steps)
                            if t == 0:
                                cc = coef[:, 0, :].rearrange("p (e b) -> p e b", b=3)[:, :, 0]
                                nc.vector.tensor_scalar(cc, cc, con("valid"), None, ALU.mult).then_inc(dve_step, 1)
                                steps += 1
                                dve.wait_ge(dve_step, steps)
                            if t >= 1:
                                dve.wait_ge(out_ready, t)
                            nc.vector.tensor_tensor(part[:, :, :], o, c.unsqueeze(2).broadcast_to([P, 6, HD]),
                                                    ALU.mult).then_inc(dve_step, 1)
                            steps += 1
                            dve.wait_ge(dve_step, steps)
                            nc.vector.tensor_reduce(o_sb[:, t, :, :], part[:, :, :].rearrange("p (e b) d -> p e d b", b=3),
                                                    AX, ALU.add).then_inc(out_ready, 1)
                        else:
                            nc.vector.reciprocal(c, l).then_inc(dve_step, 1)
                            steps += 1
                            dve.wait_ge(dve_step, steps)
                            nc.vector.tensor_tensor(o_sb[:, t, :, :], o, c.unsqueeze(2).broadcast_to([P, 2, HD]),
                                                    ALU.mult).then_inc(out_ready, 1)
                    maximum(0)
                    for n in range(len(jobs)):
                        if n + 1 < len(jobs):
                            maximum(n + 1)
                        for g in of_job[n]:
                            if g % 2 == 1:
                                copy_group(dve, nc.vector.tensor_copy, g)
                        if n + 1 == len(jobs) or jobs[n + 1][0] != jobs[n][0]:
                            finish(jobs[n][0])

                @block.tensor
                def _(pe):
                    srcs = [q_in[:, :, :]] + [k[:, :, :, :].rearrange("p t e d -> p t (e d)") for k in k_in]
                    for g in range(n_prep):
                        if g >= 2:
                            pe.wait_ge(prep_copied[g % 2], g // 2)
                        for m in range(4):
                            last = nc.tensor.transpose(sp_t[g % 2][:, m * P:(m + 1) * P], srcs[g // 2][:, (g % 2) * 4 + m, :],
                                                       con("ident"))
                        last.then_inc(prep_turned, 1)
                    pe.wait_ge(prep_copied[0], n_prep // 2)
                    pe.wait_ge(prep_copied[1], n_prep // 2)
                    pe.wait_ge(v_copied, 1)

                    def scores(n):
                        t, e, br, blocks = jobs[n]
                        if n >= 2:
                            pe.wait_ge(probs_ready if sparse else max_ready, n - 1)
                        lhs = qT[e * HD:(e + 1) * HD, t * P:(t + 1) * P]
                        s = sp_s[n % 2]
                        if blocks is None:
                            nc.tensor.matmul(s[:, 0:NCB], lhs, kc[e * HD:(e + 1) * HD, :], start=True, stop=False)
                            nc.tensor.matmul(s[:, 0:NCB], con.ident16, con.cmask16[:, t, :], start=False,
                                             stop=True).then_inc(scores_ready, 1)
                            return
                        k = kT[1 if br == 2 else 0]
                        for c0 in range(0, width[n], 512):
                            c1 = min(c0 + 512, width[n])
                            at = blocks[0] * P
                            masks = []
                            if sparse:
                                if width[n] - P >= c0 and width[n] <= c1:
                                    masks.append((width[n] - P, con.causal16))
                                if br == 2 and t >= 4 and c0 == 0:
                                    masks.append((0, con.edge16))
                            last = nc.tensor.matmul(s[:, c0:c1], lhs, k[e * HD:(e + 1) * HD, at + c0:at + c1],
                                                    start=True, stop=not masks)
                            for x, (m0, mask) in enumerate(masks):
                                last = nc.tensor.matmul(s[:, m0:m0 + P], con.ident16, mask, start=False, stop=x == len(masks) - 1)
                        last.then_inc(scores_ready, 1)

                    def turn(g):
                        n, c0, w = groups[g]
                        if g == of_job[n][0]:
                            pe.wait_ge(probs_ready, n + 1)
                        if g >= 2:
                            pe.wait_ge(prT_ready[g % 2], len([x for x in range(g) if x % 2 == g % 2]))
                        for c in range(0, w, P):
                            m = min(P, w - c)
                            last = nc.tensor.transpose(sp_t[g % 2][0:m, c:c + P], pr[n % 2][:, c0 + c:c0 + c + m], con("ident"))
                        last.then_inc(turned, 1)

                    def times_v(g):
                        n, c0, w = groups[g]
                        t, e, br, blocks = jobs[n]
                        pe.wait_ge(prT_ready[g % 2], len([x for x in range(g + 1) if x % 2 == g % 2]))
                        if g == of_job[n][0] and e == 0 and br == 0 and t >= 2:
                            pe.wait_ge(out_ready, t - 1)
                        slot = (e * NBR + br) * HD
                        o = sp_o[t % 2][:, slot:slot + HD]
                        for c in range(0, w, P):
                            if blocks is None:
                                lhs, rhs = prT[g % 2][0:NCB, 0:P], vc[:, :]
                            else:
                                kb = blocks[(c0 + c) // P]
                                lhs = prT[g % 2][:, c:c + P]
                                rhs = v_sb[1 if br == 2 else 0][:, kb, :] if sparse else v_sb[0][:, kb, e * HD:(e + 1) * HD]
                            last = nc.tensor.matmul(o, lhs, rhs, start=c0 + c == 0, stop=c0 + c + P >= width[n])
                        last.then_inc(group_used, 1)

                    scores(0)
                    for n in range(len(jobs)):
                        if n + 1 < len(jobs):
                            scores(n + 1)
                        gs = of_job[n]
                        turn(gs[0])
                        for x, g in enumerate(gs):
                            if x + 1 < len(gs):
                                turn(gs[x + 1])
                            times_v(g)
            next_round(nc, sems)


def retain(nc, con, h, mix, trig, state_out, state_in=None):
    sample = state_in is not None
    name = "ret_s" if sample else "ret"
    R = NS if sample else P
    n_rounds = 1 if sample else NT
    with Phase(nc) as ctx:
        def sb(nm, shape, dt=F32):
            return ctx.enter_context(nc.sbuf_tensor(f"{name}_{nm}", shape, dt))

        def sem(nm):
            s = ctx.semaphore(f"{name}_{nm}")
            sems.append(s)
            return s
        sems = []
        x = sb("x", [R, D])
        cs = sb("cs", [R, 2, 32])
        qk = sb("qk", [R, 8, 2, 32])
        m1 = sb("m1", [R, 8, 32])
        m2 = sb("m2", [R, 8, 32])
        qd = sb("qd", [R, BH, 2 if sample else 1, HD])
        kd = sb("kd", [R, BH, HD])
        kdm = sb("kdm", [NS, BH, NB, HD]) if sample else None
        n_t = 8 if sample else 6
        xT = sb("xT", [P, n_t, R])
        qdm = sb("qdm", [P, BH, NB // 2, NS]) if sample else None
        a = sb("a", [R, BH, R])
        n_st = NB // 2 if sample else 1
        st = sb("st", [P, NB // 2, BH, BDV]) if sample else sb("st", [P, 2, BDV])
        o = sb("o", [R, BH, BDV])
        sq = sb("sq", [R, BH, BDV])
        mean = sb("mean", [R, 4, BH])
        ps_t = ctx.enter_context(nc.psum_tensor(f"{name}_ps_t", [P, n_t, R], F32))
        ps_a = ctx.enter_context(nc.psum_tensor(f"{name}_ps_a", [P, 2, 512], F32))
        o_banks = 1 if sample else 2
        ps_o = ctx.enter_context(nc.psum_tensor(f"{name}_ps_o", [P, o_banks, 512], F32))
        ps_u = ctx.enter_context(nc.psum_tensor(f"{name}_ps_u", [P, 4 if sample else 1, 512], F32))

        def heads(ap, n, per):
            return ap[:, 0:per, 0:4 // per * n].rearrange("p e (m v) -> p m e v", v=n)
        first_load = ctx.semaphore(f"{name}_first_load")
        zeroed = ctx.semaphore(f"{name}_zeroed")
        loaded, rotated, decayed, turned, xT_ready, masked, a_raw, a_ready = (
            sem(n) for n in "loaded rotated decayed turned xT_ready masked a_raw a_ready".split())
        update_ready, o_acc, state_new, var_ready, root_ready, out_ready, stored, dve_step = (
            sem(n) for n in "update_ready o_acc state_new var_ready root_ready out_ready stored dve_step".split())

        def load(sp, i, s):
            if sample:
                sp.dma_start(x[:, :], h[1][:, QB:QB + D]).then_inc(s, 16)
                sp.dma_start(cs[:, :, :], trig[NT, 0:NS]).then_inc(s, 16)
                for e in range(2):
                    for m in range(NB // 2):
                        sp.dma_start(st[e * HD:(e + 1) * HD, m, :, :],
                                     state_in[2 * m + e].rearrange("h k v -> k h v")).then_inc(s, 16)
                return 2 + NB
            sp.dma_start(x[:, :], h[0][bass.ds(i * P, P), QB:QB + D]).then_inc(s, 16)
            sp.dma_start(cs[:, :, :].rearrange("p a f -> p (a f)"),
                         trig[bass.ds(i, 1)].rearrange("t p a f -> p (t a f)")).then_inc(s, 16)
            return 2

        with nc.Block() as block:
            @block.sync
            def _(sp):
                n = load(sp, 0, first_load)
                sp.wait_ge(first_load, 16 * n)

            if not sample:
                @block.vector
                def _(dve):
                    nc.vector.memset(st[:, :, :], 0.0).then_inc(zeroed, 1)
                    dve.wait_ge(zeroed, 1)

        def round_(i):
            with nc.Block() as block:
                @block.sync
                def _(sp):
                    if not sample:
                        sp.wait_ge(rotated, 1)
                        sp.wait_ge(state_new, 1)
                        load(sp, (i + 1) % n_rounds, loaded)
                    sp.wait_ge(out_ready, 1)
                    to = mix[T:ROWS, 512:D] if sample else mix[bass.ds(i * P, P), 512:D]
                    sp.dma_start(to, o[:, :, :].rearrange("p h e -> p (h e)")).then_inc(stored, 16)
                    if not sample:
                        sp.wait_ge(loaded, 32)
                    sp.wait_ge(stored, 16)

                @block.vector
                def _(dve):
                    steps = 0

                    def link(ins):
                        nonlocal steps
                        steps += 1
                        ins.then_inc(dve_step, 1)
                        dve.wait_ge(dve_step, steps)
                    v4 = x[:, 0:512].rearrange("p (h a f) -> p h a f", h=8, a=2)
                    x1, x2 = v4[:, :, 0, :], v4[:, :, 1, :]
                    cos = cs[:, 0, :].unsqueeze(1).broadcast_to([R, 8, 32])
                    sin = cs[:, 1, :].unsqueeze(1).broadcast_to([R, 8, 32])
                    nc.vector.tensor_tensor(m1[:, :, :], x1, cos, ALU.mult)
                    link(nc.vector.tensor_tensor(m2[:, :, :], x2, sin, ALU.mult))
                    link(nc.vector.tensor_tensor(qk[:, :, 0, :], m1[:, :, :], m2[:, :, :], ALU.subtract))
                    nc.vector.tensor_tensor(m1[:, :, :], x1, sin, ALU.mult)
                    link(nc.vector.tensor_tensor(m2[:, :, :], x2, cos, ALU.mult))
                    nc.vector.tensor_tensor(qk[:, :, 1, :], m1[:, :, :], m2[:, :, :], ALU.add).then_inc(rotated, 1)
                    dve.wait_ge(rotated, 1)
                    flat = qk[:, :, :, :].rearrange("p h a f -> p h (a f)")
                    qdec = con("qdec_s" if sample else "qdec").unsqueeze(2).broadcast_to([R, BH, HD])
                    kdec = con("kdec_s" if sample else "kdec").unsqueeze(2).broadcast_to([R, BH, HD])
                    nc.vector.tensor_tensor(qd[:, :, 0, :], flat[:, 0:4, :], qdec, ALU.mult)
                    if sample:
                        nc.vector.tensor_tensor(qd[:, :, 1, :], flat[:, 0:4, :], qdec, ALU.mult)
                    nc.vector.tensor_tensor(kd[:, :, :], flat[:, 4:8, :], kdec, ALU.mult).then_inc(decayed, 1)
                    if sample:
                        dve.wait_ge(decayed, 1)
                        for hh in range(BH):
                            last = nc.vector.tensor_tensor(kdm[:, hh, :, :], kd[:, hh, :].unsqueeze(1).broadcast_to([NS, NB, HD]),
                                                           con("kmask_s").unsqueeze(2).broadcast_to([NS, NB, HD]), ALU.mult)
                        last.then_inc(decayed, 1)
                    dve.wait_ge(turned, 1)
                    nc.vector.tensor_copy(xT[:, :, :], ps_t[:, 0:n_t, 0:R]).then_inc(xT_ready, 1)
                    if sample:
                        dve.wait_ge(xT_ready, 1)
                        for hh in range(BH):
                            last = nc.vector.tensor_tensor(qdm[:, hh, :, :], xT[:, 4 + hh, :].unsqueeze(1).broadcast_to([P, NB // 2, NS]),
                                                           con("qmask_s").rearrange("p (m t) -> p m t", t=NS), ALU.mult)
                        last.then_inc(masked, 1)
                    dve.wait_ge(a_raw, 1)
                    intra = con("intra_s" if sample else "intra").rearrange("p (h q) -> p h q", h=BH)
                    nc.vector.tensor_tensor(a[:, :, :].rearrange("p (m e) q -> p m e q", e=2), heads(ps_a[0:R, :, :], R, 2),
                                            intra.rearrange("p (m e) q -> p m e q", e=2), ALU.mult).then_inc(a_ready, 1)
                    dve.wait_ge(o_acc, 1)
                    dve.wait_ge(update_ready, 1)
                    for hh in range(BH):
                        if sample:
                            u = ps_u[:, hh, :].rearrange("p (m v) -> p m v", v=BDV)
                            last = nc.vector.scalar_tensor_tensor(out=st[:, :, hh, :], in0=st[:, :, hh, :],
                                                                  scalar=float(np.exp(LOG_G[hh] * NJ)), in1=u,
                                                                  op0=ALU.mult, op1=ALU.add)
                        else:
                            half, m = slice(hh % 2 * HD, hh % 2 * HD + HD), hh // 2
                            last = nc.vector.scalar_tensor_tensor(out=st[half, m, :], in0=st[half, m, :],
                                                                  scalar=float(np.exp(LOG_G[hh] * P)),
                                                                  in1=ps_u[half, 0, m * BDV:(m + 1) * BDV],
                                                                  op0=ALU.mult, op1=ALU.add)
                    last.then_inc(state_new, 1)
                    if sample:
                        po, o4 = ps_o[0:R, 0, :].rearrange("p (h v) -> p h v", h=BH), o[:, :, :]
                        mean0, mean_b = mean[:, 0, :], mean[:, 0, :].unsqueeze(2).broadcast_to([R, BH, BDV])
                    else:
                        po, o4 = heads(ps_o[:, :, :], BDV, 2), o[:, :, :].rearrange("p (m e) v -> p m e v", e=2)
                        mean0 = mean[:, 0, :].rearrange("p (m e) -> p m e", e=2)
                        mean_b = mean0.unsqueeze(3).broadcast_to([R, 2, 2, BDV])
                    link(nc.vector.tensor_reduce(mean0, po, AX, ALU.add))
                    link(nc.vector.tensor_scalar(mean[:, 0, :], mean[:, 0, :], 1.0 / BDV, None, ALU.mult))
                    link(nc.vector.tensor_tensor(o4, po, mean_b, ALU.subtract))
                    link(nc.vector.tensor_tensor(sq[:, :, :], o[:, :, :], o[:, :, :], ALU.mult))
                    link(nc.vector.tensor_reduce(mean[:, 1, :], sq[:, :, :], AX, ALU.add))
                    nc.vector.tensor_scalar(mean[:, 1, :], mean[:, 1, :], 1.0 / BDV, EPS_GN, ALU.mult, ALU.add).then_inc(var_ready, 1)
                    dve.wait_ge(root_ready, 1)
                    link(nc.vector.reciprocal(mean[:, 3, :], mean[:, 2, :]))
                    nc.vector.tensor_tensor(o[:, :, :], o[:, :, :], mean[:, 3, :].unsqueeze(2).broadcast_to([R, BH, BDV]),
                                            ALU.mult).then_inc(out_ready, 1)

                @block.scalar
                def _(act):
                    act.wait_ge(var_ready, 1)
                    nc.scalar.activation(mean[:, 2, :], mean[:, 1, :], ACT.Sqrt).then_inc(root_ready, 1)

                @block.tensor
                def _(pe):
                    pe.wait_ge(decayed, 2 if sample else 1)
                    flat = qk[:, :, :, :].rearrange("p h a f -> p (h a f)")
                    qdf = qd[:, :, :, :].rearrange("p h e f -> p (h e f)")
                    for m in range(4):
                        nc.tensor.transpose(ps_t[:, m, 0:R], flat[:, m * P:(m + 1) * P], con("ident")[0:R, 0:R])
                    for m in range(n_t - 4):
                        src = qdf[:, m * P:(m + 1) * P]
                        last = nc.tensor.transpose(ps_t[:, 4 + m, 0:R], src, con("ident")[0:R, 0:R])
                    last.then_inc(turned, 1)
                    pe.wait_ge(xT_ready, 1)
                    for hh in range(BH):
                        half, m = slice(hh % 2 * HD, hh % 2 * HD + HD), hh // 2
                        last = nc.tensor.matmul(ps_a[0:R, hh % 2, m * R:(m + 1) * R], xT[half, 2 + m, :], xT[half, m, :],
                                                start=True, stop=True)
                    last.then_inc(a_raw, 1)
                    v = x[:, 512:D].rearrange("p (h v) -> p h v", h=BH)
                    pe.wait_ge(a_ready, 1)
                    if sample:
                        pe.wait_ge(masked, 1)
                    for hh in range(BH):
                        half, m = slice(hh % 2 * HD, hh % 2 * HD + HD), hh // 2
                        acc = ps_o[0:R, 0, hh * BDV:(hh + 1) * BDV] if sample else ps_o[:, hh % 2, m * BDV:(m + 1) * BDV]
                        nc.tensor.matmul(acc, a[:, hh, :], v[:, hh, :], start=True, stop=False)
                        if sample:
                            for q in range(NB // 2):
                                last = nc.tensor.matmul(acc, qdm[:, hh, q, :], st[:, q, hh, :], start=False, stop=q == NB // 2 - 1)
                        else:
                            last = nc.tensor.matmul(acc, xT[half, 4 + m, :], st[half, m, :], start=False, stop=True)
                    last.then_inc(o_acc, 1)
                    for hh in range(BH):
                        half, m = slice(hh % 2 * HD, hh % 2 * HD + HD), hh // 2
                        if sample:
                            for q in range(NB // 2):
                                last = nc.tensor.matmul(ps_u[:, hh, q * BDV:(q + 1) * BDV],
                                                        kdm[:, hh, 2 * q:2 * q + 2, :].rearrange("p n k -> p (n k)"),
                                                        v[:, hh, :], start=True, stop=True)
                        else:
                            last = nc.tensor.matmul(ps_u[half, 0, m * BDV:(m + 1) * BDV], kd[:, hh, :], v[:, hh, :],
                                                    start=True, stop=True)
                    last.then_inc(update_ready, 1)
        if sample:
            round_(0)
        else:
            with nc.Fori(0, n_rounds) as i:
                round_(i)
                next_round(nc, sems)
        state_stored = ctx.semaphore(f"{name}_state_stored")
        with nc.Block() as block:
            @block.sync
            def _(sp):
                n = 0
                if sample:
                    for e in range(2):
                        for m in range(NB // 2):
                            sp.dma_start(state_out[2 * m + e].rearrange("h k v -> k h v"),
                                         st[e * HD:(e + 1) * HD, m, :, :]).then_inc(state_stored, 16)
                            n += 1
                else:
                    for hh in range(BH):
                        sp.dma_start(state_out[hh], st[hh % 2 * HD:hh % 2 * HD + HD, hh // 2, :]).then_inc(state_stored, 16)
                        n += 1
                sp.wait_ge(state_stored, 16 * n)


def attend_samples_dilated(nc, con, h_s, cache_k, cache_v, mix):
    with Phase(nc) as ctx:
        def sb(nm, shape, dt=F32):
            return ctx.enter_context(nc.sbuf_tensor(f"ds_{nm}", shape, dt))

        def sem(nm):
            s = ctx.semaphore(f"ds_{nm}")
            sems.append(s)
            return s
        sems = []
        NP = 4
        q_in = sb("q_in", [NS, 512])
        q_all = sb("q_all", [P, NB, NP * 32])
        q_cur = sb("q_cur", [P, NP * 32])
        kw, ks, kn = sb("kw", [P, 4, 512]), sb("ks", [STR, 4, 512]), sb("kn", [NJ, 512])
        vw, vs, vn = sb("vw", [P, 4, 512]), sb("vs", [STR, 4, 512]), sb("vn", [NJ, 512])
        kT = sb("kT", [P, NP, AK])
        pr = sb("pr", [32, AK])
        pw, pst, pn = sb("pw", [P, 4, 32]), sb("pst", [STR, 4, 32]), sb("pn", [NJ, 32])
        stat = sb("stat", [32, 3])
        part = sb("part", [32, 8, HD])
        o = sb("o", [32, HD])
        ps_t = [ctx.enter_context(nc.psum_tensor(f"ds_ps_t{b}", [P, 512], F32)) for b in range(2)]
        ps_s = ctx.enter_context(nc.psum_tensor("ds_ps_s", [32, 1024], F32))
        ps_p = ctx.enter_context(nc.psum_tensor("ds_ps_p", [P, 9, 32], F32))
        ps_o = ctx.enter_context(nc.psum_tensor("ds_ps_o", [32, 512], F32))
        first_k, first_v, q_loaded, q_zero, q_turned, q_placed = (
            ctx.semaphore(f"ds_{n}") for n in "first_k first_v q_loaded q_zero q_turned q_placed".split())
        k_in, v_in, q_ready, turned, copied_act, copied_dve, scores_ready, max_ready, probs_ready = (
            sem(n) for n in "k_in v_in q_ready turned copied_act copied_dve scores_ready max_ready probs_ready".split())
        probs_turned, probsT_ready, o_ready, inverse, part_ready, out_ready, stored = (
            sem(n) for n in "probs_turned probsT_ready o_ready inverse part_ready out_ready stored".split())
        copied = [copied_act, copied_dve]

        def load(sp, n, cache, w, st, new, col, s):
            c = cache[bass.ds(n, 1)].rearrange("n r c -> (n r) c")
            sp.dma_start(w[:, :, :].rearrange("p s c -> p (s c)"),
                         c[PAST - 512:PAST, :].rearrange("(p s) c -> p (s c)", s=4)).then_inc(s, 16)
            sp.dma_start(st[:, :, :].rearrange("p s c -> p (s c)"),
                         c[0:PAST - 512, :].rearrange("(p s) c -> p (s c)", s=16)[:, 0:4 * 512]).then_inc(s, 16)
            sp.dma_start(new[:, :], h_s[bass.ds(n * NJ, NJ), col:col + 512]).then_inc(s, 16)

        with nc.Block() as block:
            @block.sync
            def _(sp):
                sp.dma_start(q_in[:, :], h_s[:, QA:QA + 512]).then_inc(q_loaded, 16)
                load(sp, 0, cache_k, kw, ks, kn, KA, first_k)
                load(sp, 0, cache_v, vw, vs, vn, VA, first_v)
                sp.wait_ge(first_k, 48)
                sp.wait_ge(first_v, 48)

            @block.tensor
            def _(pe):
                pe.wait_ge(q_loaded, 16)
                for m in range(NP):
                    last = nc.tensor.transpose(ps_t[0][:, m * NS:(m + 1) * NS], q_in[:, m * P:(m + 1) * P], con("ident")[0:NS, 0:NS])
                last.then_inc(q_turned, 1)

            @block.vector
            def _(dve):
                nc.vector.memset(q_all[:, :, :], 0.0).then_inc(q_zero, 1)
                dve.wait_ge(q_zero, 1)
                dve.wait_ge(q_turned, 1)
                to = q_all[:, :, :].rearrange("p n (m h j) -> p n m h j", m=NP, h=8)
                for hh in range(8):
                    half = slice(hh % 2 * HD, hh % 2 * HD + HD)
                    src = ps_t[0][half, (hh // 2) * NS:(hh // 2 + 1) * NS].rearrange("p (n j) -> p n j", j=NJ)
                    last = nc.vector.tensor_scalar(to[half, :, hh // 2, hh, :], src, -SCALE, None, ALU.mult)
                last.then_inc(q_placed, 1)
                dve.wait_ge(q_placed, 1)

        widths = [P] * 4 + [STR] * 4 + [NJ]
        with nc.Fori(0, NB) as n:
            with nc.Block() as block:
                @block.sync
                def _(sp):
                    sp.wait_ge(turned, 9)
                    load(sp, (n + 1) % NB, cache_k, kw, ks, kn, KA, k_in)
                    sp.wait_ge(o_ready, 1)
                    load(sp, (n + 1) % NB, cache_v, vw, vs, vn, VA, v_in)
                    sp.wait_ge(out_ready, 1)
                    for hh in range(8):
                        sp.dma_start(mix[bass.ds(T + n * NJ, NJ), hh * HD:(hh + 1) * HD],
                                     o[hh * NJ:(hh + 1) * NJ, :]).then_inc(stored, 16)
                    sp.wait_ge(k_in, 48)
                    sp.wait_ge(v_in, 48)
                    sp.wait_ge(stored, 16 * 8)

                def copy_group(eng, copy, g):
                    eng.wait_ge(turned, g + 1)
                    c0 = sum(widths[:g])
                    copy(kT[:, :, c0:c0 + widths[g]],
                         ps_t[g % 2][:, :].rearrange("p (m c) -> p m c", m=NP)[:, :, 0:widths[g]]).then_inc(copied[g % 2], 1)

                @block.tensor
                def _(pe):
                    for g in range(9):
                        if g >= 2:
                            pe.wait_ge(copied[g % 2], g // 2)
                        src = kw[:, g, :] if g < 4 else ks[:, g - 4, :] if g < 8 else kn[:, :]
                        w = widths[g]
                        for m in range(NP):
                            last = nc.tensor.transpose(ps_t[g % 2][:, m * P:m * P + w], src[:, m * P:(m + 1) * P], con("ident")[0:w, 0:w])
                        last.then_inc(turned, 1)
                    pe.wait_ge(q_ready, 1)
                    pe.wait_ge(copied[0], 5)
                    pe.wait_ge(copied[1], 4)
                    for c0, c1 in ((0, 512), (512, AK)):
                        for m in range(NP):
                            last = nc.tensor.matmul(ps_s[:, c0:c1], q_cur[:, m * 32:(m + 1) * 32], kT[:, m, c0:c1],
                                                    start=m == 0, stop=m == NP - 1)
                    last.then_inc(scores_ready, 1)
                    pe.wait_ge(probs_ready, 1)
                    for g in range(9):
                        c0, w = sum(widths[:g]), widths[g]
                        last = nc.tensor.transpose(ps_p[0:w, g, :], pr[:, c0:c0 + w], con("ident")[0:32, 0:32])
                    last.then_inc(probs_turned, 1)
                    pe.wait_ge(probsT_ready, 1)
                    for g in range(9):
                        lhs = pw[:, g, :] if g < 4 else pst[:, g - 4, :] if g < 8 else pn[:, :]
                        rhs = vw[:, g, :] if g < 4 else vs[:, g - 4, :] if g < 8 else vn[:, :]
                        last = nc.tensor.matmul(ps_o[:, :], lhs, rhs, start=g == 0, stop=g == 8)
                    last.then_inc(o_ready, 1)

                @block.scalar
                def _(act):
                    for g in range(0, 9, 2):
                        copy_group(act, nc.scalar.copy, g)
                    act.wait_ge(max_ready, 1)
                    nc.scalar.activation(pr[:, :], pr[:, :], ACT.Exp, scale=-1.0, bias=stat[:, 0:1],
                                         accum_out=stat[:, 1:2]).then_inc(probs_ready, 1)

                @block.vector
                def _(dve):
                    nc.vector.tensor_copy(q_cur[:, :], q_all[:, bass.ds(n, 1), :].rearrange("p n c -> p (n c)")).then_inc(q_ready, 1)
                    for g in range(1, 9, 2):
                        copy_group(dve, nc.vector.tensor_copy, g)
                    dve.wait_ge(scores_ready, 1)
                    nc.vector.tensor_tensor_reduce(out=pr[:, :], in0=ps_s[:, 0:AK], in1=con("asbias"), scale=1.0, scalar=3e38,
                                                   op0=ALU.add, op1=ALU.min, accum_out=stat[:, 0:1]).then_inc(max_ready, 1)
                    dve.wait_ge(probs_turned, 1)
                    nc.vector.tensor_copy(pw[:, :, :], ps_p[:, 0:4, :])
                    nc.vector.tensor_copy(pst[:, :, :], ps_p[0:STR, 4:8, :])
                    nc.vector.tensor_copy(pn[:, :], ps_p[0:NJ, 8, :]).then_inc(probsT_ready, 1)
                    nc.vector.reciprocal(stat[:, 2:3], stat[:, 1:2]).then_inc(inverse, 1)
                    dve.wait_ge(inverse, 1)
                    dve.wait_ge(o_ready, 1)
                    nc.vector.scalar_tensor_tensor(out=part[:, :, :].rearrange("p h d -> p (h d)"), in0=ps_o[:, :], scalar=stat[:, 2:3],
                                                   in1=con("adiag"), op0=ALU.mult, op1=ALU.mult).then_inc(part_ready, 1)
                    dve.wait_ge(part_ready, 1)
                    nc.vector.tensor_reduce(o[:, :], part[:, :, :].rearrange("p h d -> p d h"), AX, ALU.add).then_inc(out_ready, 1)
            next_round(nc, sems)


class Compressor:

    def __init__(self, nc, ctx, con):
        self.nc, self.con = nc, con
        self.w1 = [ctx.enter_context(nc.sbuf_tensor(f"cmp_w1_{m}", [P, 16, CH], F32)) for m in range(2)]
        self.w2k = ctx.enter_context(nc.sbuf_tensor("cmp_w2k", [P, 2, 2, P], F32))
        self.w2v = ctx.enter_context(nc.sbuf_tensor("cmp_w2v", [P, 2, HD], F32))
        self.bias = ctx.enter_context(nc.sbuf_tensor("cmp_bias", [P, 2, 2], F32))

    def setup(self, w1, w2, pos):
        nc = self.nc
        with Phase(nc) as ctx:
            pe_in = ctx.enter_context(nc.sbuf_tensor("cmp_pos", [P, 2, 16], F32))
            ps = ctx.enter_context(nc.psum_tensor("cmp_ps", [P, 4], F32))
            loaded, zeroed, product, done = (ctx.semaphore(f"cmp_{n}") for n in "loaded zeroed product done".split())
            with nc.Block() as block:
                @block.sync
                def _(sp):
                    for m in range(2):
                        sp.dma_start(self.w1[m][:, :, :], w1[m].rearrange("(l p) f -> p l f", p=P)).then_inc(loaded, 16)
                        sp.dma_start(pe_in[:, m, :], pos[m].rearrange("(l a) d -> (a d) l", a=2),
                                     allow_slow_non_contiguous=True).then_inc(loaded, 16)
                    sp.dma_start(self.w2v[:, :, :], w2[1].rearrange("(c f) d -> f c d", f=P)).then_inc(loaded, 16)
                    sp.wait_ge(zeroed, 1)
                    for g in range(2):
                        sp.dma_start(self.w2k[:, :, g, g * HD:(g + 1) * HD],
                                     w2[0].rearrange("(c f) d -> f c d", f=P)).then_inc(loaded, 16)
                    sp.wait_ge(loaded, 16 * 7)

                @block.tensor
                def _(pe):
                    pe.wait_ge(loaded, 16 * 7)
                    for m in range(2):
                        for c in range(2):
                            for l in range(16):
                                last = nc.tensor.matmul(ps[:, 2 * m + c:2 * m + c + 1], self.w1[m][:, l, c * P:(c + 1) * P],
                                                        pe_in[:, m, l:l + 1], start=l == 0, stop=l == 15)
                    last.then_inc(product, 1)

                @block.vector
                def _(dve):
                    nc.vector.memset(self.w2k[:, :, :, :], 0.0).then_inc(zeroed, 1)
                    dve.wait_ge(product, 1)
                    nc.vector.tensor_copy(self.bias[:, :, :].rearrange("p m c -> p (m c)"), ps[:, :]).then_inc(done, 1)
                    dve.wait_ge(done, 1)

    def turn(self, x, q, pieces, out):
        for c in range(4):
            g, l = divmod(4 * q + c, 8)
            src = x[:, g, 2 * l:2 * l + 2, :].rearrange("p s d -> p (s d)")
            last = self.nc.tensor.transpose(out[:, c * P:c * P + pieces], src, self.con("ident")[0:pieces, 0:pieces])
        return last

    def hidden(self, m, xT, blocks, out, c):
        for l in range(16):
            s = 0 if l < 8 else 1
            last = self.nc.tensor.matmul(out[:, c * 256:c * 256 + 2 * blocks], self.w1[m][:, l, c * P:(c + 1) * P],
                                         xT[:, :, l % 8, s:s + blocks], start=l == 0, stop=l == 15)
        return last

    def down_k(self, hid, blocks, out):
        for x, (c, g) in enumerate([(c, g) for c in range(2) for g in range(2)]):
            last = self.nc.tensor.matmul(out, self.w2k[:, c, g, :], hid[:, c, g, :], start=x == 0, stop=x == 3)
        return last

    def down_v(self, hid, blocks, out):
        for g in range(2):
            for c in range(2):
                last = self.nc.tensor.matmul(out[:, g * HD:(g + 1) * HD], hid[:, c, g, :], self.w2v[:, c, :],
                                             start=c == 0, stop=c == 1)
        return last


def compress_prompt(nc, con, comp, h, kcmp, vcmp):
    with Phase(nc) as ctx:
        def sem(nm):
            return ctx.semaphore(f"cp_{nm}")
        x = [ctx.enter_context(nc.sbuf_tensor(f"cp_x{m}", [NPC, 2, 16, HD], F32)) for m in range(2)]
        xT = [ctx.enter_context(nc.sbuf_tensor(f"cp_xT{m}", [P, 2, 8, NPC], F32)) for m in range(2)]
        hid = [ctx.enter_context(nc.sbuf_tensor(f"cp_hid{m}", [P, 2, 2, NCB], F32)) for m in range(2)]
        kc = ctx.enter_context(nc.sbuf_tensor("cp_kc", [P, NCB], F32))
        vc = ctx.enter_context(nc.sbuf_tensor("cp_vc", [NCB, P], F32))
        ps_t = [ctx.enter_context(nc.psum_tensor(f"cp_t{b}", [P, 512], F32)) for b in range(2)]
        ps_h = [ctx.enter_context(nc.psum_tensor(f"cp_h{b}", [P, 512], F32)) for b in range(2)]
        ps_c = ctx.enter_context(nc.psum_tensor("cp_c", [P, 2, P], F32))
        loaded, turned, copied, hidden, active, products, ready, stored = (
            sem(n) for n in "loaded turned copied hidden active products ready stored".split())
        with nc.Block() as block:
            @block.sync
            def _(sp):
                for m, col in enumerate((KC, VC)):
                    for g in range(2):
                        sp.dma_start(x[m][:, g, :, :], h[0][:, col + g * HD:col + (g + 1) * HD].rearrange("(p s) c -> p s c", s=16)).then_inc(loaded, 16)
                sp.wait_ge(ready, 2)
                sp.dma_start(kcmp, kc[:, :]).then_inc(stored, 16)
                sp.dma_start(vcmp, vc[:, :]).then_inc(stored, 16)
                sp.wait_ge(stored, 32)

            @block.tensor
            def _(pe):
                pe.wait_ge(loaded, 64)
                for m in range(2):
                    for q in range(4):
                        g = 4 * m + q
                        if g >= 2:
                            pe.wait_ge(copied, g - 1)
                        comp.turn(x[m], q, NPC, ps_t[g % 2]).then_inc(turned, 1)
                for m in range(2):
                    pe.wait_ge(copied, 4 * (m + 1))
                    for c in range(2):
                        comp.hidden(m, xT[m], NCB, ps_h[m], c).then_inc(hidden, 1)
                pe.wait_ge(active, 4)
                comp.down_k(hid[0], NCB, ps_c[:, 0, 0:NCB])
                comp.down_v(hid[1], NCB, ps_c[0:NCB, 1, :]).then_inc(products, 1)

            @block.scalar
            def _(act):
                for m in range(2):
                    for c in range(2):
                        act.wait_ge(hidden, 2 * m + 2)
                        nc.scalar.activation(hid[m][:, c, :, :],
                                             ps_h[m][:, c * 256:c * 256 + 2 * NCB].rearrange("p (g b) -> p g b", g=2),
                                             ACT.Silu, bias=comp.bias[:, m, c:c + 1]).then_inc(active, 1)

            @block.vector
            def _(dve):
                for m in range(2):
                    for q in range(4):
                        dve.wait_ge(turned, 4 * m + q + 1)
                        nc.vector.tensor_copy(xT[m][:, q // 2, (q % 2) * 4:(q % 2) * 4 + 4, :],
                                              ps_t[q % 2][:, :].rearrange("p (l c) -> p l c", c=P)[:, :, 0:NPC]).then_inc(copied, 1)
                dve.wait_ge(products, 1)
                nc.vector.tensor_copy(kc[:, :], ps_c[:, 0, 0:NCB]).then_inc(ready, 1)
                nc.vector.tensor_copy(vc[:, :], ps_c[0:NCB, 1, :]).then_inc(ready, 1)


def attend_samples_sparse(nc, con, comp, h_s, pools, wins, page_table, branches, gathers):
    with Phase(nc) as ctx:
        def sb(nm, shape, dt=F32):
            return ctx.enter_context(nc.sbuf_tensor(f"ss_{nm}", shape, dt))

        def sem(nm):
            s = ctx.semaphore(f"ss_{nm}")
            sems.append(s)
            return s
        sems = []
        NKEY = PAST + NJ
        q_in = sb("q_in", [NS, 8, 2, HD])
        q_all = sb("q_all", [P, NB, 64])
        q_cur = sb("q_cur", [P, 64])
        pages = sb("pages", [P, NB + 1], I32)
        rows = sb("rows", [P, NB + 1], I32)
        pages_f, rows_f = sb("pages_f", [P, NB + 1]), sb("rows_f", [P, NB + 1])
        row_cur = sb("row_cur", [P, 1], I32)
        kc_in, vc_in, ks_in, vs_in = (sb(n, [P, 16, P]) for n in "kc_in vc_in ks_in vs_in".split())
        kc_p, vc_p = sb("kc_p", [P, 2, 16, HD]), sb("vc_p", [P, 2, 16, HD])
        kw_in, vw_in = sb("kw_in", [P, 4, P]), sb("vw_in", [P, 4, P])
        new_in = sb("new_in", [NJ, 4, P])
        xT = sb("xT", [P, 2, 8, P])
        hid = sb("hid", [P, 2, 2, NCS])
        kc, vc = sb("kc", [P, NCS]), sb("vc", [NCS, P])
        ksT, kwT, newT = sb("ksT", [P, PAST]), sb("kwT", [P, 512]), sb("newT", [P, 2, NJ])
        pc, pcT = sb("pc", [64, NCS]), sb("pcT", [NCS, 64])
        share, score, score2, top = sb("share", [64, NSL]), sb("score", [64, NSL]), sb("score2", [64, NSL]), sb("top", [64, 8])
        bias_b, bias = sb("bias_b", [64, NSL]), sb("bias", [64, 32, 4])
        psel, pwin = sb("psel", [64, NKEY]), sb("pwin", [64, 512 + NJ])
        pselT, pselnT = sb("pselT", [P, 16, 64]), sb("pselnT", [NJ, 64])
        pwinT, pwinnT = sb("pwinT", [P, 4, 64]), sb("pwinnT", [NJ, 64])
        mins, stat = sb("mins", [64, 8]), sb("stat", [64, 3, 3])
        o = sb("o", [64, 3, HD])
        ps_t = [ctx.enter_context(nc.psum_tensor(f"ss_ps_t{b}", [P, 512], F32)) for b in range(2)]
        ps_s = ctx.enter_context(nc.psum_tensor("ss_ps_s", [64, 4, 512], F32))
        ps_h = ctx.enter_context(nc.psum_tensor("ss_ps_h", [P, 512], F32))
        ps_m = ctx.enter_context(nc.psum_tensor("ss_ps_m", [P, 512], F32))
        M_KC, M_CS, M_SH, M_SUM, M_NEW, M_O = (slice(0, P), slice(128, 128 + NCS), slice(256, 256 + NSL), slice(290, 290 + NSL),
                                               slice(324, 332), slice(384, 512))
        pre = {n: ctx.semaphore(f"ss_{n}") for n in
               "table_in index_step index_ready first_in q_loaded q_zero q_turned q_placed".split()}
        s = {n: sem(n) for n in
             ("row_ready pieces_k pieces_v new_read sum_read win_in q_ready turned copied_act copied_dve hid_k act_k prod_k kc_ready "
              "cmp_scores cmp_max cmp_probs cmp_norm share_raw share_ready sum_raw bias_ready sel_scores sel_max sel_probs "
              "hid_v act_v prod_v vc_ready cmp_o cmp_o_ready win_scores win_max win_probs sel_o sel_o_ready win_o win_o_ready "
              "probsT_small stored dve_step").split()}
        copied = [s["copied_act"], s["copied_dve"]]

        def gather(pool, to, m, which):
            return pool.indirect_dma_start(out=to[:, :, :].rearrange("p s c -> p (s c)"), out_offset=None,
                                           in_=pools[m], in_offset=bass.IndirectOffsetOnAxis(ap=row_cur[:, 0:1], axis=0)
                                           ).then_inc(which, 16)

        def load_windows(sp, n, which):
            for to, fr in ((kw_in, wins[0]), (vw_in, wins[1])):
                sp.dma_start(to[:, :, :].rearrange("p s c -> p (s c)"),
                             fr[bass.ds(n, 1)].rearrange("n (p s) c -> p (n s c)", s=4)).then_inc(which, 16)
            sp.dma_start(new_in[:, :, :].rearrange("j m c -> j (m c)"), h_s[bass.ds(n * NJ, NJ), KS:KS + 512]).then_inc(which, 16)

        with nc.Block() as block:
            @block.sync
            def _(sp):
                for g in range(2):
                    sp.dma_start(q_in[:, :, g, :], h_s[:, QC + g * 512:QC + (g + 1) * 512].rearrange("t (r d) -> t r d", d=HD)
                                 ).then_inc(pre["q_loaded"], 16)
                for pg in range(PAST // PAGE):
                    for col, n0, n in ((0, 0, NB), (NB, 0, 1)):
                        sp.dma_start(pages[pg * 8:(pg + 1) * 8, col:col + n],
                                     page_table[n0:n0 + n, pg:pg + 1].rearrange("n a -> a n").broadcast_to([8, n]),
                                     allow_slow_non_contiguous=True).then_inc(pre["table_in"], 16)
                load_windows(sp, 0, pre["first_in"])
                sp.wait_ge(pre["first_in"], 48)

            @block.gpsimd
            def _(pool):
                pool.wait_ge(pre["index_ready"], 1)
                for m, to in enumerate((kc_in, vc_in, ks_in, vs_in)):
                    gather(pool, to, m, gathers["first"])
                pool.wait_ge(gathers["first"], 64)

            @block.tensor
            def _(pe):
                pe.wait_ge(pre["q_loaded"], 32)
                for r in range(8):
                    last = nc.tensor.transpose(ps_t[0][:, r * NS:(r + 1) * NS], q_in[:, r, :, :].rearrange("t g d -> t (g d)"), con("ident")[0:NS, 0:NS])
                last.then_inc(pre["q_turned"], 1)

            @block.vector
            def _(dve):
                count = 0

                def link(ins):
                    nonlocal count
                    count += 1
                    ins.then_inc(pre["index_step"], 1)
                    dve.wait_ge(pre["index_step"], count)
                dve.wait_ge(pre["table_in"], 16 * 2 * (PAST // PAGE))
                link(nc.vector.tensor_copy(pages_f[:, :], pages[:, :]))
                link(nc.vector.tensor_scalar(rows_f[:, :], pages_f[:, :], 8.0, con("sub"), ALU.mult, ALU.add))
                link(nc.vector.tensor_copy(rows[:, :], rows_f[:, :]))
                nc.vector.tensor_copy(row_cur[:, :], rows[:, 0:1]).then_inc(pre["index_ready"], 1)
                nc.vector.memset(q_all[:, :, :], 0.0).then_inc(pre["q_zero"], 1)
                dve.wait_ge(pre["q_zero"], 1)
                dve.wait_ge(pre["q_turned"], 1)
                to = q_all[:, :, :].rearrange("p n (g r j) -> p n g r j", g=2, r=8)
                for g in range(2):
                    half = slice(g * HD, (g + 1) * HD)
                    src = ps_t[0][half, 0:256].rearrange("p (r n j) -> p n r j", r=8, n=NB)
                    last = nc.vector.tensor_scalar(to[half, :, g, :, :], src, -SCALE, None, ALU.mult)
                last.then_inc(pre["q_placed"], 1)
                dve.wait_ge(pre["q_placed"], 1)

        def v4(ap):
            return ap.rearrange("p (c k) -> p c k", c=4)
        G_SEL, G_CK, G_WIN, G_NEW, G_CV, G_PC, G_PS, G_PW = 0, 4, 8, 9, 10, 14, 15, 17
        N_GROUPS = 18

        with nc.Fori(0, NB) as n:
            with nc.Block() as block:
                @block.sync
                def _(sp):
                    sp.wait_ge(s["win_o"], 1)
                    load_windows(sp, (n + 1) % NB, s["win_in"])
                    for b, ready in enumerate(("cmp_o_ready", "sel_o_ready", "win_o_ready")):
                        sp.wait_ge(s[ready], 1)
                        for hh in range(16):
                            sp.dma_start(branches[b, bass.ds(n * NJ, NJ), hh * HD:(hh + 1) * HD],
                                         o[hh * NJ:(hh + 1) * NJ, b, :]).then_inc(s["stored"], 16)
                    sp.wait_ge(s["stored"], 16 * 48)
                    sp.wait_ge(s["win_in"], 48)

                @block.gpsimd
                def _(pool):
                    nc.gpsimd.tensor_copy(row_cur[:, :], rows[:, bass.ds(n + 1, 1)]).then_inc(s["row_ready"], 1)
                    pool.wait_ge(s["row_ready"], 1)
                    for m, (to, fr, done) in enumerate(((kc_p, kc_in, "pieces_k"), (vc_p, vc_in, "pieces_v"))):
                        nc.gpsimd.tensor_copy(to[:, :, :, :], fr[:, :, :].rearrange("p s (g d) -> p g s d", g=2)).then_inc(s[done], 1)
                        pool.wait_ge(s[done], 1)
                        gather(pool, fr, m, gathers["kc" if m == 0 else "vc"])
                    pool.wait_ge(s["turned"], G_SEL + 4)
                    gather(pool, ks_in, 2, gathers["ks"])
                    pool.wait_ge(s["sel_o"], 1)
                    gather(pool, vs_in, 3, gathers["vs"])
                    for which in ("ks", "kc", "vc", "vs"):
                        pool.wait_ge(gathers[which], (n + 1) * 16)

                def copy_group(eng, copy, g):
                    eng.wait_ge(s["turned"], g + 1)
                    src = ps_t[g % 2]
                    done = copied[g % 2]
                    if g < G_CK:
                        copy(ksT[:, g * 512:(g + 1) * 512], src[:, :]).then_inc(done, 1)
                    elif g < G_WIN or G_CV <= g < G_PC:
                        if g == G_CV:
                            eng.wait_ge(s["hid_k"], 2)
                        if g == G_CV + 1:
                            eng.wait_ge(s["hid_k"], 2)
                        q = g - G_CK if g < G_WIN else g - G_CV
                        copy(xT[:, q // 2, (q % 2) * 4:(q % 2) * 4 + 4, :], v4(src[:, :])).then_inc(done, 1)
                    elif g == G_WIN:
                        copy(kwT[:, :], src[:, :]).then_inc(done, 1)
                    elif g == G_NEW:
                        copy(newT[:, :, :], src[:, 0:2 * NJ].rearrange("p (m j) -> p m j", j=NJ)).then_inc(done, 1)
                    elif g == G_PC:
                        copy(pcT[:, :], src[0:NCS, 0:64]).then_inc(done, 1)
                    elif g < G_PW:
                        x = g - G_PS
                        copy(pselT[:, 8 * x:8 * x + 8, :], src[:, :].rearrange("p (c k) -> p c k", c=8)).then_inc(done, 1)
                    else:
                        copy(pwinT[:, :, :], src[:, 0:256].rearrange("p (c k) -> p c k", c=4))
                        copy(pselnT[:, :], src[0:NJ, 256:320])
                        copy(pwinnT[:, :], src[0:NJ, 320:384]).then_inc(done, 1)

                @block.tensor
                def _(pe):
                    id64 = con("ident")[0:64, 0:64]

                    def bank(g):
                        if g >= 2:
                            pe.wait_ge(copied[g % 2], g // 2)
                        return ps_t[g % 2]

                    def all_copied(g):
                        pe.wait_ge(copied[0], g // 2 + 1)
                        pe.wait_ge(copied[1], (g + 1) // 2)
                    for g in range(G_SEL, G_SEL + 4):
                        to = bank(g)
                        for c in range(4):
                            last = nc.tensor.transpose(to[:, c * P:(c + 1) * P], ks_in[:, 4 * g + c, :], con("ident"))
                        last.then_inc(s["turned"], 1)
                    pe.wait_ge(s["pieces_k"], 1)
                    for q in range(4):
                        comp.turn(kc_p, q, P, bank(G_CK + q)).then_inc(s["turned"], 1)
                    to = bank(G_WIN)
                    for c in range(4):
                        last = nc.tensor.transpose(to[:, c * P:(c + 1) * P], kw_in[:, c, :], con("ident"))
                    last.then_inc(s["turned"], 1)
                    to = bank(G_NEW)
                    for c in range(2):
                        last = nc.tensor.transpose(to[:, c * NJ:(c + 1) * NJ], new_in[:, 2 * c, :], con("ident")[0:NJ, 0:NJ])
                    last.then_inc(s["turned"], 1)
                    all_copied(G_NEW)
                    pe.wait_ge(s["q_ready"], 1)
                    for c in range(2):
                        comp.hidden(0, xT, NCS, ps_h, c).then_inc(s["hid_k"], 1)
                    for c in range(4):
                        nc.tensor.matmul(ps_s[:, c, :], q_cur[:, :], ksT[:, c * 512:(c + 1) * 512], start=True, stop=True)
                    nc.tensor.matmul(ps_m[0:64, M_NEW.start:M_NEW.start + NJ], q_cur[:, :], newT[:, 0, :], start=True, stop=True)
                    nc.tensor.matmul(ps_m[0:64, M_NEW.start + NJ:M_NEW.stop], q_cur[:, :], newT[:, 1, :], start=True,
                                     stop=True).then_inc(s["sel_scores"], 1)
                    pe.wait_ge(s["act_k"], 2)
                    pe.wait_ge(s["new_read"], 1)
                    comp.down_k(hid, NCS, ps_m[:, 0:NCS]).then_inc(s["prod_k"], 1)
                    pe.wait_ge(s["pieces_v"], 1)
                    for q in range(4):
                        comp.turn(vc_p, q, P, bank(G_CV + q)).then_inc(s["turned"], 1)
                    pe.wait_ge(s["kc_ready"], 1)
                    nc.tensor.matmul(ps_m[0:64, M_CS], q_cur[:, :], kc[:, :], start=True, stop=True).then_inc(s["cmp_scores"], 1)
                    all_copied(G_CV + 3)
                    for c in range(2):
                        comp.hidden(1, xT, NCS, ps_h, c).then_inc(s["hid_v"], 1)
                    pe.wait_ge(s["cmp_norm"], 1)
                    to = bank(G_PC)
                    nc.tensor.transpose(to[0:NCS, 0:64], pc[:, :], id64).then_inc(s["turned"], 1)
                    all_copied(G_PC)
                    nc.tensor.matmul(ps_m[0:64, M_SH], pcT[:, :], con("overlap"), start=True, stop=True).then_inc(s["share_raw"], 1)
                    pe.wait_ge(s["share_ready"], 1)
                    nc.tensor.matmul(ps_m[0:64, M_SUM], con("same"), share[:, :], start=True, stop=True).then_inc(s["sum_raw"], 1)
                    pe.wait_ge(s["act_v"], 2)
                    pe.wait_ge(s["sum_read"], 1)
                    comp.down_v(hid, NCS, ps_m[0:NCS, M_KC]).then_inc(s["prod_v"], 1)
                    nc.tensor.matmul(ps_h[0:64, :], q_cur[:, :], kwT[:, :], start=True, stop=True).then_inc(s["win_scores"], 1)
                    pe.wait_ge(s["vc_ready"], 1)
                    nc.tensor.matmul(ps_m[0:64, M_O], pcT[:, :], vc[:, :], start=True, stop=True).then_inc(s["cmp_o"], 1)
                    pe.wait_ge(s["sel_probs"], 1)
                    for g in (G_PS, G_PS + 1):
                        to = bank(g)
                        for c in range(8):
                            k0 = (8 * (g - G_PS) + c) * P
                            last = nc.tensor.transpose(to[:, c * 64:(c + 1) * 64], psel[:, k0:k0 + P], id64)
                        last.then_inc(s["turned"], 1)
                    pe.wait_ge(s["win_probs"], 1)
                    to = bank(G_PW)
                    for c in range(4):
                        nc.tensor.transpose(to[:, c * 64:(c + 1) * 64], pwin[:, c * P:(c + 1) * P], id64)
                    nc.tensor.transpose(to[0:NJ, 256:320], psel[:, PAST:NKEY], id64)
                    nc.tensor.transpose(to[0:NJ, 320:384], pwin[:, 512:512 + NJ], id64).then_inc(s["turned"], 1)
                    all_copied(G_PW)
                    pe.wait_ge(s["cmp_o_ready"], 1)
                    for c in range(16):
                        nc.tensor.matmul(ps_m[0:64, M_O], pselT[:, c, :], vs_in[:, c, :], start=c == 0, stop=False)
                    nc.tensor.matmul(ps_m[0:64, M_O], pselnT[:, :], new_in[:, 1, :], start=False, stop=True).then_inc(s["sel_o"], 1)
                    pe.wait_ge(s["sel_o_ready"], 1)
                    for c in range(4):
                        nc.tensor.matmul(ps_m[0:64, M_O], pwinT[:, c, :], vw_in[:, c, :], start=c == 0, stop=False)
                    nc.tensor.matmul(ps_m[0:64, M_O], pwinnT[:, :], new_in[:, 3, :], start=False, stop=True).then_inc(s["win_o"], 1)

                @block.scalar
                def _(act):
                    def silu(m, done, hidden):
                        act.wait_ge(s[hidden], 2)
                        if m == 1:
                            act.wait_ge(s["prod_k"], 1)
                        for c in range(2):
                            nc.scalar.activation(hid[:, c, :, :],
                                                 ps_h[:, c * 256:c * 256 + 2 * NCS].rearrange("p (g b) -> p g b", g=2),
                                                 ACT.Silu, bias=comp.bias[:, m, c:c + 1]).then_inc(s[done], 1)
                    for g in range(0, G_CV, 2):
                        copy_group(act, nc.scalar.copy, g)
                    silu(0, "act_k", "hid_k")
                    copy_group(act, nc.scalar.copy, G_CV)
                    copy_group(act, nc.scalar.copy, G_CV + 2)
                    act.wait_ge(s["cmp_max"], 1)
                    nc.scalar.activation(pc[:, :], ps_m[0:64, M_CS], ACT.Exp, scale=-1.0, bias=stat[:, 0, 0:1],
                                         accum_out=stat[:, 0, 1:2]).then_inc(s["cmp_probs"], 1)
                    copy_group(act, nc.scalar.copy, G_PC)
                    silu(1, "act_v", "hid_v")
                    act.wait_ge(s["sel_max"], 1)
                    nc.scalar.activation(psel[:, :], psel[:, :], ACT.Exp, scale=-1.0, bias=stat[:, 1, 0:1],
                                         accum_out=stat[:, 1, 1:2]).then_inc(s["sel_probs"], 1)
                    act.wait_ge(s["win_max"], 1)
                    nc.scalar.activation(pwin[:, :], pwin[:, :], ACT.Exp, scale=-1.0, bias=stat[:, 2, 0:1],
                                         accum_out=stat[:, 2, 1:2]).then_inc(s["win_probs"], 1)
                    copy_group(act, nc.scalar.copy, G_PS + 1)

                @block.vector
                def _(dve):
                    count = 0

                    def link(ins):
                        nonlocal count
                        count += 1
                        ins.then_inc(s["dve_step"], 1)
                        dve.wait_ge(s["dve_step"], count)

                    def write_out(b, done, ready):
                        dve.wait_ge(s[done], 1)
                        for g in range(2):
                            r = slice(32 * g, 32 * g + 32)
                            src = ps_m[r, M_O.start + g * HD:M_O.start + (g + 1) * HD]
                            if b == 0:
                                last = nc.vector.tensor_copy(o[r, b, :], src)
                            else:
                                last = nc.vector.tensor_scalar(o[r, b, :], src, stat[r, b, 2:3], None, ALU.mult)
                        last.then_inc(s[ready], 1)
                    nc.vector.tensor_copy(q_cur[:, :], q_all[:, bass.ds(n, 1), :].rearrange("p n c -> p (n c)")).then_inc(s["q_ready"], 1)
                    for g in range(1, G_CV, 2):
                        copy_group(dve, nc.vector.tensor_copy, g)
                    dve.wait_ge(s["sel_scores"], 1)
                    for x, dst in enumerate((psel[:, PAST:NKEY], pwin[:, 512:512 + NJ])):
                        last = nc.vector.tensor_tensor_reduce(out=dst, in0=ps_m[0:64, M_NEW.start + x * NJ:M_NEW.start + (x + 1) * NJ],
                                                              in1=con("newmask"), scale=1.0, scalar=3e38, op0=ALU.add,
                                                              op1=ALU.min, accum_out=mins[:, 4 + x:5 + x])
                    last.then_inc(s["new_read"], 1)
                    dve.wait_ge(s["prod_k"], 1)
                    nc.vector.tensor_copy(kc[:, :], ps_m[:, 0:NCS]).then_inc(s["kc_ready"], 1)
                    copy_group(dve, nc.vector.tensor_copy, G_CV + 1)
                    dve.wait_ge(s["cmp_scores"], 1)
                    nc.vector.tensor_reduce(stat[:, 0, 0:1], ps_m[0:64, M_CS], AX, ALU.min).then_inc(s["cmp_max"], 1)
                    copy_group(dve, nc.vector.tensor_copy, G_CV + 3)
                    dve.wait_ge(s["cmp_probs"], 1)
                    link(nc.vector.reciprocal(stat[:, 0, 2:3], stat[:, 0, 1:2]))
                    nc.vector.tensor_scalar(pc[:, :], pc[:, :], stat[:, 0, 2:3], None, ALU.mult).then_inc(s["cmp_norm"], 1)
                    dve.wait_ge(s["share_raw"], 1)
                    nc.vector.tensor_copy(share[:, :], ps_m[0:64, M_SH]).then_inc(s["share_ready"], 1)
                    dve.wait_ge(s["sum_raw"], 1)
                    nc.vector.tensor_copy(score[:, :], ps_m[0:64, M_SUM]).then_inc(s["sum_read"], 1)
                    dve.wait_ge(s["sum_read"], 1)
                    nc.vector.memset(score[:, 0:1], 1e9)
                    link(nc.vector.memset(score[:, 31:33], 1e9))
                    link(nc.vector.max(top[:, :], score[:, :]))
                    link(nc.vector.match_replace(score2[:, :], top[:, :], score[:, :], -3e38))
                    link(nc.vector.max(top[:, :], score2[:, :]))
                    link(nc.vector.match_replace(score[:, :], top[:, :], score2[:, :], -3e38))
                    link(nc.vector.tensor_scalar(bias_b[:, :], score[:, :], -1e37, BIG, ALU.is_gt, ALU.mult))
                    link(nc.vector.tensor_copy(bias[:, :, :], bias_b[:, 0:32].unsqueeze(2).broadcast_to([64, 32, 4])))
                    dve.wait_ge(s["sel_scores"], 1)
                    fb = bias[:, :, :].rearrange("p b s -> p (b s)").unsqueeze(1).broadcast_to([64, 4, P])
                    for c in range(4):
                        last = nc.vector.tensor_tensor_reduce(out=psel[:, c * 512:(c + 1) * 512].rearrange("p (s k) -> p s k", s=4),
                                                       in0=ps_s[:, c, :].rearrange("p (s k) -> p s k", s=4), in1=fb,
                                                       scale=1.0, scalar=3e38, op0=ALU.add, op1=ALU.min,
                                                       accum_out=mins[:, c:c + 1])
                        last.then_inc(s["dve_step"], 1)
                        count += 1
                    dve.wait_ge(s["dve_step"], count)
                    nc.vector.tensor_reduce(stat[:, 1, 0:1], mins[:, 0:5], AX, ALU.min).then_inc(s["sel_max"], 1)
                    dve.wait_ge(s["prod_v"], 1)
                    nc.vector.tensor_copy(vc[:, :], ps_m[0:NCS, M_KC]).then_inc(s["vc_ready"], 1)
                    dve.wait_ge(s["win_scores"], 1)
                    link(nc.vector.tensor_tensor_reduce(out=pwin[:, 0:512], in0=ps_h[0:64, :], in1=con("winmask"), scale=1.0,
                                                        scalar=3e38, op0=ALU.add, op1=ALU.min, accum_out=mins[:, 6:7]))
                    nc.vector.tensor_reduce(stat[:, 2, 0:1], mins[:, 5:7], AX, ALU.min).then_inc(s["win_max"], 1)
                    write_out(0, "cmp_o", "cmp_o_ready")
                    copy_group(dve, nc.vector.tensor_copy, G_PS)
                    dve.wait_ge(s["sel_probs"], 1)
                    dve.wait_ge(s["win_probs"], 1)
                    link(nc.vector.reciprocal(stat[:, 1:3, 2], stat[:, 1:3, 1]))
                    copy_group(dve, nc.vector.tensor_copy, G_PW)
                    write_out(1, "sel_o", "sel_o_ready")
                    write_out(2, "win_o", "win_o_ready")
            next_round(nc, sems)


def mix_sample_branches(nc, h_s, branches, mix_s):
    with Phase(nc) as ctx:
        b = ctx.enter_context(nc.sbuf_tensor("mb_b", [NS, 3, D], F32))
        gl = ctx.enter_context(nc.sbuf_tensor("mb_gl", [NS, 48], F32))
        out = ctx.enter_context(nc.sbuf_tensor("mb_out", [NS, D], F32))
        loaded, gates, step, ready, stored = (ctx.semaphore(f"mb_{n}") for n in "loaded gates step ready stored".split())
        with nc.Block() as block:
            @block.sync
            def _(sp):
                sp.dma_start(b[:, :, :], branches.rearrange("b t c -> t b c")).then_inc(loaded, 16)
                sp.dma_start(gl[:, :], h_s[:, GL:GL + 48]).then_inc(loaded, 16)
                sp.wait_ge(ready, 1)
                sp.dma_start(mix_s, out[:, :]).then_inc(stored, 16)
                sp.wait_ge(stored, 16)

            @block.scalar
            def _(act):
                act.wait_ge(loaded, 32)
                nc.scalar.activation(gl[:, :], gl[:, :], ACT.Sigmoid).then_inc(gates, 1)

            @block.vector
            def _(dve):
                dve.wait_ge(loaded, 32)
                dve.wait_ge(gates, 1)
                for x in range(3):
                    v = b[:, x, :].rearrange("t (h d) -> t h d", d=HD)
                    g = gl[:, :].rearrange("t (h x) -> t h x", x=3)[:, :, x].unsqueeze(2).broadcast_to([NS, 16, HD])
                    last = nc.vector.tensor_tensor(v, v, g, ALU.mult)
                last.then_inc(step, 1)
                dve.wait_ge(step, 1)
                nc.vector.tensor_tensor(out[:, :], b[:, 0, :], b[:, 1, :], ALU.add).then_inc(step, 1)
                dve.wait_ge(step, 2)
                nc.vector.tensor_tensor(out[:, :], out[:, :], b[:, 2, :], ALU.add).then_inc(ready, 1)


def store_rows(nc, name, pairs):
    with Phase(nc) as ctx:
        stored = ctx.semaphore(f"{name}_stored")
        with nc.Block() as block:
            @block.sync
            def _(sp):
                for to, fr in pairs:
                    sp.dma_start(to, fr).then_inc(stored, 16)
                sp.wait_ge(stored, 16 * len(pairs))


class Constants:

    def __init__(self, nc, ctx, dram):
        self.all = ctx.enter_context(nc.sbuf_tensor("constants", [P, CONST.shape[1]], F32))
        t16 = ctx.enter_context(nc.sbuf_tensor("constants16", [P, 3 * P + NT * NCB], BF16))
        self.ident16, self.causal16, self.edge16 = (t16[:, k * P:(k + 1) * P] for k in range(3))
        self.cmask16 = t16[:, 3 * P:].rearrange("p (t c) -> p t c", t=NT)
        self.rows = {n: P for n in COLS}
        self.rows.update(asbias=32, adiag=32, newmask=64, winmask=64, same=64, overlap=NCS, intra_s=NS, qdec_s=NS,
                         kdec_s=NS, kmask_s=NS)
        with Phase(nc) as phase, nc.Block() as block:
            loaded, cast = phase.semaphore("constants_in"), phase.semaphore("constants_cast")

            @block.sync
            def _(sp):
                sp.dma_start(self.all[:, :], dram).then_inc(loaded, 16)

            @block.vector
            def _(dve):
                dve.wait_ge(loaded, 16)
                for to, name in ((self.ident16, "ident"), (self.causal16, "causal"), (self.edge16, "edge"), (t16[:, 3 * P:], "cmask")):
                    last = nc.vector.tensor_copy(to, self(name))
                last.then_inc(cast, 1)
                dve.wait_ge(cast, 1)

    def __call__(self, name):
        a, b = COLS[name]
        return self.all[0:self.rows[name], a:b]


def build(nc, i, o):
    h0 = nc.dram_tensor("h0", [ROWS, E_COLS], F32, kind="Internal").ap()
    h1 = nc.dram_tensor("h1", [ROWS, O_COLS], F32, kind="Internal").ap()
    mix0 = nc.dram_tensor("mix0", [ROWS, D], F32, kind="Internal").ap()
    mix1 = nc.dram_tensor("mix1", [ROWS, D], F32, kind="Internal").ap()
    x1 = nc.dram_tensor("x1", [ROWS, D], F32, kind="Internal").ap()
    x2 = nc.dram_tensor("x2", [ROWS, D], F32, kind="Internal").ap()
    kcmp = nc.dram_tensor("kcmp", [P, NCB], F32, kind="Internal").ap()
    vcmp = nc.dram_tensor("vcmp", [NCB, P], F32, kind="Internal").ap()
    branches = nc.dram_tensor("branches", [3, NS, D], F32, kind="Internal").ap()

    def both(a):
        return a[0:T, :], a[T:ROWS, :]
    with ExitStack() as ctx:
        con = Constants(nc, ctx, i["const"])
        gathers = {n: ctx.enter_context(nc.semaphore("gathered_" + n)) for n in ("first", "kc", "vc", "ks", "vs")}
        ident = con("ident")
        x0 = (i["x_prompt"], i["x_sample"])
        project(nc, ident, "norm", x0, i["even_w_in"], E_COLS, both(h0), gain=i["even_norm"])
        store_rows(nc, "even", [(o["a_k_p"], h0[0:T, KA:KA + 512]), (o["a_k_s"], h0[T:, KA:KA + 512]),
                                (o["a_v_p"], h0[0:T, VA:VA + 512]), (o["a_v_s"], h0[T:, VA:VA + 512])])
        attend_prompt(nc, con, "dilated", both(h0), mix0, 4)
        retain(nc, con, both(h0), mix0, i["trig"], o["ret_p"])
        retain(nc, con, both(h0), mix0, i["trig"], o["ret_s"], state_in=i["state_ret"])
        attend_samples_dilated(nc, con, h0[T:ROWS, :], i["cache_a_k"], i["cache_a_v"], mix0)
        project(nc, ident, "gate", both(mix0), i["even_w_out"], D, both(x1),
                gates=(both(h0), (ZA, ZA + 512), (ZB, ZB + 512)), residual=x0)
        project(nc, ident, "norm", both(x1), i["odd_w_in"], O_COLS, both(h1), gain=i["odd_norm"])
        pairs = []
        for name, col in (("kc", KC), ("vc", VC), ("ks", KS), ("vs", VS), ("kw", KW), ("vw", VW)):
            first = T - 512 if name in ("kw", "vw") else 0
            pairs.append((o[name + "_p"], h1[first:T, col:col + P]))
            pairs.append((o[name + "_s"], h1[T:, col:col + P]))
        store_rows(nc, "odd", pairs)
        with ExitStack() as inner:
            comp = Compressor(nc, inner, con)
            comp.setup((i["cmp_w1_k"], i["cmp_w1_v"]), (i["cmp_w2_k"], i["cmp_w2_v"]), (i["cmp_pos_k"], i["cmp_pos_v"]))
            compress_prompt(nc, con, comp, both(h1), kcmp, vcmp)
            attend_samples_sparse(nc, con, comp, h1[T:ROWS, :], [i["pool_" + n] for n in ("kc", "vc", "ks", "vs")],
                                  (i["cache_c_kwin"], i["cache_c_vwin"]), i["page_table"], branches, gathers)
        mix_sample_branches(nc, h1[T:ROWS, :], branches, mix1[T:ROWS, :])
        attend_prompt(nc, con, "sparse", both(h1), mix1, 8, kcmp, vcmp)
        project(nc, ident, "gate", both(mix1), i["odd_w_out"], D, both(x2), gates=(both(h1), (ZC, ZC + D)), residual=both(x1))
        final_norm(nc, both(x2), i["final_norm"], (o["y_p"], o["y_s"]))


_IN = {"x_prompt": (T, D), "x_sample": (NS, D), "cache_a_k": (NB, PAST, 512), "cache_a_v": (NB, PAST, 512),
       "state_ret": (NB, BH, HD, BDV), "cache_c_kcmp": (NPOOL * 8, 2048), "cache_c_vcmp": (NPOOL * 8, 2048),
       "cache_c_ksel": (NPOOL * 8, 2048), "cache_c_vsel": (NPOOL * 8, 2048), "cache_c_kwin": (NB, 512, P),
       "cache_c_vwin": (NB, 512, P), "page_table": (NB, PAST // PAGE), "even_norm": (D,), "even_w_in": (D, E_COLS),
       "even_w_out": (D, D), "odd_norm": (D,), "odd_w_in": (D, O_COLS), "odd_w_out": (D, D), "cmp_pos_k": (32, HD),
       "cmp_w1_k": (2048, CH), "cmp_w2_k": (CH, HD), "cmp_pos_v": (32, HD), "cmp_w1_v": (2048, CH), "cmp_w2_v": (CH, HD),
       "final_norm": (D,)}
_OUT = [("y_p", (1, T, D)), ("y_s", (NB, NJ, D)), ("a_k_p", (1, 1, T, 8, HD)), ("a_k_s", (1, NB, NJ, 8, HD)),
        ("a_v_p", (1, 1, T, 8, HD)), ("a_v_s", (1, NB, NJ, 8, HD)), ("ret_p", (1, 1, BH, HD, BDV)),
        ("ret_s", (1, NB, BH, HD, BDV))] + [
    (f"{n}_{w}", ((1, 1, T // (2 if n in ("kw", "vw") else 1), 2, HD) if w == "p" else (1, NB, NJ, 2, HD)))
    for n in ("kc", "vc", "ks", "vs", "kw", "vw") for w in ("p", "s")]


def kernel(**inputs):
    import concourse.bacc as _bacc
    from concourse.bass_utils import run_bass_kernel_spmd as _run

    nc = _bacc.Bacc("TRN2", target_bir_lowering=False, num_devices=1)
    arrays, ins, outs = {}, {}, {}
    laid = {n: np.ascontiguousarray(inputs[n]).reshape(shape) for n, shape in _IN.items()}
    laid["const"], laid["trig"] = CONST, TRIG
    for name, a in laid.items():
        arrays["in_" + name] = a
        ins[name] = nc.dram_tensor("in_" + name, a.shape, mybir.dt.from_np(a.dtype), kind="ExternalInput").ap()
    for short, full in (("kc", "kcmp"), ("vc", "vcmp"), ("ks", "ksel"), ("vs", "vsel")):
        ins["pool_" + short] = ins["cache_c_" + full]
    flat = {"y_p": (T, D), "y_s": (NS, D), "ret_p": (BH, HD, BDV), "ret_s": (NB, BH, HD, BDV)}
    for name, shape in _OUT:
        cols = 512 if name[:2] == "a_" else P
        s2 = flat.get(name, (int(np.prod(shape)) // cols, cols))
        outs[name] = nc.dram_tensor("out_" + name, s2, F32, kind="ExternalOutput").ap()
    build(nc, ins, outs)
    r = _run(nc, [arrays], core_ids=[0])
    return tuple(r.results[0]["out_" + name].reshape(shape) for name, shape in _OUT)
```

```python
import concourse.bass as bass
from concourse import mybir
import numpy as np
import math
from contextlib import ExitStack

F32 = mybir.dt.float32
BF16 = mybir.dt.bfloat16
F32R = mybir.dt.float32r
I32 = mybir.dt.int32
ALU = mybir.AluOpType
ACT = mybir.ActivationFunctionType
AX = mybir.AxisListType.X

P = 128
D = 1024
T = 1024
NT = T // P
NB, NJ = 8, 4
NS = NB * NJ
ROWS = T + NS
HD = 64
PAST = 2048
PAGE = 128
NPOOL = 160
SCALE = HD ** -0.5
BIG = 1e30
EPS_RMS, EPS_GN = 1e-6, 1e-5
QA, KA, VA, ZA, QB, KB, VB, ZB, E_COLS = 0, 512, 1024, 1536, 2048, 2304, 2560, 3072, 3584
QC, KC, VC, KS, VS, KW, VW, GL, ZC, O_COLS = 0, 1024, 1152, 1280, 1408, 1536, 1664, 1792, 1840, 2864
KD = D // P
CUT_AFTER = 5
BH, BDV = 4, 128
NPC = T // 16
NCB = NPC - 1
NPS = PAST // 16
NCS = NPS - 1
NSL = 33
CH = 256
STR = 96
AK = 4 * P + 4 * STR + NJ


def _constants():
    cols, parts = {}, []

    def put(name, a):
        a = np.asarray(a, np.float64).reshape(np.asarray(a).shape[0], -1)
        full = np.zeros((P, a.shape[1]), np.float32)
        full[:a.shape[0]] = a
        at = sum(x.shape[1] for x in parts)
        parts.append(full)
        cols[name] = (at, at + a.shape[1])

    p = np.arange(P)[:, None]
    f = np.arange(P)[None, :]
    put("ident", np.eye(P))
    put("causal", np.where(f > p, BIG, 0.0))
    put("edge", np.where(f < p, BIG, 0.0))
    t, c = np.arange(NT)[None, :, None], np.arange(NCB)[None, None, :]
    put("cmask", np.where(16 * c + 31 > 128 * t + p[:, :, None], BIG, 0.0))

    def many(dist):
        n = ((dist <= 128).astype(int) + ((dist % 4 == 0) & (dist <= 512)) + ((dist % 16 == 0) & (dist <= 2048)))
        n = np.where(dist >= 0, n, 0)
        return np.where(n > 0, -np.log(np.maximum(n, 1)), BIG)

    put("abias", many(p + (NT - 1) * P - np.arange(NT * P)[None, :]))
    row = np.arange(32)[:, None]
    j = row % NJ
    win = PAST - 512 + 4 * np.arange(P)[None, :] + np.arange(4)[:, None]
    strided = 16 * np.arange(STR)[None, :] + np.arange(4)[:, None]
    new = PAST + np.arange(NJ)
    pos = np.concatenate([win.ravel(), strided.ravel(), new])[None, :]
    put("asbias", many(PAST + j - pos))
    put("adiag", np.repeat((row // NJ == np.arange(8)[None, :]).astype(float), HD, axis=1))
    row = np.arange(64)[:, None]
    j = row % NJ
    put("newmask", np.where(np.arange(NJ)[None, :] > j, BIG, 0.0))
    put("winmask", np.where((4 * np.arange(P)[None, :] + np.arange(4)[:, None]).ravel()[None, :] < j, BIG, 0.0))
    put("same", ((row // 32 == row.T // 32) & (row % NJ == row.T % NJ)).astype(float))
    c, b = np.arange(NCS)[:, None], np.arange(NSL)[None, :]
    over = np.minimum(16 * c + 32, 64 * b + 64) - np.maximum(16 * c, 64 * b)
    put("overlap", np.clip(over, 0, None) / 32.0)
    put("valid", (p >= 31).astype(float))
    put("sub", p % 8)
    lg = np.log1p(-np.exp2(-5.0 - np.arange(BH)))
    h = np.arange(BH)[None, :]
    k3, q3, h3 = np.arange(P)[:, None, None], np.arange(P)[None, None, :], np.arange(BH)[None, :, None]
    put("intra", np.where(q3 >= k3, np.exp(lg[h3] * np.maximum(q3 - k3, 0)), 0.0) * SCALE)
    put("qdec", np.exp(lg[h] * (p + 1.0)))
    put("kdec", np.exp(lg[h] * (P - 1.0 - p)) * SCALE)
    k3, q3 = np.arange(NS)[:, None, None], np.arange(NS)[None, None, :]
    put("intra_s", np.where((q3 >= k3) & (q3 // NJ == k3 // NJ), np.exp(lg[h3] * np.maximum(q3 - k3, 0)), 0.0) * SCALE)
    js = np.arange(NS)[:, None] % NJ
    put("qdec_s", np.exp(lg[h] * (js + 1.0)))
    put("kdec_s", np.exp(lg[h] * (NJ - 1.0 - js)) * SCALE)
    m3, t3 = np.arange(NB // 2)[None, :, None], np.arange(NS)[None, None, :]
    put("qmask_s", (t3 // NJ == 2 * m3 + p[:, :, None] // HD).astype(float))
    put("kmask_s", (np.arange(NS)[:, None] // NJ == np.arange(NB)[None, :]).astype(float))
    freqs = (10000.0 ** (-np.arange(32) / 32.0)).astype(np.float32)
    tok = np.concatenate([np.arange(T), np.zeros(P)]).reshape(NT + 1, P)
    tok[NT, :NS] = PAST + np.arange(NS) % NJ
    ang = (tok.astype(np.float32)[:, :, None] * freqs[None, None, :]).astype(np.float64)
    trig = np.stack([np.cos(ang), np.sin(ang)], axis=2).astype(np.float32)
    return np.concatenate(parts, axis=1), cols, trig, lg


CONST, COLS, TRIG, LOG_G = _constants()


def gemm_tiles():
    return [(t, P if t < NT else NS) for t in range(NT + 1)]


def next_round(nc, sems):
    nums = sorted(s.num for s in sems)
    first = nums[0]
    for at, num in enumerate(nums):
        if at + 1 == len(nums) or nums[at + 1] != num + 1:
            nc.sync.sem_clear(range(first, num + 1))
            first = nums[at + 1] if at + 1 < len(nums) else None
    nc.all_engine_barrier()


class Phase(ExitStack):

    def __init__(self, nc):
        super().__init__()
        self.nc, self.semaphores = nc, []

    def semaphore(self, name):
        s = self.enter_context(self.nc.semaphore(name))
        self.semaphores.append(s)
        return s

    def __exit__(self, *error):
        if error[0] is None:
            next_round(self.nc, self.semaphores)
        return super().__exit__(*error)


def project(nc, ident, kind, src, w, n_cols, dst, gain=None, gates=None, residual=None):
    chunk = next(c for c in range(448, 0, -2) if n_cols % c == 0)
    n_chunks = n_cols // chunk
    with Phase(nc) as ctx:
        def sb(name, shape, dt=F32):
            return ctx.enter_context(nc.sbuf_tensor(f"{dst[0].tensor.name}_{name}", shape, dt))

        def sem(name):
            return ctx.semaphore(f"{dst[0].tensor.name}_{name}")

        y_lo, y_hi = (sb(n, [P, KD, (NT + 1) * P], F32R) for n in ("y_lo", "y_hi"))
        w_raw = sb("w_raw", [P, KD, chunk])
        w_lo, w_hi = (sb(n, [P, KD, 2, chunk], F32R) for n in ("w_lo", "w_hi"))
        res = sb("res", [P, 3, chunk])
        outb = sb("out", [P, 3, chunk])
        x = sb("x", [P, 2, D])
        z = sb("z", [P, 2, D])
        y = sb("y", [P, 2, D])
        g = sb("g", [P, D])
        stat = sb("stat", [P, 2, 4])
        tps = [ctx.enter_context(nc.psum_tensor(f"{dst[0].tensor.name}_tps{b}", [P, KD, P], F32)) for b in range(2)]
        acc = [ctx.enter_context(nc.psum_tensor(f"{dst[0].tensor.name}_acc{b}", [P, 512], F32)) for b in range(3)]
        gain_in = sem("gain_in")
        loaded = [sem(f"loaded{b}") for b in range(2)]
        squares = [sem(f"squares{b}") for b in range(2)]
        means = [sem(f"means{b}") for b in range(2)]
        roots = [sem(f"roots{b}") for b in range(2)]
        inverses = [sem(f"inverses{b}") for b in range(2)]
        rows_ready = [sem(f"rows_ready{b}") for b in range(2)]
        turned = [sem(f"turned{b}") for b in range(2)]
        yT_written = [sem(f"yT_written{b}") for b in range(2)]
        y_high = [sem(f"y_high{b}") for b in range(2)]
        w_in, w_high, w_cut = sem("w_in"), sem("w_high"), sem("w_cut")
        w_used = sem("w_used")
        pad_zero = sem("pad_zero")
        res_in = [sem(f"res_in{b}") for b in range(3)]
        product = [sem(f"product{b}") for b in range(3)]
        evacuated = [sem(f"evacuated{b}") for b in range(3)]
        stored = [sem(f"stored{b}") for b in range(3)]
        n_loads = 1 if kind == "norm" else len(gates)

        def all_tiles(e, step):
            with e.Fori(0, NT // 2) as i:
                for b in range(2):
                    step(i, b, lambda a: a[0][bass.ds((i * 2 + b) * P, P), :], P)
            step(NT // 2, 0, lambda a: a[1], NS)

        def buffer_of(w_, i):
            return w_[:, :, bass.ds(i % 2, 1), :].rearrange("p k a c -> p k (a c)")

        def load_w(e, i):
            e.dma_start(w_raw[:, :, :], w[:, bass.ds(i * chunk, chunk)].rearrange("(k p) c -> p k c", p=P)).then_inc(w_in, 16)

        with nc.Block() as block:
            @block.sync
            def _(sp):
                for b in range(3):
                    sp.sem_inc(stored[b], 16)
                if kind == "norm":
                    sp.dma_start(g[:, :], gain.partition_broadcast(P)).then_inc(gain_in, 16)

                def load(u, b, rows, n):
                    sp.wait_ge(rows_ready[b], u + 1)
                    sp.dma_start(x[0:n, b, :], rows(src)).then_inc(loaded[b], 16)
                    if kind == "gate":
                        at = 0
                        for c0, c1 in gates[1:]:
                            sp.dma_start(z[0:n, b, at:at + c1 - c0], rows(gates[0])[:, c0:c1]).then_inc(loaded[b], 16)
                            at += c1 - c0
                all_tiles(sp, load)

                def store(i, t, n):
                    k = i * 3 + t // 3
                    sp.wait_ge(evacuated[t % 3], k + 2)
                    to = dst[0][t * P:t * P + n, :] if t < NT else dst[1]
                    sp.dma_start(to[:, bass.ds(i * chunk, chunk)], outb[0:n, t % 3, :]).then_inc(stored[t % 3], 16)

                with sp.Fori(0, n_chunks - 1) as i:
                    sp.wait_ge(w_cut, i + 1)
                    load_w(sp, i + 1)
                    for t, n in gemm_tiles():
                        store(i, t, n)
                for t, n in gemm_tiles():
                    store(n_chunks - 1, t, n)
                for b in range(3):
                    sp.wait_ge(stored[b], 16 * (3 * n_chunks + 1))

            @block.scalar
            def _(act):
                def stats(u, b, rows, n):
                    if kind == "gate":
                        act.wait_ge(loaded[b], (u + 1) * (16 * (len(gates))))
                        nc.scalar.activation(z[0:n, b, :], z[0:n, b, :], ACT.Silu).then_inc(squares[b], 1)
                    else:
                        act.wait_ge(loaded[b], (u + 1) * 16)
                        nc.scalar.activation(z[0:n, b, :], x[0:n, b, :], ACT.Square,
                                             accum_out=stat[0:n, b, 0:1]).then_inc(squares[b], 1)
                        act.wait_ge(means[b], u + 1)
                        nc.scalar.activation(stat[0:n, b, 2:3], stat[0:n, b, 1:2], ACT.Sqrt).then_inc(roots[b], 1)

                def evacuate(i, b, n, col):
                    act.wait_ge(turned[b], i + 2)
                    nc.scalar.copy(y_hi[:, :, col], tps[b][:, :, 0:n]).then_inc(y_high[b], 1)

                def w_high_part(i):
                    act.wait_ge(w_in, (i + 1) * 16)
                    act.wait_ge(w_used, i + 1)
                    nc.scalar.copy(buffer_of(w_hi, i), w_raw[:, :, :]).then_inc(w_high, 1)

                def load_residual(i, t, n):
                    act.wait_ge(evacuated[t % 3], i * 3 + t // 3 + 1)
                    fr = residual[0][t * P:t * P + n, :] if t < NT else residual[1]
                    act.dma_start(res[0:n, t % 3, :], fr[:, bass.ds(i * chunk, chunk)]).then_inc(res_in[t % 3], 16)
                act.wait_ge(loaded[0], 16 * n_loads)
                load_w(act, 0)
                for b in range(2):
                    act.sem_inc(yT_written[b], 1)
                act.sem_inc(w_used, 1)
                with act.Fori(0, NT // 2) as i:
                    for b in range(2):
                        stats(i, b, None, P)
                    for b in range(2):
                        evacuate(i, b, P, bass.ds((i * 2 + b) * P, P))
                stats(NT // 2, 0, None, NS)
                w_high_part(0)
                evacuate(NT // 2, 0, NS, slice(T, T + NS))
                with act.Fori(0, n_chunks - 1) as i:
                    for t, n in gemm_tiles():
                        if residual is not None:
                            load_residual(i, t, n)
                        if t == CUT_AFTER:
                            w_high_part(i + 1)
                if residual is not None:
                    for t, n in gemm_tiles():
                        load_residual(n_chunks - 1, t, n)

            @block.vector
            def _(dve):
                if kind == "norm":
                    dve.wait_ge(gain_in, 16)

                def rows_of(u, b, rows, n):
                    if kind == "gate":
                        dve.wait_ge(squares[b], u + 1)
                        dve.wait_ge(loaded[b], (u + 1) * (16 * (len(gates))))
                        dve.wait_ge(turned[b], u + 1)
                        nc.vector.tensor_tensor(y[0:n, b, :], x[0:n, b, :], z[0:n, b, :], ALU.mult).then_inc(rows_ready[b], 1)
                        return
                    dve.wait_ge(squares[b], u + 1)
                    nc.vector.tensor_scalar(stat[0:n, b, 1:2], stat[0:n, b, 0:1], 1.0 / D, EPS_RMS, ALU.mult, ALU.add).then_inc(means[b], 1)
                    dve.wait_ge(roots[b], u + 1)
                    nc.vector.reciprocal(stat[0:n, b, 3:4], stat[0:n, b, 2:3]).then_inc(inverses[b], 1)
                    dve.wait_ge(inverses[b], u + 1)
                    dve.wait_ge(turned[b], u + 1)
                    nc.vector.scalar_tensor_tensor(out=y[0:n, b, :], in0=x[0:n, b, :], scalar=stat[0:n, b, 3:4],
                                                   in1=g[0:n, :], op0=ALU.mult, op1=ALU.mult).then_inc(rows_ready[b], 1)
                for b in range(2):
                    dve.sem_inc(rows_ready[b], 1)
                for b in range(3):
                    dve.sem_inc(evacuated[b], 1)
                nc.vector.memset(y[:, 0, 0:KD * (P - NS)], 0.0).then_inc(pad_zero, 1)
                dve.wait_ge(pad_zero, 1)
                zeros = y[:, 0, 0:KD * (P - NS)].rearrange("p (k c) -> p k c", k=KD)
                nc.vector.tensor_copy(y_hi[:, :, ROWS:], zeros)
                nc.vector.tensor_copy(y_lo[:, :, ROWS:], zeros).then_inc(pad_zero, 1)
                dve.wait_ge(pad_zero, 2)

                def y_low_part(i, b, n, col):
                    dve.wait_ge(y_high[b], i + 1)
                    nc.vector.tensor_tensor(y_lo[:, :, col], tps[b][:, :, 0:n], y_hi[:, :, col].bitcast(F32),
                                            ALU.subtract).then_inc(yT_written[b], 1)

                def w_low_part(i):
                    dve.wait_ge(w_high, i + 1)
                    nc.vector.tensor_tensor(buffer_of(w_lo, i), w_raw[:, :, :], buffer_of(w_hi, i).bitcast(F32),
                                            ALU.subtract).then_inc(w_cut, 1)

                def take_product(i, t, n):
                    k = i * 3 + t // 3
                    dve.wait_ge(product[t % 3], k + 1)
                    dve.wait_ge(stored[t % 3], (k + 1) * 16)
                    if residual is None:
                        nc.vector.tensor_copy(outb[0:n, t % 3, :], acc[t % 3][0:n, 0:chunk]).then_inc(evacuated[t % 3], 1)
                    else:
                        dve.wait_ge(res_in[t % 3], (k + 1) * 16)
                        nc.vector.tensor_tensor(outb[0:n, t % 3, :], acc[t % 3][0:n, 0:chunk], res[0:n, t % 3, :],
                                                ALU.add).then_inc(evacuated[t % 3], 1)
                with dve.Fori(0, NT // 2) as i:
                    for b in range(2):
                        rows_of(i, b, None, P)
                    for b in range(2):
                        y_low_part(i, b, P, bass.ds((i * 2 + b) * P, P))
                rows_of(NT // 2, 0, None, NS)
                w_low_part(0)
                y_low_part(NT // 2, 0, NS, slice(T, T + NS))
                with dve.Fori(0, n_chunks - 1) as i:
                    for t, n in gemm_tiles():
                        take_product(i, t, n)
                        if t == CUT_AFTER:
                            w_low_part(i + 1)
                for t, n in gemm_tiles():
                    take_product(n_chunks - 1, t, n)

            @block.tensor
            def _(pe):
                for b in range(2):
                    pe.sem_inc(turned[b], 1)

                def turn(u, b, rows, n):
                    pe.wait_ge(rows_ready[b], u + 2)
                    pe.wait_ge(yT_written[b], u + 1)
                    for k in range(KD):
                        last = nc.tensor.transpose(tps[b][:, k, 0:n], y[0:n, b, k * P:(k + 1) * P], ident[0:n, 0:n])
                    last.then_inc(turned[b], 1)
                all_tiles(pe, turn)
                pe.wait_ge(yT_written[0], NT // 2 + 2)
                pe.wait_ge(yT_written[1], NT // 2 + 1)
                pe.wait_ge(pad_zero, 2)
                with pe.Fori(0, n_chunks) as i:
                    pe.wait_ge(w_cut, i + 1)
                    for t, n in gemm_tiles():
                        pe.wait_ge(evacuated[t % 3], i * 3 + t // 3 + 1)
                        for k in range(KD):
                            for x, (rows, cols) in enumerate(((y_lo, w_hi), (y_hi, w_lo), (y_hi, w_hi))):
                                last = nc.tensor.matmul(acc[t % 3][:, 0:chunk], rows[:, k, t * P:(t + 1) * P],
                                                        cols[:, k, bass.ds(i % 2, 1), :].rearrange("p a c -> p (a c)"),
                                                        start=(k == 0 and x == 0), stop=(k == KD - 1 and x == 2))
                                if t == 1 and k == 0 and x == 0:
                                    last.then_inc(w_used, 1)
                        last.then_inc(product[t % 3], 1)


def final_norm(nc, src, gain, dst):
    with Phase(nc) as ctx:
        x = ctx.enter_context(nc.sbuf_tensor("fn_x", [P, NT + 1, D], F32))
        sq = ctx.enter_context(nc.sbuf_tensor("fn_sq", [P, D], F32))
        g = ctx.enter_context(nc.sbuf_tensor("fn_g", [P, D], F32))
        stat = ctx.enter_context(nc.sbuf_tensor("fn_stat", [P, 4, NT + 1], F32))
        loaded = [ctx.semaphore(f"fn_loaded{t}") for t in range(NT + 1)]
        gain_in = ctx.semaphore("fn_gain_in")
        squares = ctx.semaphore("fn_squares")
        means = ctx.semaphore("fn_means")
        roots = ctx.semaphore("fn_roots")
        inverses = ctx.semaphore("fn_inverses")
        normed = ctx.semaphore("fn_normed")
        stored = ctx.semaphore("fn_stored")
        cleared = ctx.semaphore("fn_cleared")
        with nc.Block() as block:
            @block.sync
            def _(sp):
                sp.dma_start(g[:, :], gain.partition_broadcast(P)).then_inc(gain_in, 16)
                for t, n in gemm_tiles():
                    fr = src[0][t * P:t * P + n, :] if t < NT else src[1]
                    sp.dma_start(x[0:n, t, :], fr).then_inc(loaded[t], 16)
                for t, n in gemm_tiles():
                    sp.wait_ge(normed, t + 1)
                    to = dst[0][t * P:t * P + n, :] if t < NT else dst[1]
                    sp.dma_start(to, x[0:n, t, :]).then_inc(stored, 16)
                sp.wait_ge(stored, 16 * (NT + 1))

            @block.scalar
            def _(act):
                act.wait_ge(cleared, 1)
                for t, n in gemm_tiles():
                    act.wait_ge(loaded[t], 16)
                    if t:
                        act.wait_ge(squares, t)
                    nc.scalar.activation(sq[0:n, :], x[0:n, t, :], ACT.Square, accum_out=stat[0:n, 0, t:t + 1]).then_inc(squares, 1)
                act.wait_ge(means, 1)
                nc.scalar.activation(stat[:, 2, :], stat[:, 1, :], ACT.Sqrt).then_inc(roots, 1)

            @block.vector
            def _(dve):
                nc.vector.memset(stat[:, 0, :], 1.0).then_inc(cleared, 1)
                dve.wait_ge(squares, NT + 1)
                nc.vector.tensor_scalar(stat[:, 1, :], stat[:, 0, :], 1.0 / D, EPS_RMS, ALU.mult, ALU.add).then_inc(means, 1)
                dve.wait_ge(roots, 1)
                nc.vector.reciprocal(stat[:, 3, :], stat[:, 2, :]).then_inc(inverses, 1)
                dve.wait_ge(inverses, 1)
                dve.wait_ge(gain_in, 16)
                for t, n in gemm_tiles():
                    nc.vector.scalar_tensor_tensor(out=x[0:n, t, :], in0=x[0:n, t, :], scalar=stat[0:n, 3, t:t + 1],
                                                   in1=g[0:n, :], op0=ALU.mult, op1=ALU.mult).then_inc(normed, 1)


def attend_prompt(nc, con, kind, h, mix, n_pairs, kcmp=None, vcmp=None):
    sparse = kind == "sparse"
    NBR = 3 if sparse else 1
    n_rounds = n_pairs // 2
    with Phase(nc) as ctx:
        def sb(name, shape, dt=F32):
            return ctx.enter_context(nc.sbuf_tensor(f"{kind}_{name}", shape, dt))

        def sem(name):
            s = ctx.semaphore(f"{kind}_{name}")
            sems.append(s)
            return s
        sems = []
        q_in = sb("q_in", [P, NT, 2, 2, HD])
        k_in = sb("k_in", [P, NT, 2, 2, HD])
        q_ac = [sb(f"q_ac{b}", [P, 2, 2, T], BF16) for b in range(2)]
        k_abc = [sb(f"k_abc{b}", [P, 2, 3, T], BF16) for b in range(1 if sparse else 2)]
        rest = [sb(f"rest{b}", [P, 512]) for b in range(2)]
        v_sb = [sb(f"v{b}", [P, 2, NT, HD]) if sparse else sb(f"v{b}", [P, NT, P]) for b in range(1 if sparse else 2)]
        pr = [sb(f"pr{b}", [P, T]) for b in range(2)]
        prT = [sb(f"prT{b}", [P, 4 * P]) for b in range(4)]
        o_sb = [sb(f"o{b}", [P, NT, 2, HD]) for b in range(2)]
        nmax = sb("nmax", [P, 2, 2])
        lsum = sb("lsum", [P, 4, 2 * NBR])
        coef = sb("coef", [P, 2, 2 * NBR])
        part = sb("part", [P, 2 * NBR, HD])
        if sparse:
            k_all = sb("k_all", [P, 2, 2, 3, T], BF16)
            v_all = sb("v_all", [P, 2, NT, 2, HD])
            gl_in = sb("gl_in", [P, NT, 6])
            gate_e = sb("gate_e", [P, NT, 6])
            gate_den = [sb(f"gate_den{b}", [P, NT, 6]) for b in range(2)]
            kc_in = sb("kc_in", [P, 2, NCB])
            kc_rest = sb("kc_rest", [P, 2, NCB])
            kc_all = sb("kc_all", [P, 2, 3, NCB], BF16)
            kc = sb("kc", [P, 3, NCB], BF16)
            vc_all = sb("vc_all", [NCB, 2, HD])
            vc = sb("vc", [NCB, HD])
        ps_s = [ctx.enter_context(nc.psum_tensor(f"{kind}_ps_s{b}", [P, T], F32)) for b in range(2)]
        ps_t = [ctx.enter_context(nc.psum_tensor(f"{kind}_ps_t{b}", [P, 4 * P], F32)) for b in range(2)]
        ps_o = [ctx.enter_context(nc.psum_tensor(f"{kind}_ps_o{b}", [P, 512], F32)) for b in range(2)]
        loaded = [sem("loaded_first"), sem("loaded_second")]
        k_loaded = [sem("k_loaded_sel"), sem("k_loaded_win")]
        copied_act, copied_dve, copied_pool = sem("copied_act"), sem("copied_dve"), sem("copied_pool")
        cut_first, cut_rest, cut_second, cut_done = sem("cut_first"), sem("cut_rest"), sem("cut_second"), sem("cut_done")
        gate_exp, gate_ready = sem("gate_exp"), sem("gate_ready")
        scores_ready, max_ready, probs_ready = sem("scores_ready"), sem("max_ready"), sem("probs_ready")
        turned = sem("turned")
        bank_free = [sem("bank_free0"), sem("bank_free1")]
        group_used, out_ready, stored, dve_step = sem("group_used"), sem("out_ready"), sem("stored"), sem("dve_step")
        kc_step, vc_loaded = sem("kc_step"), sem("vc_loaded")
        hp = h[0].rearrange("(t p) c -> p t c", p=P)

        def load_pair(sp, i, b, s):
            q0 = QC if sparse else QA
            todo = []
            for e in range(2):
                for dup in range(2):
                    todo.append((q_in[:, :, e, dup, :], hp[:, :, bass.ds(i * P + (q0 + e * HD), HD)]))
                    if not sparse:
                        todo.append((k_in[:, :, e, dup, :], hp[:, :, bass.ds(i * P + (KA + e * HD), HD)]))
            if sparse:
                todo.append((gl_in[:, :, :], hp[:, :, bass.ds(i * 6 + GL, 6)]))
            else:
                todo.append((v_sb[b][:, :, :], hp[:, :, bass.ds(i * P + VA, P)]))
            for out, in_ in todo:
                sp.dma_start(out, in_).then_inc(s, 16)
            return len(todo)

        N_LOADS = 5 if sparse else 9

        jobs = []
        for b in range(2):
            for t in range(NT):
                for e in range(2):
                    if sparse:
                        jobs.append((b, t, e, 1, list(range(t + 1))))
                        jobs.append((b, t, e, 2, list(range(max(0, t - 4), t + 1))))
                    else:
                        jobs.append((b, t, e, 0, list(range(t + 1))))
                if sparse:
                    jobs.append((b, t, None, 0, None))
        width = [2 * 64 if blocks is None else P * len(blocks) for *_, blocks in jobs]
        groups = []
        of_job = []
        for n, w in enumerate(width):
            of_job.append([])
            for c0 in range(0, w, 4 * P):
                of_job[n].append(len(groups))
                groups.append((n, c0, min(4 * P, w - c0)))
        last_group = {(j[0] * NT + j[1]): of_job[n][-1] for n, j in enumerate(jobs)}
        last_of_pair = [max(g for t, g in last_group.items() if t < NT), len(groups) - 1]

        by_act, busy_act, busy_dve = [], 0.0, 0.0
        for n, w in enumerate(width):
            busy_act += (2 if jobs[n][4] is None else 1) * 250 + w * 1.04
            busy_dve += 150 + w * 1.04 + (900 / (5 if sparse else 2))
            for g in of_job[n]:
                by_act.append(busy_act < busy_dve)
                if by_act[-1]:
                    busy_act += 200 + groups[g][2] * 0.9
                else:
                    busy_dve += 120 + groups[g][2] * 1.04

        units = [("q", e, x) for e in range(2) for x in range(2)]
        if not sparse:
            units += [("k", e, x) for e in range(2) for x in range(2)]

        steps = [("scores", 0), ("max", 0), ("exp", 0), ("scores", 1), ("max", 1)]
        per_pair = len(jobs) // 2
        start = per_pair // 4
        every = (per_pair - start - 2) // len(units)
        for n in range(len(jobs)):
            if n + 1 < len(jobs):
                steps.append(("exp", n + 1))
            for g in of_job[n]:
                steps += [("turn", g), ("take", g)]
            if n + 2 < len(jobs):
                steps += [("scores", n + 2), ("max", n + 2)]
            if n:
                steps += [("times_v", g) for g in of_job[n - 1]]
            if n >= 2 and jobs[n - 2][:2] != jobs[n - 1][:2]:
                steps.append(("finish", jobs[n - 2][0] * NT + jobs[n - 2][1]))
            k = n % per_pair
            if k >= start and (k - start) % every == 0 and (k - start) // every < len(units):
                steps.append(("cut", (n // per_pair, (k - start) // every)))
        steps += [("times_v", g) for g in of_job[-1]] + [("finish", 2 * NT - 1)]
        place, order = {}, 0
        for what, x in steps:
            if what in ("turn", "cut"):
                place[what, x] = order
                order += 1

        def bank(what, x):
            return place[what, x] % 2, place[what, x] // 2

        def parts_of(unit, b):
            what, e, x = unit
            cols = slice(x * 512, x * 512 + 512)
            if what == "q":
                return q_ac[b][:, e, 0, cols], None, q_ac[b][:, e, 1, cols]
            k = k_abc[b] if not sparse else k_all[:, b]
            return k[:, e, 0, cols], k[:, e, 1, cols], k[:, e, 2, cols]

        def cut_act(act, unit, b, src, n_turned, c):
            act.wait_ge(turned, n_turned)
            nc.scalar.activation(parts_of(unit, b)[0], src, ACT.Copy, scale=-SCALE if unit[0] == "q" else 1.0).then_inc(cut_first, 1)

        def cut_dve(dve, unit, b, src, c, free):
            dve.wait_ge(cut_first, c + 1)
            if c >= 2:
                dve.wait_ge(cut_done, c - 1)
            nc.vector.scalar_tensor_tensor(out=rest[c % 2][:, :], in0=src, scalar=-SCALE if unit[0] == "q" else 1.0,
                                           in1=parts_of(unit, b)[0], op0=ALU.mult, op1=ALU.subtract).then_inc(free, 1)

        def cut_pool(pool, unit, b, c, free, n_free):
            pool.wait_ge(free, n_free)
            first, second, third = parts_of(unit, b)
            lo, hi = slice(0, HD), slice(HD, P)
            if unit[0] == "q":
                nc.gpsimd.tensor_copy(third[lo], first[lo]).then_inc(cut_second, 1)
                pool.wait_ge(cut_second, 2 * c + 1)
                nc.gpsimd.tensor_copy(first[hi], rest[c % 2][hi, :]).then_inc(cut_second, 1)
                pool.wait_ge(cut_second, 2 * c + 2)
                nc.gpsimd.tensor_tensor(third[hi], rest[c % 2][hi, :], first[hi], ALU.subtract).then_inc(cut_done, 1)
            else:
                nc.gpsimd.tensor_copy(third[hi], first[hi]).then_inc(cut_second, 1)
                pool.wait_ge(cut_second, 2 * c + 1)
                nc.gpsimd.tensor_copy(second, rest[c % 2][:, :]).then_inc(cut_second, 1)
                pool.wait_ge(cut_second, 2 * c + 2)
                nc.gpsimd.tensor_tensor(third[lo], rest[c % 2][lo, :], second[lo], ALU.subtract).then_inc(cut_done, 1)
            pool.wait_ge(cut_done, c + 1)

        def cut_pe(pe, unit, to, src=None):
            what, e, x = unit
            src = (q_in if what == "q" else k_in) if src is None else src
            for m in range(4):
                last = nc.tensor.transpose(to[:, m * P:(m + 1) * P], src[:, 4 * x + m, e, :, :].rearrange("p a d -> p (a d)"),
                                           con("ident"))
            last.then_inc(turned, 1)

        first_cuts = [(u, 0) for u in units]
        if sparse:
            first_cuts += [(("k", m, x), g) for m in range(2) for g in range(2) for x in range(2)]
        with nc.Block() as block:
            @block.sync
            def _(sp):
                n = load_pair(sp, 0, 0, loaded[0])
                if sparse:
                    for half in range(2):
                        for g in range(2):
                            sp.dma_start(kc_in[half * HD:(half + 1) * HD, g, :], kcmp[g * HD:(g + 1) * HD, :]).then_inc(vc_loaded, 16)
                    sp.dma_start(vc_all[:, :, :].rearrange("c g d -> c (g d)"), vcmp).then_inc(vc_loaded, 16)
                    for m, (kcol, vcol) in enumerate(((KS, VS), (KW, VW))):
                        if m == 1:
                            sp.wait_ge(turned, len(units) + 4)
                        for g in range(2):
                            for dup in range(2):
                                sp.dma_start(k_in[:, :, g, dup, :], hp[:, :, kcol + g * HD:kcol + (g + 1) * HD]).then_inc(k_loaded[m], 16)
                        sp.dma_start(v_all[:, m, :, :, :].rearrange("p t g d -> p t (g d)"), hp[:, :, vcol:vcol + P]).then_inc(k_loaded[m], 16)
                    sp.wait_ge(k_loaded[0], 80)
                    sp.wait_ge(k_loaded[1], 80)
                    sp.wait_ge(vc_loaded, 80)
                sp.wait_ge(loaded[0], 16 * n)

            @block.tensor
            def _(pe):
                pe.wait_ge(loaded[0], 16 * N_LOADS)
                for c, (unit, b) in enumerate(first_cuts):
                    if c >= 2:
                        pe.wait_ge(bank_free[c % 2], c // 2)
                    if c >= len(units):
                        pe.wait_ge(k_loaded[unit[1]], 80)
                        what, m, x = unit
                        cut_pe(pe, (what, b, x), ps_t[c % 2])
                    else:
                        cut_pe(pe, unit, ps_t[c % 2])

            @block.scalar
            def _(act):
                if sparse:
                    act.wait_ge(loaded[0], 16 * N_LOADS)
                    nc.scalar.activation(gate_e[:, :, :], gl_in[:, :, :], ACT.Exp, scale=-1.0).then_inc(gate_exp, 1)
                    act.wait_ge(vc_loaded, 80)
                    nc.scalar.copy(kc_all[:, :, 0, :], kc_in[:, :, :]).then_inc(kc_step, 1)
                for c, (unit, b) in enumerate(first_cuts):
                    cut_act(act, unit, b, ps_t[c % 2][:, :], c + 1, c)

            @block.vector
            def _(dve):
                if sparse:
                    dve.wait_ge(gate_exp, 1)
                    nc.vector.tensor_scalar(gate_den[0][:, :, :], gate_e[:, :, :], 1.0, None, ALU.add).then_inc(gate_ready, 1)
                    dve.wait_ge(gate_ready, 1)
                    dve.wait_ge(kc_step, 1)
                    nc.vector.tensor_tensor(kc_rest[:, :, :], kc_in[:, :, :], kc_all[:, :, 0, :], ALU.subtract).then_inc(kc_step, 1)
                    dve.wait_ge(kc_step, 2)
                    nc.vector.tensor_copy(kc_all[HD:P, :, 2, :], kc_all[HD:P, :, 0, :])
                    nc.vector.tensor_copy(kc_all[:, :, 1, :], kc_rest[:, :, :]).then_inc(kc_step, 1)
                    dve.wait_ge(kc_step, 3)
                    nc.vector.tensor_tensor(kc_all[0:HD, :, 2, :], kc_rest[0:HD, :, :], kc_all[0:HD, :, 1, :], ALU.subtract).then_inc(kc_step, 1)
                    dve.wait_ge(kc_step, 4)
                for c, (unit, b) in enumerate(first_cuts):
                    cut_dve(dve, unit, b, ps_t[c % 2][:, :], c, bank_free[c % 2])

            @block.gpsimd
            def _(pool):
                for c, (unit, b) in enumerate(first_cuts):
                    cut_pool(pool, unit, b, c, bank_free[c % 2], c // 2 + 1)
                pool.wait_ge(cut_done, len(first_cuts))
        next_round(nc, sems)

        with nc.Fori(0, n_rounds) as i:
            with nc.Block() as block:
                group_of_round = i // 2 if sparse else 0

                @block.sync
                def _(sp):
                    load_pair(sp, i * 2 + 1, 1, loaded[0])
                    for tt in range(2 * NT):
                        if tt == NT:
                            sp.wait_ge(turned, place["cut", (0, len(units) - 1)] + 1)
                            sp.wait_ge(group_used, last_of_pair[0] + 1)
                            if sparse:
                                sp.wait_ge(gate_exp, 1)
                            load_pair(sp, (i * 2 + 2) % n_pairs, 0, loaded[1])
                        sp.wait_ge(out_ready, tt + 1)
                        b, t = divmod(tt, NT)
                        sp.dma_start(mix[t * P:(t + 1) * P, bass.ds((i * 2 + b) * P, P)],
                                     o_sb[b][:, t, :, :].rearrange("p e d -> p (e d)")).then_inc(stored, 16)
                    sp.wait_ge(loaded[0], 16 * N_LOADS)
                    sp.wait_ge(loaded[1], 16 * N_LOADS)
                    sp.wait_ge(stored, 16 * 2 * NT)

                def cut_of(x):
                    b, u = x
                    return units[u], 1 - b, b * len(units) + u

                @block.gpsimd
                def _(pool):
                    if sparse:
                        nc.gpsimd.tensor_copy(kc[:, :, :], kc_all[:, bass.ds(group_of_round, 1), :, :].rearrange("p g x c -> p (g x) c"))
                        nc.gpsimd.tensor_copy(vc[:, :], vc_all[:, bass.ds(group_of_round, 1), :].rearrange("p g d -> p (g d)")).then_inc(copied_pool, 1)
                    for what, x in steps:
                        if what == "cut":
                            unit, b, c = cut_of(x)
                            nb, nu = bank(what, x)
                            cut_pool(pool, unit, b, c, bank_free[nb], nu + 1)
                    pool.wait_ge(cut_done, 2 * len(units))

                def take(eng, copy, g):
                    n, _, w = groups[g]
                    nb, nu = bank("turn", g)
                    eng.wait_ge(turned, place["turn", g] + 1)
                    if g >= 4:
                        eng.wait_ge(group_used, g - 3)
                    rows = NCB if jobs[n][4] is None else P
                    w = 2 * P if jobs[n][4] is None else w
                    copy(prT[g % 4][0:rows, 0:w], ps_t[nb][0:rows, 0:w]).then_inc(bank_free[nb], 1)

                @block.scalar
                def _(act):
                    if sparse:
                        nc.scalar.copy(v_sb[0][:, 0, :, :], v_all[:, 0, :, bass.ds(group_of_round, 1), :].rearrange("p t g d -> p t (g d)"))
                        nc.scalar.copy(v_sb[0][:, 1, :, :], v_all[:, 1, :, bass.ds(group_of_round, 1), :].rearrange("p t g d -> p t (g d)")).then_inc(copied_act, 1)
                    for what, x in steps:
                        if what == "exp":
                            n = x
                            b, t, e, br, blocks = jobs[n]
                            tt = b * NT + t
                            act.wait_ge(max_ready, n + 1)
                            if n >= 2:
                                act.wait_ge(turned, place["turn", of_job[n - 2][-1]] + 1)
                            if tt >= 4:
                                act.wait_ge(out_ready, tt - 3)
                            if blocks is None:
                                for e in range(2):
                                    last = nc.scalar.activation(pr[n % 2][:, e * 64:e * 64 + NCB], ps_s[n % 2][:, e * 64:e * 64 + NCB], ACT.Exp,
                                                                scale=-1.0, bias=nmax[:, n % 2, e:e + 1],
                                                                accum_out=lsum[:, tt % 4, e * 3:e * 3 + 1])
                                last.then_inc(probs_ready, 1)
                            else:
                                src = ps_s[n % 2] if sparse else pr[n % 2]
                                nc.scalar.activation(pr[n % 2][:, 0:width[n]], src[:, 0:width[n]], ACT.Exp, scale=-1.0,
                                                     bias=nmax[:, n % 2, 0:1],
                                                     accum_out=lsum[:, tt % 4, e * NBR + br:e * NBR + br + 1]).then_inc(probs_ready, 1)
                        elif what == "take" and by_act[x]:
                            take(act, nc.scalar.copy, x)
                        elif what == "cut":
                            unit, b, c = cut_of(x)
                            cut_act(act, unit, b, ps_t[bank(what, x)[0]][:, :], place[what, x] + 1, c)
                            if sparse and x[1] == 0:
                                act.wait_ge(loaded[x[0]], 16 * N_LOADS)
                                if x[0] == 1:
                                    act.wait_ge(gate_ready, 1)
                                nc.scalar.activation(gate_e[:, :, :], gl_in[:, :, :], ACT.Exp, scale=-1.0).then_inc(gate_exp, 1)

                @block.vector
                def _(dve):
                    count = 0

                    def link(ins):
                        nonlocal count
                        count += 1
                        ins.then_inc(dve_step, 1)
                        dve.wait_ge(dve_step, count)

                    def maximum(n):
                        b, t, e, br, blocks = jobs[n]
                        dve.wait_ge(scores_ready, n + 1)
                        if n >= 2:
                            dve.wait_ge(probs_ready, n - 1)
                        s = ps_s[n % 2]
                        if blocks is None:
                            nc.vector.tensor_reduce(nmax[:, n % 2, :], s[:, 0:128].rearrange("p (e c) -> p e c", e=2)[:, :, 0:NCB], AX,
                                                    ALU.min).then_inc(max_ready, 1)
                        elif sparse:
                            nc.vector.tensor_reduce(nmax[:, n % 2, 0:1], s[:, 0:width[n]], AX, ALU.min).then_inc(max_ready, 1)
                        else:
                            if n >= 2:
                                dve.wait_ge(turned, place["turn", of_job[n - 2][-1]] + 1)
                            nc.vector.tensor_tensor_reduce(
                                out=pr[n % 2][:, 0:width[n]], in0=s[:, 0:width[n]],
                                in1=con("abias")[:, (NT - 1 - t) * P:], scale=1.0, scalar=3e38, op0=ALU.add, op1=ALU.min,
                                accum_out=nmax[:, n % 2, 0:1]).then_inc(max_ready, 1)

                    def finish(tt):
                        b, t = divmod(tt, NT)
                        dve.wait_ge(group_used, last_group[tt] + 1)
                        l, c = lsum[:, tt % 4, :], coef[:, tt % 2, :]
                        o = ps_o[tt % 2][:, 0:2 * NBR * HD].rearrange("p (s d) -> p s d", d=HD)
                        if sparse:
                            link(nc.vector.tensor_tensor(c, l, gate_den[b][:, t, :], ALU.mult))
                            link(nc.vector.reciprocal(c, c))
                            if t == 0:
                                cc = c.rearrange("p (e b) -> p e b", b=3)[:, :, 0]
                                link(nc.vector.tensor_scalar(cc, cc, con("valid"), None, ALU.mult))
                            link(nc.vector.tensor_tensor(part[:, :, :], o, c.unsqueeze(2).broadcast_to([P, 6, HD]), ALU.mult))
                            nc.vector.tensor_reduce(o_sb[b][:, t, :, :], part[:, :, :].rearrange("p (e b) d -> p e d b", b=3),
                                                    AX, ALU.add).then_inc(out_ready, 1)
                            dve.wait_ge(out_ready, tt + 1)
                        else:
                            link(nc.vector.reciprocal(c, l))
                            nc.vector.tensor_tensor(o_sb[b][:, t, :, :], o, c.unsqueeze(2).broadcast_to([P, 2, HD]),
                                                    ALU.mult).then_inc(out_ready, 1)
                    if sparse:
                        nc.vector.tensor_copy(k_abc[0][:, :, :, :], k_all[:, bass.ds(group_of_round, 1), :, :, :].rearrange(
                            "p g m x t -> p (g m) x t")).then_inc(copied_dve, 1)
                    for what, x in steps:
                        if what == "max":
                            maximum(x)
                        elif what == "take" and not by_act[x]:
                            take(dve, nc.vector.tensor_copy, x)
                        elif what == "finish":
                            finish(x)
                        elif what == "cut":
                            unit, b, c = cut_of(x)
                            if sparse and x[1] == 0 and x[0] == 1:
                                pass
                            cut_dve(dve, unit, b, ps_t[bank(what, x)[0]][:, :], c, bank_free[bank(what, x)[0]])
                            if sparse and x[1] == len(units) - 1:
                                dve.wait_ge(gate_exp, x[0] + 1)
                                nc.vector.tensor_scalar(gate_den[1 - x[0]][:, :, :], gate_e[:, :, :], 1.0, None, ALU.add).then_inc(gate_ready, 1)
                                dve.wait_ge(gate_ready, x[0] + 1)

                @block.tensor
                def _(pe):
                    if sparse:
                        pe.wait_ge(copied_dve, 1)
                        pe.wait_ge(copied_pool, 1)
                        pe.wait_ge(copied_act, 1)

                    def products(out, b, e, t, k3, first, last_):
                        for x in range(3):
                            q = q_ac[b][:, e, 1 if x == 2 else 0, t * P:(t + 1) * P]
                            ins = nc.tensor.matmul(out, q, k3(x), start=first and x == 0, stop=last_ and x == 2)
                        return ins

                    def scores(n):
                        b, t, e, br, blocks = jobs[n]
                        if n >= 2:
                            pe.wait_ge(probs_ready if sparse else max_ready, n - 1)
                        if n == per_pair or (n == per_pair + 1 and False):
                            pe.wait_ge(cut_done, len(units))
                            pe.wait_ge(loaded[0], 16 * N_LOADS)
                        s = ps_s[n % 2]
                        if blocks is None:
                            for e in range(2):
                                out = s[:, e * 64:e * 64 + NCB]
                                products(out, b, e, t, lambda x: kc[:, x, :], True, False)
                                last = nc.tensor.matmul(out, con.ident16, con.cmask16[:, t, :], start=False, stop=True)
                            last.then_inc(scores_ready, 1)
                            return
                        kb, ki = (k_abc[0], br - 1) if sparse else (k_abc[b], e)
                        for c0 in range(0, width[n], 512):
                            c1 = min(c0 + 512, width[n])
                            at = blocks[0] * P
                            masks = []
                            if sparse:
                                if width[n] - P >= c0 and width[n] <= c1:
                                    masks.append((width[n] - P, con.causal16))
                                if br == 2 and t >= 4 and c0 == 0:
                                    masks.append((0, con.edge16))
                            last = products(s[:, c0:c1], b, e, t, lambda x: kb[:, ki, x, at + c0:at + c1], True, not masks)
                            for x, (m0, mask) in enumerate(masks):
                                last = nc.tensor.matmul(s[:, m0:m0 + P], con.ident16, mask, start=False, stop=x == len(masks) - 1)
                        last.then_inc(scores_ready, 1)

                    def turn(g):
                        n, c0, w = groups[g]
                        if g == of_job[n][0]:
                            pe.wait_ge(probs_ready, n + 1)
                        to = enter("turn", g)
                        if jobs[n][4] is None:
                            for e in range(2):
                                last = nc.tensor.transpose(to[0:NCB, e * P:(e + 1) * P], pr[n % 2][:, e * 64:e * 64 + NCB], con("ident"))
                        else:
                            for c in range(0, w, P):
                                last = nc.tensor.transpose(to[:, c:c + P], pr[n % 2][:, c0 + c:c0 + c + P], con("ident"))
                        last.then_inc(turned, 1)

                    def enter(what, x):
                        nb, nu = bank(what, x)
                        if nu:
                            pe.wait_ge(bank_free[nb], nu)
                        return ps_t[nb]

                    def times_v(g):
                        n, c0, w = groups[g]
                        b, t, e, br, blocks = jobs[n]
                        tt = b * NT + t
                        nb, nu = bank("turn", g)
                        pe.wait_ge(bank_free[nb], nu + 1)
                        if tt >= 2 and (n == 0 or jobs[n - 1][:2] != jobs[n][:2]) and g == of_job[n][0]:
                            pe.wait_ge(out_ready, tt - 1)
                        if blocks is None:
                            for e in range(2):
                                last = nc.tensor.matmul(ps_o[tt % 2][:, e * 3 * HD:(e * 3 + 1) * HD], prT[g % 4][0:NCB, e * P:(e + 1) * P],
                                                        vc[:, :], start=True, stop=True)
                            last.then_inc(group_used, 1)
                            return
                        slot = (e * NBR + br) * HD
                        for c in range(0, w, P):
                            kb = blocks[(c0 + c) // P]
                            rhs = v_sb[0][:, br - 1, kb, :] if sparse else v_sb[b][:, kb, e * HD:(e + 1) * HD]
                            last = nc.tensor.matmul(ps_o[tt % 2][:, slot:slot + HD], prT[g % 4][:, c:c + P], rhs,
                                                    start=c0 + c == 0, stop=c0 + c + P >= width[n])
                        last.then_inc(group_used, 1)
                    for what, x in steps:
                        if what == "scores":
                            scores(x)
                        elif what == "turn":
                            turn(x)
                        elif what == "times_v":
                            times_v(x)
                        elif what == "cut":
                            pe.wait_ge(loaded[x[0]], 16 * N_LOADS)
                            cut_pe(pe, units[x[1]], enter(what, x))
            next_round(nc, sems)


def retain(nc, con, h, mix, trig, state_out, state_in=None):
    sample = state_in is not None
    name = "ret_s" if sample else "ret"
    R = NS if sample else P
    n_rounds = 1 if sample else NT
    with Phase(nc) as ctx:
        def sb(nm, shape, dt=F32):
            return ctx.enter_context(nc.sbuf_tensor(f"{name}_{nm}", shape, dt))

        def sem(nm):
            s = ctx.semaphore(f"{name}_{nm}")
            sems.append(s)
            return s
        sems = []
        x = sb("x", [R, D])
        cs = sb("cs", [R, 2, 32])
        qk = sb("qk", [R, 8, 2, 32])
        m1 = sb("m1", [R, 8, 32])
        m2 = sb("m2", [R, 8, 32])
        qd = sb("qd", [R, BH, 2 if sample else 1, HD])
        kd = sb("kd", [R, BH, HD])
        kdm = sb("kdm", [NS, BH, NB, HD]) if sample else None
        n_t = 8 if sample else 6
        xT = sb("xT", [P, n_t, R])
        qdm = sb("qdm", [P, BH, NB // 2, NS]) if sample else None
        a = sb("a", [R, BH, R])
        n_st = NB // 2 if sample else 1
        st = sb("st", [P, NB // 2, BH, BDV]) if sample else sb("st", [P, 2, BDV])
        o = sb("o", [R, BH, BDV])
        sq = sb("sq", [R, BH, BDV])
        mean = sb("mean", [R, 4, BH])
        ps_t = ctx.enter_context(nc.psum_tensor(f"{name}_ps_t", [P, n_t, R], F32))
        ps_a = ctx.enter_context(nc.psum_tensor(f"{name}_ps_a", [P, 2, 512], F32))
        o_banks = 1 if sample else 2
        ps_o = ctx.enter_context(nc.psum_tensor(f"{name}_ps_o", [P, o_banks, 512], F32))
        ps_u = ctx.enter_context(nc.psum_tensor(f"{name}_ps_u", [P, 4 if sample else 1, 512], F32))

        def heads(ap, n, per):
            return ap[:, 0:per, 0:4 // per * n].rearrange("p e (m v) -> p m e v", v=n)
        first_load = ctx.semaphore(f"{name}_first_load")
        zeroed = ctx.semaphore(f"{name}_zeroed")
        loaded, rotated, decayed, turned, xT_ready, masked, a_raw, a_ready = (
            sem(n) for n in "loaded rotated decayed turned xT_ready masked a_raw a_ready".split())
        update_ready, o_acc, state_new, var_ready, root_ready, out_ready, stored, dve_step = (
            sem(n) for n in "update_ready o_acc state_new var_ready root_ready out_ready stored dve_step".split())

        def load(sp, i, s):
            if sample:
                sp.dma_start(x[:, :], h[1][:, QB:QB + D]).then_inc(s, 16)
                sp.dma_start(cs[:, :, :], trig[NT, 0:NS]).then_inc(s, 16)
                for e in range(2):
                    for m in range(NB // 2):
                        sp.dma_start(st[e * HD:(e + 1) * HD, m, :, :],
                                     state_in[2 * m + e].rearrange("h k v -> k h v")).then_inc(s, 16)
                return 2 + NB
            sp.dma_start(x[:, :], h[0][bass.ds(i * P, P), QB:QB + D]).then_inc(s, 16)
            sp.dma_start(cs[:, :, :].rearrange("p a f -> p (a f)"),
                         trig[bass.ds(i, 1)].rearrange("t p a f -> p (t a f)")).then_inc(s, 16)
            return 2

        with nc.Block() as block:
            @block.sync
            def _(sp):
                n = load(sp, 0, first_load)
                sp.wait_ge(first_load, 16 * n)

            if not sample:
                @block.vector
                def _(dve):
                    nc.vector.memset(st[:, :, :], 0.0).then_inc(zeroed, 1)
                    dve.wait_ge(zeroed, 1)

        def round_(i):
            with nc.Block() as block:
                @block.sync
                def _(sp):
                    if not sample:
                        sp.wait_ge(rotated, 1)
                        sp.wait_ge(state_new, 1)
                        load(sp, (i + 1) % n_rounds, loaded)
                    sp.wait_ge(out_ready, 1)
                    to = mix[T:ROWS, 512:D] if sample else mix[bass.ds(i * P, P), 512:D]
                    sp.dma_start(to, o[:, :, :].rearrange("p h e -> p (h e)")).then_inc(stored, 16)
                    if not sample:
                        sp.wait_ge(loaded, 32)
                    sp.wait_ge(stored, 16)

                @block.vector
                def _(dve):
                    steps = 0

                    def link(ins):
                        nonlocal steps
                        steps += 1
                        ins.then_inc(dve_step, 1)
                        dve.wait_ge(dve_step, steps)
                    v4 = x[:, 0:512].rearrange("p (h a f) -> p h a f", h=8, a=2)
                    x1, x2 = v4[:, :, 0, :], v4[:, :, 1, :]
                    cos = cs[:, 0, :].unsqueeze(1).broadcast_to([R, 8, 32])
                    sin = cs[:, 1, :].unsqueeze(1).broadcast_to([R, 8, 32])
                    nc.vector.tensor_tensor(m1[:, :, :], x1, cos, ALU.mult)
                    link(nc.vector.tensor_tensor(m2[:, :, :], x2, sin, ALU.mult))
                    link(nc.vector.tensor_tensor(qk[:, :, 0, :], m1[:, :, :], m2[:, :, :], ALU.subtract))
                    nc.vector.tensor_tensor(m1[:, :, :], x1, sin, ALU.mult)
                    link(nc.vector.tensor_tensor(m2[:, :, :], x2, cos, ALU.mult))
                    nc.vector.tensor_tensor(qk[:, :, 1, :], m1[:, :, :], m2[:, :, :], ALU.add).then_inc(rotated, 1)
                    dve.wait_ge(rotated, 1)
                    flat = qk[:, :, :, :].rearrange("p h a f -> p h (a f)")
                    qdec = con("qdec_s" if sample else "qdec").unsqueeze(2).broadcast_to([R, BH, HD])
                    kdec = con("kdec_s" if sample else "kdec").unsqueeze(2).broadcast_to([R, BH, HD])
                    nc.vector.tensor_tensor(qd[:, :, 0, :], flat[:, 0:4, :], qdec, ALU.mult)
                    if sample:
                        nc.vector.tensor_tensor(qd[:, :, 1, :], flat[:, 0:4, :], qdec, ALU.mult)
                    nc.vector.tensor_tensor(kd[:, :, :], flat[:, 4:8, :], kdec, ALU.mult).then_inc(decayed, 1)
                    if sample:
                        dve.wait_ge(decayed, 1)
                        for hh in range(BH):
                            last = nc.vector.tensor_tensor(kdm[:, hh, :, :], kd[:, hh, :].unsqueeze(1).broadcast_to([NS, NB, HD]),
                                                           con("kmask_s").unsqueeze(2).broadcast_to([NS, NB, HD]), ALU.mult)
                        last.then_inc(decayed, 1)
                    dve.wait_ge(turned, 1)
                    nc.vector.tensor_copy(xT[:, :, :], ps_t[:, 0:n_t, 0:R]).then_inc(xT_ready, 1)
                    if sample:
                        dve.wait_ge(xT_ready, 1)
                        for hh in range(BH):
                            last = nc.vector.tensor_tensor(qdm[:, hh, :, :], xT[:, 4 + hh, :].unsqueeze(1).broadcast_to([P, NB // 2, NS]),
                                                           con("qmask_s").rearrange("p (m t) -> p m t", t=NS), ALU.mult)
                        last.then_inc(masked, 1)
                    dve.wait_ge(a_raw, 1)
                    intra = con("intra_s" if sample else "intra").rearrange("p (h q) -> p h q", h=BH)
                    nc.vector.tensor_tensor(a[:, :, :].rearrange("p (m e) q -> p m e q", e=2), heads(ps_a[0:R, :, :], R, 2),
                                            intra.rearrange("p (m e) q -> p m e q", e=2), ALU.mult).then_inc(a_ready, 1)
                    dve.wait_ge(o_acc, 1)
                    dve.wait_ge(update_ready, 1)
                    for hh in range(BH):
                        if sample:
                            u = ps_u[:, hh, :].rearrange("p (m v) -> p m v", v=BDV)
                            last = nc.vector.scalar_tensor_tensor(out=st[:, :, hh, :], in0=st[:, :, hh, :],
                                                                  scalar=float(np.exp(LOG_G[hh] * NJ)), in1=u,
                                                                  op0=ALU.mult, op1=ALU.add)
                        else:
                            half, m = slice(hh % 2 * HD, hh % 2 * HD + HD), hh // 2
                            last = nc.vector.scalar_tensor_tensor(out=st[half, m, :], in0=st[half, m, :],
                                                                  scalar=float(np.exp(LOG_G[hh] * P)),
                                                                  in1=ps_u[half, 0, m * BDV:(m + 1) * BDV],
                                                                  op0=ALU.mult, op1=ALU.add)
                    last.then_inc(state_new, 1)
                    if sample:
                        po, o4 = ps_o[0:R, 0, :].rearrange("p (h v) -> p h v", h=BH), o[:, :, :]
                        mean0, mean_b = mean[:, 0, :], mean[:, 0, :].unsqueeze(2).broadcast_to([R, BH, BDV])
                    else:
                        po, o4 = heads(ps_o[:, :, :], BDV, 2), o[:, :, :].rearrange("p (m e) v -> p m e v", e=2)
                        mean0 = mean[:, 0, :].rearrange("p (m e) -> p m e", e=2)
                        mean_b = mean0.unsqueeze(3).broadcast_to([R, 2, 2, BDV])
                    link(nc.vector.tensor_reduce(mean0, po, AX, ALU.add))
                    link(nc.vector.tensor_scalar(mean[:, 0, :], mean[:, 0, :], 1.0 / BDV, None, ALU.mult))
                    link(nc.vector.tensor_tensor(o4, po, mean_b, ALU.subtract))
                    link(nc.vector.tensor_tensor(sq[:, :, :], o[:, :, :], o[:, :, :], ALU.mult))
                    link(nc.vector.tensor_reduce(mean[:, 1, :], sq[:, :, :], AX, ALU.add))
                    nc.vector.tensor_scalar(mean[:, 1, :], mean[:, 1, :], 1.0 / BDV, EPS_GN, ALU.mult, ALU.add).then_inc(var_ready, 1)
                    dve.wait_ge(root_ready, 1)
                    link(nc.vector.reciprocal(mean[:, 3, :], mean[:, 2, :]))
                    nc.vector.tensor_tensor(o[:, :, :], o[:, :, :], mean[:, 3, :].unsqueeze(2).broadcast_to([R, BH, BDV]),
                                            ALU.mult).then_inc(out_ready, 1)

                @block.scalar
                def _(act):
                    act.wait_ge(var_ready, 1)
                    nc.scalar.activation(mean[:, 2, :], mean[:, 1, :], ACT.Sqrt).then_inc(root_ready, 1)

                @block.tensor
                def _(pe):
                    pe.wait_ge(decayed, 2 if sample else 1)
                    flat = qk[:, :, :, :].rearrange("p h a f -> p (h a f)")
                    qdf = qd[:, :, :, :].rearrange("p h e f -> p (h e f)")
                    for m in range(4):
                        nc.tensor.transpose(ps_t[:, m, 0:R], flat[:, m * P:(m + 1) * P], con("ident")[0:R, 0:R])
                    for m in range(n_t - 4):
                        src = qdf[:, m * P:(m + 1) * P]
                        last = nc.tensor.transpose(ps_t[:, 4 + m, 0:R], src, con("ident")[0:R, 0:R])
                    last.then_inc(turned, 1)
                    pe.wait_ge(xT_ready, 1)
                    for hh in range(BH):
                        half, m = slice(hh % 2 * HD, hh % 2 * HD + HD), hh // 2
                        last = nc.tensor.matmul(ps_a[0:R, hh % 2, m * R:(m + 1) * R], xT[half, 2 + m, :], xT[half, m, :],
                                                start=True, stop=True)
                    last.then_inc(a_raw, 1)
                    v = x[:, 512:D].rearrange("p (h v) -> p h v", h=BH)
                    pe.wait_ge(a_ready, 1)
                    if sample:
                        pe.wait_ge(masked, 1)
                    for hh in range(BH):
                        half, m = slice(hh % 2 * HD, hh % 2 * HD + HD), hh // 2
                        acc = ps_o[0:R, 0, hh * BDV:(hh + 1) * BDV] if sample else ps_o[:, hh % 2, m * BDV:(m + 1) * BDV]
                        nc.tensor.matmul(acc, a[:, hh, :], v[:, hh, :], start=True, stop=False)
                        if sample:
                            for q in range(NB // 2):
                                last = nc.tensor.matmul(acc, qdm[:, hh, q, :], st[:, q, hh, :], start=False, stop=q == NB // 2 - 1)
                        else:
                            last = nc.tensor.matmul(acc, xT[half, 4 + m, :], st[half, m, :], start=False, stop=True)
                    last.then_inc(o_acc, 1)
                    for hh in range(BH):
                        half, m = slice(hh % 2 * HD, hh % 2 * HD + HD), hh // 2
                        if sample:
                            for q in range(NB // 2):
                                last = nc.tensor.matmul(ps_u[:, hh, q * BDV:(q + 1) * BDV],
                                                        kdm[:, hh, 2 * q:2 * q + 2, :].rearrange("p n k -> p (n k)"),
                                                        v[:, hh, :], start=True, stop=True)
                        else:
                            last = nc.tensor.matmul(ps_u[half, 0, m * BDV:(m + 1) * BDV], kd[:, hh, :], v[:, hh, :],
                                                    start=True, stop=True)
                    last.then_inc(update_ready, 1)
        if sample:
            round_(0)
        else:
            with nc.Fori(0, n_rounds) as i:
                round_(i)
                next_round(nc, sems)
        state_stored = ctx.semaphore(f"{name}_state_stored")
        with nc.Block() as block:
            @block.sync
            def _(sp):
                n = 0
                if sample:
                    for e in range(2):
                        for m in range(NB // 2):
                            sp.dma_start(state_out[2 * m + e].rearrange("h k v -> k h v"),
                                         st[e * HD:(e + 1) * HD, m, :, :]).then_inc(state_stored, 16)
                            n += 1
                else:
                    for hh in range(BH):
                        sp.dma_start(state_out[hh], st[hh % 2 * HD:hh % 2 * HD + HD, hh // 2, :]).then_inc(state_stored, 16)
                        n += 1
                sp.wait_ge(state_stored, 16 * n)


def attend_samples_dilated(nc, con, h_s, cache_k, cache_v, mix):
    with Phase(nc) as ctx:
        def sb(nm, shape, dt=F32):
            return ctx.enter_context(nc.sbuf_tensor(f"ds_{nm}", shape, dt))

        def sem(nm):
            s = ctx.semaphore(f"ds_{nm}")
            sems.append(s)
            return s
        sems = []
        NP = 4
        q_in = sb("q_in", [NS, 512])
        q_all = sb("q_all", [P, NB, NP * 32])
        q_cur = sb("q_cur", [P, NP * 32])
        kw, ks, kn = sb("kw", [P, 4, 512]), sb("ks", [STR, 4, 512]), sb("kn", [NJ, 512])
        vw, vs, vn = sb("vw", [P, 4, 512]), sb("vs", [STR, 4, 512]), sb("vn", [NJ, 512])
        kT = sb("kT", [P, NP, AK])
        pr = sb("pr", [32, AK])
        pw, pst, pn = sb("pw", [P, 4, 32]), sb("pst", [STR, 4, 32]), sb("pn", [NJ, 32])
        stat = sb("stat", [32, 3])
        part = sb("part", [32, 8, HD])
        o = sb("o", [32, HD])
        ps_t = [ctx.enter_context(nc.psum_tensor(f"ds_ps_t{b}", [P, 512], F32)) for b in range(2)]
        ps_s = ctx.enter_context(nc.psum_tensor("ds_ps_s", [32, 1024], F32))
        ps_p = ctx.enter_context(nc.psum_tensor("ds_ps_p", [P, 9, 32], F32))
        ps_o = ctx.enter_context(nc.psum_tensor("ds_ps_o", [32, 512], F32))
        first_k, first_v, q_loaded, q_zero, q_turned, q_placed = (
            ctx.semaphore(f"ds_{n}") for n in "first_k first_v q_loaded q_zero q_turned q_placed".split())
        k_in, v_in, q_ready, turned, copied_act, copied_dve, scores_ready, max_ready, probs_ready = (
            sem(n) for n in "k_in v_in q_ready turned copied_act copied_dve scores_ready max_ready probs_ready".split())
        probs_turned, probsT_ready, o_ready, inverse, part_ready, out_ready, stored = (
            sem(n) for n in "probs_turned probsT_ready o_ready inverse part_ready out_ready stored".split())
        copied = [copied_act, copied_dve]

        def load(sp, n, cache, w, st, new, col, s):
            c = cache[bass.ds(n, 1)].rearrange("n r c -> (n r) c")
            sp.dma_start(w[:, :, :].rearrange("p s c -> p (s c)"),
                         c[PAST - 512:PAST, :].rearrange("(p s) c -> p (s c)", s=4)).then_inc(s, 16)
            sp.dma_start(st[:, :, :].rearrange("p s c -> p (s c)"),
                         c[0:PAST - 512, :].rearrange("(p s) c -> p (s c)", s=16)[:, 0:4 * 512]).then_inc(s, 16)
            sp.dma_start(new[:, :], h_s[bass.ds(n * NJ, NJ), col:col + 512]).then_inc(s, 16)

        with nc.Block() as block:
            @block.sync
            def _(sp):
                sp.dma_start(q_in[:, :], h_s[:, QA:QA + 512]).then_inc(q_loaded, 16)
                load(sp, 0, cache_k, kw, ks, kn, KA, first_k)
                load(sp, 0, cache_v, vw, vs, vn, VA, first_v)
                sp.wait_ge(first_k, 48)
                sp.wait_ge(first_v, 48)

            @block.tensor
            def _(pe):
                pe.wait_ge(q_loaded, 16)
                for m in range(NP):
                    last = nc.tensor.transpose(ps_t[0][:, m * NS:(m + 1) * NS], q_in[:, m * P:(m + 1) * P], con("ident")[0:NS, 0:NS])
                last.then_inc(q_turned, 1)

            @block.vector
            def _(dve):
                nc.vector.memset(q_all[:, :, :], 0.0).then_inc(q_zero, 1)
                dve.wait_ge(q_zero, 1)
                dve.wait_ge(q_turned, 1)
                to = q_all[:, :, :].rearrange("p n (m h j) -> p n m h j", m=NP, h=8)
                for hh in range(8):
                    half = slice(hh % 2 * HD, hh % 2 * HD + HD)
                    src = ps_t[0][half, (hh // 2) * NS:(hh // 2 + 1) * NS].rearrange("p (n j) -> p n j", j=NJ)
                    last = nc.vector.tensor_scalar(to[half, :, hh // 2, hh, :], src, -SCALE, None, ALU.mult)
                last.then_inc(q_placed, 1)
                dve.wait_ge(q_placed, 1)

        widths = [P] * 4 + [STR] * 4 + [NJ]
        with nc.Fori(0, NB) as n:
            with nc.Block() as block:
                @block.sync
                def _(sp):
                    sp.wait_ge(turned, 9)
                    load(sp, (n + 1) % NB, cache_k, kw, ks, kn, KA, k_in)
                    sp.wait_ge(o_ready, 1)
                    load(sp, (n + 1) % NB, cache_v, vw, vs, vn, VA, v_in)
                    sp.wait_ge(out_ready, 1)
                    for hh in range(8):
                        sp.dma_start(mix[bass.ds(T + n * NJ, NJ), hh * HD:(hh + 1) * HD],
                                     o[hh * NJ:(hh + 1) * NJ, :]).then_inc(stored, 16)
                    sp.wait_ge(k_in, 48)
                    sp.wait_ge(v_in, 48)
                    sp.wait_ge(stored, 16 * 8)

                def copy_group(eng, copy, g):
                    eng.wait_ge(turned, g + 1)
                    c0 = sum(widths[:g])
                    copy(kT[:, :, c0:c0 + widths[g]],
                         ps_t[g % 2][:, :].rearrange("p (m c) -> p m c", m=NP)[:, :, 0:widths[g]]).then_inc(copied[g % 2], 1)

                @block.tensor
                def _(pe):
                    for g in range(9):
                        if g >= 2:
                            pe.wait_ge(copied[g % 2], g // 2)
                        src = kw[:, g, :] if g < 4 else ks[:, g - 4, :] if g < 8 else kn[:, :]
                        w = widths[g]
                        for m in range(NP):
                            last = nc.tensor.transpose(ps_t[g % 2][:, m * P:m * P + w], src[:, m * P:(m + 1) * P], con("ident")[0:w, 0:w])
                        last.then_inc(turned, 1)
                    pe.wait_ge(q_ready, 1)
                    pe.wait_ge(copied[0], 5)
                    pe.wait_ge(copied[1], 4)
                    for c0, c1 in ((0, 512), (512, AK)):
                        for m in range(NP):
                            last = nc.tensor.matmul(ps_s[:, c0:c1], q_cur[:, m * 32:(m + 1) * 32], kT[:, m, c0:c1],
                                                    start=m == 0, stop=m == NP - 1)
                    last.then_inc(scores_ready, 1)
                    pe.wait_ge(probs_ready, 1)
                    for g in range(9):
                        c0, w = sum(widths[:g]), widths[g]
                        last = nc.tensor.transpose(ps_p[0:w, g, :], pr[:, c0:c0 + w], con("ident")[0:32, 0:32])
                    last.then_inc(probs_turned, 1)
                    pe.wait_ge(probsT_ready, 1)
                    for g in range(9):
                        lhs = pw[:, g, :] if g < 4 else pst[:, g - 4, :] if g < 8 else pn[:, :]
                        rhs = vw[:, g, :] if g < 4 else vs[:, g - 4, :] if g < 8 else vn[:, :]
                        last = nc.tensor.matmul(ps_o[:, :], lhs, rhs, start=g == 0, stop=g == 8)
                    last.then_inc(o_ready, 1)

                @block.scalar
                def _(act):
                    for g in range(0, 9, 2):
                        copy_group(act, nc.scalar.copy, g)
                    act.wait_ge(max_ready, 1)
                    nc.scalar.activation(pr[:, :], pr[:, :], ACT.Exp, scale=-1.0, bias=stat[:, 0:1],
                                         accum_out=stat[:, 1:2]).then_inc(probs_ready, 1)

                @block.vector
                def _(dve):
                    nc.vector.tensor_copy(q_cur[:, :], q_all[:, bass.ds(n, 1), :].rearrange("p n c -> p (n c)")).then_inc(q_ready, 1)
                    for g in range(1, 9, 2):
                        copy_group(dve, nc.vector.tensor_copy, g)
                    dve.wait_ge(scores_ready, 1)
                    nc.vector.tensor_tensor_reduce(out=pr[:, :], in0=ps_s[:, 0:AK], in1=con("asbias"), scale=1.0, scalar=3e38,
                                                   op0=ALU.add, op1=ALU.min, accum_out=stat[:, 0:1]).then_inc(max_ready, 1)
                    dve.wait_ge(probs_turned, 1)
                    nc.vector.tensor_copy(pw[:, :, :], ps_p[:, 0:4, :])
                    nc.vector.tensor_copy(pst[:, :, :], ps_p[0:STR, 4:8, :])
                    nc.vector.tensor_copy(pn[:, :], ps_p[0:NJ, 8, :]).then_inc(probsT_ready, 1)
                    nc.vector.reciprocal(stat[:, 2:3], stat[:, 1:2]).then_inc(inverse, 1)
                    dve.wait_ge(inverse, 1)
                    dve.wait_ge(o_ready, 1)
                    nc.vector.scalar_tensor_tensor(out=part[:, :, :].rearrange("p h d -> p (h d)"), in0=ps_o[:, :], scalar=stat[:, 2:3],
                                                   in1=con("adiag"), op0=ALU.mult, op1=ALU.mult).then_inc(part_ready, 1)
                    dve.wait_ge(part_ready, 1)
                    nc.vector.tensor_reduce(o[:, :], part[:, :, :].rearrange("p h d -> p d h"), AX, ALU.add).then_inc(out_ready, 1)
            next_round(nc, sems)


class Compressor:

    def __init__(self, nc, ctx, con):
        self.nc, self.con = nc, con
        self.w1 = [ctx.enter_context(nc.sbuf_tensor(f"cmp_w1_{m}", [P, 16, CH], F32)) for m in range(2)]
        self.w2k = ctx.enter_context(nc.sbuf_tensor("cmp_w2k", [P, 2, 2, P], F32))
        self.w2v = ctx.enter_context(nc.sbuf_tensor("cmp_w2v", [P, 2, HD], F32))
        self.bias = ctx.enter_context(nc.sbuf_tensor("cmp_bias", [P, 2, 2], F32))

    def setup(self, w1, w2, pos):
        nc = self.nc
        with Phase(nc) as ctx:
            pe_in = ctx.enter_context(nc.sbuf_tensor("cmp_pos", [P, 2, 16], F32))
            ps = ctx.enter_context(nc.psum_tensor("cmp_ps", [P, 4], F32))
            loaded, zeroed, product, done = (ctx.semaphore(f"cmp_{n}") for n in "loaded zeroed product done".split())
            with nc.Block() as block:
                @block.sync
                def _(sp):
                    for m in range(2):
                        sp.dma_start(self.w1[m][:, :, :], w1[m].rearrange("(l p) f -> p l f", p=P)).then_inc(loaded, 16)
                        sp.dma_start(pe_in[:, m, :], pos[m].rearrange("(l a) d -> (a d) l", a=2),
                                     allow_slow_non_contiguous=True).then_inc(loaded, 16)
                    sp.dma_start(self.w2v[:, :, :], w2[1].rearrange("(c f) d -> f c d", f=P)).then_inc(loaded, 16)
                    sp.wait_ge(zeroed, 1)
                    for g in range(2):
                        sp.dma_start(self.w2k[:, :, g, g * HD:(g + 1) * HD],
                                     w2[0].rearrange("(c f) d -> f c d", f=P)).then_inc(loaded, 16)
                    sp.wait_ge(loaded, 16 * 7)

                @block.tensor
                def _(pe):
                    pe.wait_ge(loaded, 16 * 7)
                    for m in range(2):
                        for c in range(2):
                            for l in range(16):
                                last = nc.tensor.matmul(ps[:, 2 * m + c:2 * m + c + 1], self.w1[m][:, l, c * P:(c + 1) * P],
                                                        pe_in[:, m, l:l + 1], start=l == 0, stop=l == 15)
                    last.then_inc(product, 1)

                @block.vector
                def _(dve):
                    nc.vector.memset(self.w2k[:, :, :, :], 0.0).then_inc(zeroed, 1)
                    dve.wait_ge(product, 1)
                    nc.vector.tensor_copy(self.bias[:, :, :].rearrange("p m c -> p (m c)"), ps[:, :]).then_inc(done, 1)
                    dve.wait_ge(done, 1)

    def turn(self, x, q, pieces, out):
        for c in range(4):
            g, l = divmod(4 * q + c, 8)
            src = x[:, g, 2 * l:2 * l + 2, :].rearrange("p s d -> p (s d)")
            last = self.nc.tensor.transpose(out[:, c * P:c * P + pieces], src, self.con("ident")[0:pieces, 0:pieces])
        return last

    def hidden(self, m, xT, blocks, out, c):
        for l in range(16):
            s = 0 if l < 8 else 1
            last = self.nc.tensor.matmul(out[:, c * 256:c * 256 + 2 * blocks], self.w1[m][:, l, c * P:(c + 1) * P],
                                         xT[:, :, l % 8, s:s + blocks], start=l == 0, stop=l == 15)
        return last

    def down_k(self, hid, blocks, out):
        for x, (c, g) in enumerate([(c, g) for c in range(2) for g in range(2)]):
            last = self.nc.tensor.matmul(out, self.w2k[:, c, g, :], hid[:, c, g, :], start=x == 0, stop=x == 3)
        return last

    def down_v(self, hid, blocks, out):
        for g in range(2):
            for c in range(2):
                last = self.nc.tensor.matmul(out[:, g * HD:(g + 1) * HD], hid[:, c, g, :], self.w2v[:, c, :],
                                             start=c == 0, stop=c == 1)
        return last


def compress_prompt(nc, con, comp, h, kcmp, vcmp):
    with Phase(nc) as ctx:
        def sem(nm):
            return ctx.semaphore(f"cp_{nm}")
        x = [ctx.enter_context(nc.sbuf_tensor(f"cp_x{m}", [NPC, 2, 16, HD], F32)) for m in range(2)]
        xT = [ctx.enter_context(nc.sbuf_tensor(f"cp_xT{m}", [P, 2, 8, NPC], F32)) for m in range(2)]
        hid = [ctx.enter_context(nc.sbuf_tensor(f"cp_hid{m}", [P, 2, 2, NCB], F32)) for m in range(2)]
        kc = ctx.enter_context(nc.sbuf_tensor("cp_kc", [P, NCB], F32))
        vc = ctx.enter_context(nc.sbuf_tensor("cp_vc", [NCB, P], F32))
        ps_t = [ctx.enter_context(nc.psum_tensor(f"cp_t{b}", [P, 512], F32)) for b in range(2)]
        ps_h = [ctx.enter_context(nc.psum_tensor(f"cp_h{b}", [P, 512], F32)) for b in range(2)]
        ps_c = ctx.enter_context(nc.psum_tensor("cp_c", [P, 2, P], F32))
        loaded, turned, copied, hidden, active, products, ready, stored = (
            sem(n) for n in "loaded turned copied hidden active products ready stored".split())
        with nc.Block() as block:
            @block.sync
            def _(sp):
                for m, col in enumerate((KC, VC)):
                    for g in range(2):
                        sp.dma_start(x[m][:, g, :, :], h[0][:, col + g * HD:col + (g + 1) * HD].rearrange("(p s) c -> p s c", s=16)).then_inc(loaded, 16)
                sp.wait_ge(ready, 2)
                sp.dma_start(kcmp, kc[:, :]).then_inc(stored, 16)
                sp.dma_start(vcmp, vc[:, :]).then_inc(stored, 16)
                sp.wait_ge(stored, 32)

            @block.tensor
            def _(pe):
                pe.wait_ge(loaded, 64)
                for m in range(2):
                    for q in range(4):
                        g = 4 * m + q
                        if g >= 2:
                            pe.wait_ge(copied, g - 1)
                        comp.turn(x[m], q, NPC, ps_t[g % 2]).then_inc(turned, 1)
                for m in range(2):
                    pe.wait_ge(copied, 4 * (m + 1))
                    for c in range(2):
                        comp.hidden(m, xT[m], NCB, ps_h[m], c).then_inc(hidden, 1)
                pe.wait_ge(active, 4)
                comp.down_k(hid[0], NCB, ps_c[:, 0, 0:NCB])
                comp.down_v(hid[1], NCB, ps_c[0:NCB, 1, :]).then_inc(products, 1)

            @block.scalar
            def _(act):
                for m in range(2):
                    for c in range(2):
                        act.wait_ge(hidden, 2 * m + 2)
                        nc.scalar.activation(hid[m][:, c, :, :],
                                             ps_h[m][:, c * 256:c * 256 + 2 * NCB].rearrange("p (g b) -> p g b", g=2),
                                             ACT.Silu, bias=comp.bias[:, m, c:c + 1]).then_inc(active, 1)

            @block.vector
            def _(dve):
                for m in range(2):
                    for q in range(4):
                        dve.wait_ge(turned, 4 * m + q + 1)
                        nc.vector.tensor_copy(xT[m][:, q // 2, (q % 2) * 4:(q % 2) * 4 + 4, :],
                                              ps_t[q % 2][:, :].rearrange("p (l c) -> p l c", c=P)[:, :, 0:NPC]).then_inc(copied, 1)
                dve.wait_ge(products, 1)
                nc.vector.tensor_copy(kc[:, :], ps_c[:, 0, 0:NCB]).then_inc(ready, 1)
                nc.vector.tensor_copy(vc[:, :], ps_c[0:NCB, 1, :]).then_inc(ready, 1)


def attend_samples_sparse(nc, con, comp, h_s, pools, wins, page_table, branches, gathers):
    with Phase(nc) as ctx:
        def sb(nm, shape, dt=F32):
            return ctx.enter_context(nc.sbuf_tensor(f"ss_{nm}", shape, dt))

        def sem(nm):
            s = ctx.semaphore(f"ss_{nm}")
            sems.append(s)
            return s
        sems = []
        NKEY = PAST + NJ
        q_in = sb("q_in", [NS, 8, 2, HD])
        q_all = sb("q_all", [P, NB, 64])
        q_cur = sb("q_cur", [P, 64])
        pages = sb("pages", [P, NB + 1], I32)
        rows = sb("rows", [P, NB + 1], I32)
        pages_f, rows_f = sb("pages_f", [P, NB + 1]), sb("rows_f", [P, NB + 1])
        row_cur = sb("row_cur", [P, 1], I32)
        kc_in, vc_in, ks_in, vs_in = (sb(n, [P, 16, P]) for n in "kc_in vc_in ks_in vs_in".split())
        kc_p, vc_p = sb("kc_p", [P, 2, 16, HD]), sb("vc_p", [P, 2, 16, HD])
        kw_in, vw_in = sb("kw_in", [P, 4, P]), sb("vw_in", [P, 4, P])
        new_in = sb("new_in", [NJ, 4, P])
        xT = sb("xT", [P, 2, 8, P])
        hid = sb("hid", [P, 2, 2, NCS])
        kc, vc = sb("kc", [P, NCS]), sb("vc", [NCS, P])
        ksT, kwT, newT = sb("ksT", [P, PAST]), sb("kwT", [P, 512]), sb("newT", [P, 2, NJ])
        pc, pcT = sb("pc", [64, NCS]), sb("pcT", [NCS, 64])
        share, score, score2, top = sb("share", [64, NSL]), sb("score", [64, NSL]), sb("score2", [64, NSL]), sb("top", [64, 8])
        bias_b, bias = sb("bias_b", [64, NSL]), sb("bias", [64, 32, 4])
        psel, pwin = sb("psel", [64, NKEY]), sb("pwin", [64, 512 + NJ])
        pselT, pselnT = sb("pselT", [P, 16, 64]), sb("pselnT", [NJ, 64])
        pwinT, pwinnT = sb("pwinT", [P, 4, 64]), sb("pwinnT", [NJ, 64])
        mins, stat = sb("mins", [64, 8]), sb("stat", [64, 3, 3])
        o = sb("o", [64, 3, HD])
        ps_t = [ctx.enter_context(nc.psum_tensor(f"ss_ps_t{b}", [P, 512], F32)) for b in range(2)]
        ps_s = ctx.enter_context(nc.psum_tensor("ss_ps_s", [64, 4, 512], F32))
        ps_h = ctx.enter_context(nc.psum_tensor("ss_ps_h", [P, 512], F32))
        ps_m = ctx.enter_context(nc.psum_tensor("ss_ps_m", [P, 512], F32))
        M_KC, M_CS, M_SH, M_SUM, M_NEW, M_O = (slice(0, P), slice(128, 128 + NCS), slice(256, 256 + NSL), slice(290, 290 + NSL),
                                               slice(324, 332), slice(384, 512))
        pre = {n: ctx.semaphore(f"ss_{n}") for n in
               "table_in index_step index_ready q_loaded q_zero q_turned q_placed".split()}
        win_in, stored = ctx.semaphore("ss_win_in"), ctx.semaphore("ss_stored")
        s = {n: sem(n) for n in
             ("rows_in windows_in row_ready pieces_k pieces_v new_read sum_read q_ready turned copied_act copied_dve hid_k act_k prod_k kc_ready "
              "cmp_scores cmp_max cmp_probs cmp_norm share_raw share_ready sum_raw bias_ready sel_scores sel_max sel_probs "
              "hid_v act_v prod_v vc_ready cmp_o cmp_o_ready win_scores win_max win_probs sel_o sel_o_ready win_o win_o_ready "
              "dve_step").split()}
        copied = [s["copied_act"], s["copied_dve"]]

        def gather(pool, to, m, which):
            return pool.indirect_dma_start(out=to[:, :, :].rearrange("p s c -> p (s c)"), out_offset=None,
                                           in_=pools[m], in_offset=bass.IndirectOffsetOnAxis(ap=row_cur[:, 0:1], axis=0)
                                           ).then_inc(which, 16)

        def load_windows(sp, n, which):
            for to, fr in ((kw_in, wins[0]), (vw_in, wins[1])):
                sp.dma_start(to[:, :, :].rearrange("p s c -> p (s c)"),
                             fr[bass.ds(n, 1)].rearrange("n (p s) c -> p (n s c)", s=4)).then_inc(which, 16)
            sp.dma_start(new_in[:, :, :].rearrange("j m c -> j (m c)"), h_s[bass.ds(n * NJ, NJ), KS:KS + 512]).then_inc(which, 16)

        with nc.Block() as block:
            @block.sync
            def _(sp):
                for g in range(2):
                    sp.dma_start(q_in[:, :, g, :], h_s[:, QC + g * 512:QC + (g + 1) * 512].rearrange("t (r d) -> t r d", d=HD)
                                 ).then_inc(pre["q_loaded"], 16)
                for pg in range(PAST // PAGE):
                    for col, n0, n in ((0, 0, NB), (NB, 0, 1)):
                        sp.dma_start(pages[pg * 8:(pg + 1) * 8, col:col + n],
                                     page_table[n0:n0 + n, pg:pg + 1].rearrange("n a -> a n").broadcast_to([8, n]),
                                     allow_slow_non_contiguous=True).then_inc(pre["table_in"], 16)
                load_windows(sp, 0, win_in)
                sp.sem_inc(stored, 48)

            @block.gpsimd
            def _(pool):
                pool.wait_ge(pre["index_ready"], 1)
                for m, to in enumerate((kc_in, vc_in, ks_in, vs_in)):
                    gather(pool, to, m, gathers[("kc", "vc", "ks", "vs")[m]])

            @block.tensor
            def _(pe):
                pe.wait_ge(pre["q_loaded"], 32)
                for r in range(8):
                    last = nc.tensor.transpose(ps_t[0][:, r * NS:(r + 1) * NS], q_in[:, r, :, :].rearrange("t g d -> t (g d)"), con("ident")[0:NS, 0:NS])
                last.then_inc(pre["q_turned"], 1)

            @block.vector
            def _(dve):
                count = 0

                def link(ins):
                    nonlocal count
                    count += 1
                    ins.then_inc(pre["index_step"], 1)
                    dve.wait_ge(pre["index_step"], count)
                dve.wait_ge(pre["table_in"], 16 * 2 * (PAST // PAGE))
                link(nc.vector.tensor_copy(pages_f[:, :], pages[:, :]))
                link(nc.vector.tensor_scalar(rows_f[:, :], pages_f[:, :], 8.0, con("sub"), ALU.mult, ALU.add))
                link(nc.vector.tensor_copy(rows[:, :], rows_f[:, :]))
                nc.vector.tensor_copy(row_cur[:, :], rows[:, 0:1]).then_inc(pre["index_ready"], 1)
                nc.vector.memset(q_all[:, :, :], 0.0).then_inc(pre["q_zero"], 1)
                dve.wait_ge(pre["q_zero"], 1)
                dve.wait_ge(pre["q_turned"], 1)
                to = q_all[:, :, :].rearrange("p n (g r j) -> p n g r j", g=2, r=8)
                for g in range(2):
                    half = slice(g * HD, (g + 1) * HD)
                    src = ps_t[0][half, 0:256].rearrange("p (r n j) -> p n r j", r=8, n=NB)
                    last = nc.vector.tensor_scalar(to[half, :, g, :, :], src, -SCALE, None, ALU.mult)
                last.then_inc(pre["q_placed"], 1)
                dve.wait_ge(pre["q_placed"], 1)

        def v4(ap):
            return ap.rearrange("p (c k) -> p c k", c=4)
        G_SEL, G_CK, G_WIN, G_NEW, G_CV, G_PC, G_PS, G_PW = 0, 4, 8, 9, 10, 14, 15, 17
        N_GROUPS = 18

        with nc.Fori(0, NB) as n:
            with nc.Block() as block:
                @block.sync
                def _(sp):
                    sp.wait_ge(win_in, (n + 1) * 48)
                    sp.wait_ge(stored, (n + 1) * 48)
                    sp.sem_inc(s["windows_in"], 1)
                    for b, ready in enumerate(("cmp_o_ready", "sel_o_ready", "win_o_ready")):
                        sp.wait_ge(s[ready], 1)
                        if b == 2:
                            load_windows(sp, (n + 1) % NB, win_in)
                        sp.dma_start(branches[b, bass.ds(n * 64, 64), :], o[:, b, :]).then_inc(stored, 16)

                @block.gpsimd
                def _(pool):
                    for which in ("ks", "kc", "vc", "vs"):
                        pool.wait_ge(gathers[which], (n + 1) * 16)
                        pool.sem_inc(s["rows_in"], 1)
                    nc.gpsimd.tensor_copy(row_cur[:, :], rows[:, bass.ds(n + 1, 1)]).then_inc(s["row_ready"], 1)
                    pool.wait_ge(s["row_ready"], 1)
                    nc.gpsimd.tensor_copy(vc_p[:, :, :, :], vc_in[:, :, :].rearrange("p s (g d) -> p g s d", g=2)).then_inc(s["pieces_v"], 1)
                    pool.wait_ge(s["pieces_v"], 1)
                    gather(pool, vc_in, 1, gathers["vc"])
                    pool.wait_ge(s["pieces_k"], 2)
                    gather(pool, kc_in, 0, gathers["kc"])
                    pool.wait_ge(s["turned"], G_SEL + 4)
                    gather(pool, ks_in, 2, gathers["ks"])
                    pool.wait_ge(s["sel_o"], 1)
                    gather(pool, vs_in, 3, gathers["vs"])

                def copy_pieces_k(eng, copy, g):
                    eng.wait_ge(s["rows_in"], 2)
                    copy(kc_p[:, g, :, :], kc_in[:, :, g * HD:(g + 1) * HD]).then_inc(s["pieces_k"], 1)

                def copy_group(eng, copy, g):
                    eng.wait_ge(s["turned"], g + 1)
                    src = ps_t[g % 2]
                    done = copied[g % 2]
                    if g < G_CK:
                        copy(ksT[:, g * 512:(g + 1) * 512], src[:, :]).then_inc(done, 1)
                    elif g < G_WIN or G_CV <= g < G_PC:
                        if g == G_CV:
                            eng.wait_ge(s["hid_k"], 2)
                        if g == G_CV + 1:
                            eng.wait_ge(s["hid_k"], 2)
                        q = g - G_CK if g < G_WIN else g - G_CV
                        copy(xT[:, q // 2, (q % 2) * 4:(q % 2) * 4 + 4, :], v4(src[:, :])).then_inc(done, 1)
                    elif g == G_WIN:
                        copy(kwT[:, :], src[:, :]).then_inc(done, 1)
                    elif g == G_NEW:
                        copy(newT[:, :, :], src[:, 0:2 * NJ].rearrange("p (m j) -> p m j", j=NJ)).then_inc(done, 1)
                    elif g == G_PC:
                        copy(pcT[:, :], src[0:NCS, 0:64]).then_inc(done, 1)
                    elif g < G_PW:
                        x = g - G_PS
                        copy(pselT[:, 8 * x:8 * x + 8, :], src[:, :].rearrange("p (c k) -> p c k", c=8)).then_inc(done, 1)
                    else:
                        copy(pwinT[:, :, :], src[:, 0:256].rearrange("p (c k) -> p c k", c=4))
                        copy(pselnT[:, :], src[0:NJ, 256:320])
                        copy(pwinnT[:, :], src[0:NJ, 320:384]).then_inc(done, 1)

                @block.tensor
                def _(pe):
                    id64 = con("ident")[0:64, 0:64]

                    def bank(g):
                        if g >= 2:
                            pe.wait_ge(copied[g % 2], g // 2)
                        return ps_t[g % 2]

                    def all_copied(g):
                        pe.wait_ge(copied[0], g // 2 + 1)
                        pe.wait_ge(copied[1], (g + 1) // 2)
                    pe.wait_ge(s["rows_in"], 1)
                    for g in range(G_SEL, G_SEL + 4):
                        to = bank(g)
                        for c in range(4):
                            last = nc.tensor.transpose(to[:, c * P:(c + 1) * P], ks_in[:, 4 * g + c, :], con("ident"))
                        last.then_inc(s["turned"], 1)
                    pe.wait_ge(s["pieces_k"], 2)
                    for q in range(4):
                        comp.turn(kc_p, q, P, bank(G_CK + q)).then_inc(s["turned"], 1)
                    pe.wait_ge(s["windows_in"], 1)
                    to = bank(G_WIN)
                    for c in range(4):
                        last = nc.tensor.transpose(to[:, c * P:(c + 1) * P], kw_in[:, c, :], con("ident"))
                    last.then_inc(s["turned"], 1)
                    to = bank(G_NEW)
                    for c in range(2):
                        last = nc.tensor.transpose(to[:, c * NJ:(c + 1) * NJ], new_in[:, 2 * c, :], con("ident")[0:NJ, 0:NJ])
                    last.then_inc(s["turned"], 1)
                    all_copied(G_NEW)
                    pe.wait_ge(s["q_ready"], 1)
                    for c in range(2):
                        comp.hidden(0, xT, NCS, ps_h, c).then_inc(s["hid_k"], 1)
                    for c in range(4):
                        nc.tensor.matmul(ps_s[:, c, :], q_cur[:, :], ksT[:, c * 512:(c + 1) * 512], start=True, stop=True)
                    nc.tensor.matmul(ps_m[0:64, M_NEW.start:M_NEW.start + NJ], q_cur[:, :], newT[:, 0, :], start=True, stop=True)
                    nc.tensor.matmul(ps_m[0:64, M_NEW.start + NJ:M_NEW.stop], q_cur[:, :], newT[:, 1, :], start=True,
                                     stop=True).then_inc(s["sel_scores"], 1)
                    pe.wait_ge(s["act_k"], 2)
                    pe.wait_ge(s["new_read"], 1)
                    comp.down_k(hid, NCS, ps_m[:, 0:NCS]).then_inc(s["prod_k"], 1)
                    pe.wait_ge(s["pieces_v"], 1)
                    for q in range(4):
                        comp.turn(vc_p, q, P, bank(G_CV + q)).then_inc(s["turned"], 1)
                    pe.wait_ge(s["kc_ready"], 1)
                    nc.tensor.matmul(ps_m[0:64, M_CS], q_cur[:, :], kc[:, :], start=True, stop=True).then_inc(s["cmp_scores"], 1)
                    all_copied(G_CV + 3)
                    for c in range(2):
                        comp.hidden(1, xT, NCS, ps_h, c).then_inc(s["hid_v"], 1)
                    pe.wait_ge(s["cmp_norm"], 1)
                    to = bank(G_PC)
                    nc.tensor.transpose(to[0:NCS, 0:64], pc[:, :], id64).then_inc(s["turned"], 1)
                    all_copied(G_PC)
                    nc.tensor.matmul(ps_m[0:64, M_SH], pcT[:, :], con("overlap"), start=True, stop=True).then_inc(s["share_raw"], 1)
                    pe.wait_ge(s["share_ready"], 1)
                    nc.tensor.matmul(ps_m[0:64, M_SUM], con("same"), share[:, :], start=True, stop=True).then_inc(s["sum_raw"], 1)
                    pe.wait_ge(s["act_v"], 2)
                    pe.wait_ge(s["sum_read"], 1)
                    comp.down_v(hid, NCS, ps_m[0:NCS, M_KC]).then_inc(s["prod_v"], 1)
                    nc.tensor.matmul(ps_h[0:64, :], q_cur[:, :], kwT[:, :], start=True, stop=True).then_inc(s["win_scores"], 1)
                    pe.wait_ge(s["vc_ready"], 1)
                    nc.tensor.matmul(ps_m[0:64, M_O], pcT[:, :], vc[:, :], start=True, stop=True).then_inc(s["cmp_o"], 1)
                    pe.wait_ge(s["sel_probs"], 1)
                    for g in (G_PS, G_PS + 1):
                        to = bank(g)
                        for c in range(8):
                            k0 = (8 * (g - G_PS) + c) * P
                            last = nc.tensor.transpose(to[:, c * 64:(c + 1) * 64], psel[:, k0:k0 + P], id64)
                        last.then_inc(s["turned"], 1)
                    pe.wait_ge(s["win_probs"], 1)
                    to = bank(G_PW)
                    for c in range(4):
                        nc.tensor.transpose(to[:, c * 64:(c + 1) * 64], pwin[:, c * P:(c + 1) * P], id64)
                    nc.tensor.transpose(to[0:NJ, 256:320], psel[:, PAST:NKEY], id64)
                    nc.tensor.transpose(to[0:NJ, 320:384], pwin[:, 512:512 + NJ], id64).then_inc(s["turned"], 1)
                    all_copied(G_PW)
                    pe.wait_ge(s["cmp_o_ready"], 1)
                    pe.wait_ge(s["rows_in"], 4)
                    for c in range(16):
                        nc.tensor.matmul(ps_m[0:64, M_O], pselT[:, c, :], vs_in[:, c, :], start=c == 0, stop=False)
                    nc.tensor.matmul(ps_m[0:64, M_O], pselnT[:, :], new_in[:, 1, :], start=False, stop=True).then_inc(s["sel_o"], 1)
                    pe.wait_ge(s["sel_o_ready"], 1)
                    for c in range(4):
                        nc.tensor.matmul(ps_m[0:64, M_O], pwinT[:, c, :], vw_in[:, c, :], start=c == 0, stop=False)
                    nc.tensor.matmul(ps_m[0:64, M_O], pwinnT[:, :], new_in[:, 3, :], start=False, stop=True).then_inc(s["win_o"], 1)

                @block.scalar
                def _(act):
                    def silu(m, done, hidden):
                        act.wait_ge(s[hidden], 2)
                        if m == 1:
                            act.wait_ge(s["prod_k"], 1)
                        for c in range(2):
                            nc.scalar.activation(hid[:, c, :, :],
                                                 ps_h[:, c * 256:c * 256 + 2 * NCS].rearrange("p (g b) -> p g b", g=2),
                                                 ACT.Silu, bias=comp.bias[:, m, c:c + 1]).then_inc(s[done], 1)
                    copy_group(act, nc.scalar.copy, 0)
                    copy_pieces_k(act, nc.scalar.copy, 0)
                    for g in range(2, G_CV, 2):
                        copy_group(act, nc.scalar.copy, g)
                    silu(0, "act_k", "hid_k")
                    copy_group(act, nc.scalar.copy, G_CV)
                    copy_group(act, nc.scalar.copy, G_CV + 2)
                    act.wait_ge(s["cmp_max"], 1)
                    nc.scalar.activation(pc[:, :], ps_m[0:64, M_CS], ACT.Exp, scale=-1.0, bias=stat[:, 0, 0:1],
                                         accum_out=stat[:, 0, 1:2]).then_inc(s["cmp_probs"], 1)
                    copy_group(act, nc.scalar.copy, G_PC)
                    silu(1, "act_v", "hid_v")
                    act.wait_ge(s["sel_max"], 1)
                    nc.scalar.activation(psel[:, :], psel[:, :], ACT.Exp, scale=-1.0, bias=stat[:, 1, 0:1],
                                         accum_out=stat[:, 1, 1:2]).then_inc(s["sel_probs"], 1)
                    act.wait_ge(s["win_max"], 1)
                    nc.scalar.activation(pwin[:, :], pwin[:, :], ACT.Exp, scale=-1.0, bias=stat[:, 2, 0:1],
                                         accum_out=stat[:, 2, 1:2]).then_inc(s["win_probs"], 1)
                    copy_group(act, nc.scalar.copy, G_PS + 1)

                @block.vector
                def _(dve):
                    count = 0

                    def link(ins):
                        nonlocal count
                        count += 1
                        ins.then_inc(s["dve_step"], 1)
                        dve.wait_ge(s["dve_step"], count)

                    def write_out(b, done, ready):
                        if b == 0:
                            dve.wait_ge(s["windows_in"], 1)
                        dve.wait_ge(s[done], 1)
                        for g in range(2):
                            r = slice(32 * g, 32 * g + 32)
                            src = ps_m[r, M_O.start + g * HD:M_O.start + (g + 1) * HD]
                            if b == 0:
                                last = nc.vector.tensor_copy(o[r, b, :], src)
                            else:
                                last = nc.vector.tensor_scalar(o[r, b, :], src, stat[r, b, 2:3], None, ALU.mult)
                        last.then_inc(s[ready], 1)
                    nc.vector.tensor_copy(q_cur[:, :], q_all[:, bass.ds(n, 1), :].rearrange("p n c -> p (n c)")).then_inc(s["q_ready"], 1)
                    copy_pieces_k(dve, nc.vector.tensor_copy, 1)
                    for g in range(1, G_CV, 2):
                        copy_group(dve, nc.vector.tensor_copy, g)
                    dve.wait_ge(s["sel_scores"], 1)
                    for x, dst in enumerate((psel[:, PAST:NKEY], pwin[:, 512:512 + NJ])):
                        last = nc.vector.tensor_tensor_reduce(out=dst, in0=ps_m[0:64, M_NEW.start + x * NJ:M_NEW.start + (x + 1) * NJ],
                                                              in1=con("newmask"), scale=1.0, scalar=3e38, op0=ALU.add,
                                                              op1=ALU.min, accum_out=mins[:, 4 + x:5 + x])
                    last.then_inc(s["new_read"], 1)
                    dve.wait_ge(s["prod_k"], 1)
                    nc.vector.tensor_copy(kc[:, :], ps_m[:, 0:NCS]).then_inc(s["kc_ready"], 1)
                    copy_group(dve, nc.vector.tensor_copy, G_CV + 1)
                    dve.wait_ge(s["cmp_scores"], 1)
                    nc.vector.tensor_reduce(stat[:, 0, 0:1], ps_m[0:64, M_CS], AX, ALU.min).then_inc(s["cmp_max"], 1)
                    copy_group(dve, nc.vector.tensor_copy, G_CV + 3)
                    dve.wait_ge(s["cmp_probs"], 1)
                    link(nc.vector.reciprocal(stat[:, 0, 2:3], stat[:, 0, 1:2]))
                    nc.vector.tensor_scalar(pc[:, :], pc[:, :], stat[:, 0, 2:3], None, ALU.mult).then_inc(s["cmp_norm"], 1)
                    dve.wait_ge(s["share_raw"], 1)
                    nc.vector.tensor_copy(share[:, :], ps_m[0:64, M_SH]).then_inc(s["share_ready"], 1)
                    dve.wait_ge(s["sum_raw"], 1)
                    nc.vector.tensor_copy(score[:, :], ps_m[0:64, M_SUM]).then_inc(s["sum_read"], 1)
                    dve.wait_ge(s["sum_read"], 1)
                    nc.vector.memset(score[:, 0:1], 1e9)
                    link(nc.vector.memset(score[:, 31:33], 1e9))
                    link(nc.vector.max(top[:, :], score[:, :]))
                    link(nc.vector.match_replace(score2[:, :], top[:, :], score[:, :], -3e38))
                    link(nc.vector.max(top[:, :], score2[:, :]))
                    link(nc.vector.match_replace(score[:, :], top[:, :], score2[:, :], -3e38))
                    link(nc.vector.tensor_scalar(bias_b[:, :], score[:, :], -1e37, BIG, ALU.is_gt, ALU.mult))
                    link(nc.vector.tensor_copy(bias[:, :, :], bias_b[:, 0:32].unsqueeze(2).broadcast_to([64, 32, 4])))
                    dve.wait_ge(s["sel_scores"], 1)
                    fb = bias[:, :, :].rearrange("p b s -> p (b s)").unsqueeze(1).broadcast_to([64, 4, P])
                    for c in range(4):
                        last = nc.vector.tensor_tensor_reduce(out=psel[:, c * 512:(c + 1) * 512].rearrange("p (s k) -> p s k", s=4),
                                                       in0=ps_s[:, c, :].rearrange("p (s k) -> p s k", s=4), in1=fb,
                                                       scale=1.0, scalar=3e38, op0=ALU.add, op1=ALU.min,
                                                       accum_out=mins[:, c:c + 1])
                        last.then_inc(s["dve_step"], 1)
                        count += 1
                    dve.wait_ge(s["dve_step"], count)
                    nc.vector.tensor_reduce(stat[:, 1, 0:1], mins[:, 0:5], AX, ALU.min).then_inc(s["sel_max"], 1)
                    dve.wait_ge(s["prod_v"], 1)
                    nc.vector.tensor_copy(vc[:, :], ps_m[0:NCS, M_KC]).then_inc(s["vc_ready"], 1)
                    dve.wait_ge(s["win_scores"], 1)
                    link(nc.vector.tensor_tensor_reduce(out=pwin[:, 0:512], in0=ps_h[0:64, :], in1=con("winmask"), scale=1.0,
                                                        scalar=3e38, op0=ALU.add, op1=ALU.min, accum_out=mins[:, 6:7]))
                    nc.vector.tensor_reduce(stat[:, 2, 0:1], mins[:, 5:7], AX, ALU.min).then_inc(s["win_max"], 1)
                    write_out(0, "cmp_o", "cmp_o_ready")
                    copy_group(dve, nc.vector.tensor_copy, G_PS)
                    dve.wait_ge(s["sel_probs"], 1)
                    dve.wait_ge(s["win_probs"], 1)
                    link(nc.vector.reciprocal(stat[:, 1:3, 2], stat[:, 1:3, 1]))
                    copy_group(dve, nc.vector.tensor_copy, G_PW)
                    write_out(1, "sel_o", "sel_o_ready")
                    write_out(2, "win_o", "win_o_ready")
            next_round(nc, sems)

        with nc.Block() as block:
            @block.sync
            def _(sp):
                sp.wait_ge(stored, (NB + 1) * 48)
                sp.wait_ge(win_in, (NB + 1) * 48)

            @block.gpsimd
            def _(pool):
                for which in ("ks", "kc", "vc", "vs"):
                    pool.wait_ge(gathers[which], (NB + 1) * 16)


def mix_sample_branches(nc, h_s, branches, mix_s):
    with Phase(nc) as ctx:
        b = ctx.enter_context(nc.sbuf_tensor("mb_b", [NS, 3, D], F32))
        gl = ctx.enter_context(nc.sbuf_tensor("mb_gl", [NS, 48], F32))
        out = ctx.enter_context(nc.sbuf_tensor("mb_out", [NS, D], F32))
        loaded, gates, step, ready, stored = (ctx.semaphore(f"mb_{n}") for n in "loaded gates step ready stored".split())
        n_loads = 1 + 3 * NB

        def load(eng, samples):
            for n in samples:
                for x in range(3):
                    eng.dma_start(b[n * NJ:(n + 1) * NJ, x, :].rearrange("j (h d) -> j h d", d=HD),
                                  branches[x, n * 64:(n + 1) * 64, :].rearrange("(h j) d -> j h d", j=NJ)).then_inc(loaded, 16)
        with nc.Block() as block:
            @block.sync
            def _(sp):
                sp.dma_start(gl[:, :], h_s[:, GL:GL + 48]).then_inc(loaded, 16)
                load(sp, range(0, NB, 2))
                sp.wait_ge(ready, 1)
                sp.dma_start(mix_s, out[:, :]).then_inc(stored, 16)
                sp.wait_ge(stored, 16)

            @block.scalar
            def _(act):
                load(act, range(1, NB, 2))
                act.wait_ge(loaded, 16 * n_loads)
                nc.scalar.activation(gl[:, :], gl[:, :], ACT.Sigmoid).then_inc(gates, 1)

            @block.vector
            def _(dve):
                dve.wait_ge(loaded, 16 * n_loads)
                dve.wait_ge(gates, 1)
                for x in range(3):
                    v = b[:, x, :].rearrange("t (h d) -> t h d", d=HD)
                    g = gl[:, :].rearrange("t (h x) -> t h x", x=3)[:, :, x].unsqueeze(2).broadcast_to([NS, 16, HD])
                    last = nc.vector.tensor_tensor(v, v, g, ALU.mult)
                last.then_inc(step, 1)
                dve.wait_ge(step, 1)
                nc.vector.tensor_tensor(out[:, :], b[:, 0, :], b[:, 1, :], ALU.add).then_inc(step, 1)
                dve.wait_ge(step, 2)
                nc.vector.tensor_tensor(out[:, :], out[:, :], b[:, 2, :], ALU.add).then_inc(ready, 1)


def store_rows(nc, name, pairs):
    with Phase(nc) as ctx:
        stored = ctx.semaphore(f"{name}_stored")
        with nc.Block() as block:
            @block.sync
            def _(sp):
                for to, fr in pairs:
                    sp.dma_start(to, fr).then_inc(stored, 16)
                sp.wait_ge(stored, 16 * len(pairs))


class Constants:

    def __init__(self, nc, ctx, dram):
        self.all = ctx.enter_context(nc.sbuf_tensor("constants", [P, CONST.shape[1]], F32))
        t16 = ctx.enter_context(nc.sbuf_tensor("constants16", [P, 3 * P + NT * NCB], BF16))
        self.ident16, self.causal16, self.edge16 = (t16[:, k * P:(k + 1) * P] for k in range(3))
        self.cmask16 = t16[:, 3 * P:].rearrange("p (t c) -> p t c", t=NT)
        self.rows = {n: P for n in COLS}
        self.rows.update(asbias=32, adiag=32, newmask=64, winmask=64, same=64, overlap=NCS, intra_s=NS, qdec_s=NS,
                         kdec_s=NS, kmask_s=NS)
        with Phase(nc) as phase, nc.Block() as block:
            loaded, cast = phase.semaphore("constants_in"), phase.semaphore("constants_cast")

            @block.sync
            def _(sp):
                sp.dma_start(self.all[:, :], dram).then_inc(loaded, 16)

            @block.vector
            def _(dve):
                dve.wait_ge(loaded, 16)
                for to, name in ((self.ident16, "ident"), (self.causal16, "causal"), (self.edge16, "edge"), (t16[:, 3 * P:], "cmask")):
                    last = nc.vector.tensor_copy(to, self(name))
                last.then_inc(cast, 1)
                dve.wait_ge(cast, 1)

    def __call__(self, name):
        a, b = COLS[name]
        return self.all[0:self.rows[name], a:b]


def build(nc, i, o):
    h0 = nc.dram_tensor("h0", [ROWS, E_COLS], F32, kind="Internal").ap()
    h1 = nc.dram_tensor("h1", [ROWS, O_COLS], F32, kind="Internal").ap()
    mix0 = nc.dram_tensor("mix0", [ROWS, D], F32, kind="Internal").ap()
    mix1 = nc.dram_tensor("mix1", [ROWS, D], F32, kind="Internal").ap()
    x1 = nc.dram_tensor("x1", [ROWS, D], F32, kind="Internal").ap()
    x2 = nc.dram_tensor("x2", [ROWS, D], F32, kind="Internal").ap()
    kcmp = nc.dram_tensor("kcmp", [P, NCB], F32, kind="Internal").ap()
    vcmp = nc.dram_tensor("vcmp", [NCB, P], F32, kind="Internal").ap()
    branches = nc.dram_tensor("branches", [3, NB * 64, HD], F32, kind="Internal").ap()

    def both(a):
        return a[0:T, :], a[T:ROWS, :]
    with ExitStack() as ctx:
        con = Constants(nc, ctx, i["const"])
        gathers = {n: ctx.enter_context(nc.semaphore("gathered_" + n)) for n in ("kc", "vc", "ks", "vs")}
        ident = con("ident")
        x0 = (i["x_prompt"], i["x_sample"])
        project(nc, ident, "norm", x0, i["even_w_in"], E_COLS, both(h0), gain=i["even_norm"])
        store_rows(nc, "even", [(o["a_k_p"], h0[0:T, KA:KA + 512]), (o["a_k_s"], h0[T:, KA:KA + 512]),
                                (o["a_v_p"], h0[0:T, VA:VA + 512]), (o["a_v_s"], h0[T:, VA:VA + 512])])
        attend_prompt(nc, con, "dilated", both(h0), mix0, 4)
        retain(nc, con, both(h0), mix0, i["trig"], o["ret_p"])
        retain(nc, con, both(h0), mix0, i["trig"], o["ret_s"], state_in=i["state_ret"])
        attend_samples_dilated(nc, con, h0[T:ROWS, :], i["cache_a_k"], i["cache_a_v"], mix0)
        project(nc, ident, "gate", both(mix0), i["even_w_out"], D, both(x1),
                gates=(both(h0), (ZA, ZA + 512), (ZB, ZB + 512)), residual=x0)
        project(nc, ident, "norm", both(x1), i["odd_w_in"], O_COLS, both(h1), gain=i["odd_norm"])
        pairs = []
        for name, col in (("kc", KC), ("vc", VC), ("ks", KS), ("vs", VS), ("kw", KW), ("vw", VW)):
            first = T - 512 if name in ("kw", "vw") else 0
            pairs.append((o[name + "_p"], h1[first:T, col:col + P]))
            pairs.append((o[name + "_s"], h1[T:, col:col + P]))
        store_rows(nc, "odd", pairs)
        with ExitStack() as inner:
            comp = Compressor(nc, inner, con)
            comp.setup((i["cmp_w1_k"], i["cmp_w1_v"]), (i["cmp_w2_k"], i["cmp_w2_v"]), (i["cmp_pos_k"], i["cmp_pos_v"]))
            compress_prompt(nc, con, comp, both(h1), kcmp, vcmp)
            attend_samples_sparse(nc, con, comp, h1[T:ROWS, :], [i["pool_" + n] for n in ("kc", "vc", "ks", "vs")],
                                  (i["cache_c_kwin"], i["cache_c_vwin"]), i["page_table"], branches, gathers)
        mix_sample_branches(nc, h1[T:ROWS, :], branches, mix1[T:ROWS, :])
        attend_prompt(nc, con, "sparse", both(h1), mix1, 8, kcmp, vcmp)
        project(nc, ident, "gate", both(mix1), i["odd_w_out"], D, both(x2), gates=(both(h1), (ZC, ZC + D)), residual=both(x1))
        final_norm(nc, both(x2), i["final_norm"], (o["y_p"], o["y_s"]))


_IN = {"x_prompt": (T, D), "x_sample": (NS, D), "cache_a_k": (NB, PAST, 512), "cache_a_v": (NB, PAST, 512),
       "state_ret": (NB, BH, HD, BDV), "cache_c_kcmp": (NPOOL * 8, 2048), "cache_c_vcmp": (NPOOL * 8, 2048),
       "cache_c_ksel": (NPOOL * 8, 2048), "cache_c_vsel": (NPOOL * 8, 2048), "cache_c_kwin": (NB, 512, P),
       "cache_c_vwin": (NB, 512, P), "page_table": (NB, PAST // PAGE), "even_norm": (D,), "even_w_in": (D, E_COLS),
       "even_w_out": (D, D), "odd_norm": (D,), "odd_w_in": (D, O_COLS), "odd_w_out": (D, D), "cmp_pos_k": (32, HD),
       "cmp_w1_k": (2048, CH), "cmp_w2_k": (CH, HD), "cmp_pos_v": (32, HD), "cmp_w1_v": (2048, CH), "cmp_w2_v": (CH, HD),
       "final_norm": (D,)}
_OUT = [("y_p", (1, T, D)), ("y_s", (NB, NJ, D)), ("a_k_p", (1, 1, T, 8, HD)), ("a_k_s", (1, NB, NJ, 8, HD)),
        ("a_v_p", (1, 1, T, 8, HD)), ("a_v_s", (1, NB, NJ, 8, HD)), ("ret_p", (1, 1, BH, HD, BDV)),
        ("ret_s", (1, NB, BH, HD, BDV))] + [
    (f"{n}_{w}", ((1, 1, T // (2 if n in ("kw", "vw") else 1), 2, HD) if w == "p" else (1, NB, NJ, 2, HD)))
    for n in ("kc", "vc", "ks", "vs", "kw", "vw") for w in ("p", "s")]


def kernel(**inputs):
    import concourse.bacc as _bacc
    from concourse.bass_utils import run_bass_kernel_spmd as _run

    nc = _bacc.Bacc("TRN2", target_bir_lowering=False, num_devices=1)
    arrays, ins, outs = {}, {}, {}
    laid = {n: np.ascontiguousarray(inputs[n]).reshape(shape) for n, shape in _IN.items()}
    laid["const"], laid["trig"] = CONST, TRIG
    for name, a in laid.items():
        arrays["in_" + name] = a
        ins[name] = nc.dram_tensor("in_" + name, a.shape, mybir.dt.from_np(a.dtype), kind="ExternalInput").ap()
    for short, full in (("kc", "kcmp"), ("vc", "vcmp"), ("ks", "ksel"), ("vs", "vsel")):
        ins["pool_" + short] = ins["cache_c_" + full]
    flat = {"y_p": (T, D), "y_s": (NS, D), "ret_p": (BH, HD, BDV), "ret_s": (NB, BH, HD, BDV)}
    for name, shape in _OUT:
        cols = 512 if name[:2] == "a_" else P
        s2 = flat.get(name, (int(np.prod(shape)) // cols, cols))
        outs[name] = nc.dram_tensor("out_" + name, s2, F32, kind="ExternalOutput").ap()
    build(nc, ins, outs)
    r = _run(nc, [arrays], core_ids=[0])
    return tuple(r.results[0]["out_" + name].reshape(shape) for name, shape in _OUT)
```

```python
import concourse.bass as bass
from concourse import mybir
import numpy as np
import math
from contextlib import ExitStack

F32 = mybir.dt.float32
BF16 = mybir.dt.bfloat16
F32R = mybir.dt.float32r
I32 = mybir.dt.int32
ALU = mybir.AluOpType
ACT = mybir.ActivationFunctionType
AX = mybir.AxisListType.X

P = 128
D = 1024
T = 1024
NT = T // P
NB, NJ = 8, 4
NS = NB * NJ
ROWS = T + NS
HD = 64
PAST = 2048
PAGE = 128
NPOOL = 160
SCALE = HD ** -0.5
BIG = 1e30
EPS_RMS, EPS_GN = 1e-6, 1e-5
QA, KA, VA, ZA, QB, KB, VB, ZB, E_COLS = 0, 512, 1024, 1536, 2048, 2304, 2560, 3072, 3584
QC, KC, VC, KS, VS, KW, VW, GL, ZC, O_COLS = 0, 1024, 1152, 1280, 1408, 1536, 1664, 1792, 1840, 2864
KD = D // P
LAG = 4
WEIGHT_AT = 2
CUT_AFTER = 5
BH, BDV = 4, 128
NPC = T // 16
NCB = NPC - 1
NPS = PAST // 16
NCS = NPS - 1
NSL = 33
CH = 256
STR = 96
AK = 4 * P + 4 * STR + NJ


def _constants():
    cols, parts = {}, []

    def put(name, a):
        a = np.asarray(a, np.float64).reshape(np.asarray(a).shape[0], -1)
        full = np.zeros((P, a.shape[1]), np.float32)
        full[:a.shape[0]] = a
        at = sum(x.shape[1] for x in parts)
        parts.append(full)
        cols[name] = (at, at + a.shape[1])

    p = np.arange(P)[:, None]
    f = np.arange(P)[None, :]
    put("ident", np.eye(P))
    put("causal", np.where(f > p, BIG, 0.0))
    put("edge", np.where(f < p, BIG, 0.0))
    t, c = np.arange(NT)[None, :, None], np.arange(NCB)[None, None, :]
    put("cmask", np.where(16 * c + 31 > 128 * t + p[:, :, None], BIG, 0.0))

    def many(dist):
        n = ((dist <= 128).astype(int) + ((dist % 4 == 0) & (dist <= 512)) + ((dist % 16 == 0) & (dist <= 2048)))
        n = np.where(dist >= 0, n, 0)
        return np.where(n > 0, -np.log(np.maximum(n, 1)), BIG)

    put("abias", many(p + (NT - 1) * P - np.arange(NT * P)[None, :]))
    row = np.arange(32)[:, None]
    j = row % NJ
    win = PAST - 512 + 4 * np.arange(P)[None, :] + np.arange(4)[:, None]
    strided = 16 * np.arange(STR)[None, :] + np.arange(4)[:, None]
    new = PAST + np.arange(NJ)
    pos = np.concatenate([win.ravel(), strided.ravel(), new])[None, :]
    put("asbias", many(PAST + j - pos))
    put("adiag", np.repeat((row // NJ == np.arange(8)[None, :]).astype(float), HD, axis=1))
    row = np.arange(64)[:, None]
    j = row % NJ
    put("newmask", np.where(np.arange(NJ)[None, :] > j, BIG, 0.0))
    put("winmask", np.where((4 * np.arange(P)[None, :] + np.arange(4)[:, None]).ravel()[None, :] < j, BIG, 0.0))
    put("same", ((row // 32 == row.T // 32) & (row % NJ == row.T % NJ)).astype(float))
    c, b = np.arange(NCS)[:, None], np.arange(NSL)[None, :]
    over = np.minimum(16 * c + 32, 64 * b + 64) - np.maximum(16 * c, 64 * b)
    put("overlap", np.clip(over, 0, None) / 32.0)
    put("valid", (p >= 31).astype(float))
    put("sub", p % 8)
    lg = np.log1p(-np.exp2(-5.0 - np.arange(BH)))
    h = np.arange(BH)[None, :]
    k3, q3, h3 = np.arange(P)[:, None, None], np.arange(P)[None, None, :], np.arange(BH)[None, :, None]
    put("intra", np.where(q3 >= k3, np.exp(lg[h3] * np.maximum(q3 - k3, 0)), 0.0) * SCALE)
    put("qdec", np.exp(lg[h] * (p + 1.0)))
    put("kdec", np.exp(lg[h] * (P - 1.0 - p)) * SCALE)
    k3, q3 = np.arange(NS)[:, None, None], np.arange(NS)[None, None, :]
    put("intra_s", np.where((q3 >= k3) & (q3 // NJ == k3 // NJ), np.exp(lg[h3] * np.maximum(q3 - k3, 0)), 0.0) * SCALE)
    js = np.arange(NS)[:, None] % NJ
    put("qdec_s", np.exp(lg[h] * (js + 1.0)))
    put("kdec_s", np.exp(lg[h] * (NJ - 1.0 - js)) * SCALE)
    m3, t3 = np.arange(NB // 2)[None, :, None], np.arange(NS)[None, None, :]
    put("qmask_s", (t3 // NJ == 2 * m3 + p[:, :, None] // HD).astype(float))
    put("kmask_s", (np.arange(NS)[:, None] // NJ == np.arange(NB)[None, :]).astype(float))
    freqs = (10000.0 ** (-np.arange(32) / 32.0)).astype(np.float32)
    tok = np.concatenate([np.arange(T), np.zeros(P)]).reshape(NT + 1, P)
    tok[NT, :NS] = PAST + np.arange(NS) % NJ
    ang = (tok.astype(np.float32)[:, :, None] * freqs[None, None, :]).astype(np.float64)
    trig = np.stack([np.cos(ang), np.sin(ang)], axis=2).astype(np.float32)
    return np.concatenate(parts, axis=1), cols, trig, lg


CONST, COLS, TRIG, LOG_G = _constants()


def gemm_tiles():
    return [(t, P if t < NT else NS) for t in range(NT + 1)]


def next_round(nc, sems):
    nums = sorted(s.num for s in sems)
    first = nums[0]
    for at, num in enumerate(nums):
        if at + 1 == len(nums) or nums[at + 1] != num + 1:
            nc.sync.sem_clear(range(first, num + 1))
            first = nums[at + 1] if at + 1 < len(nums) else None
    nc.all_engine_barrier()


class Phase(ExitStack):

    def __init__(self, nc):
        super().__init__()
        self.nc, self.semaphores = nc, []

    def semaphore(self, name):
        s = self.enter_context(self.nc.semaphore(name))
        self.semaphores.append(s)
        return s

    def __exit__(self, *error):
        if error[0] is None:
            next_round(self.nc, self.semaphores)
        return super().__exit__(*error)


def project(nc, ident, kind, src, w, n_cols, dst, gain=None, gates=None, residual=None):
    chunk = next(c for c in range(448, 0, -2) if n_cols % c == 0)
    n_chunks = n_cols // chunk
    with Phase(nc) as ctx:
        def sb(name, shape, dt=F32):
            return ctx.enter_context(nc.sbuf_tensor(f"{dst[0].tensor.name}_{name}", shape, dt))

        def sem(name):
            return ctx.semaphore(f"{dst[0].tensor.name}_{name}")

        y_lo, y_hi = (sb(n, [P, KD, (NT + 1) * P], F32R) for n in ("y_lo", "y_hi"))
        w_raw = sb("w_raw", [P, KD, chunk])
        w_lo, w_hi = (sb(n, [P, KD, 2, chunk], F32R) for n in ("w_lo", "w_hi"))
        res = sb("res", [P, 3, chunk])
        outb = sb("out", [P, 3, chunk])
        x = sb("x", [P, 2, D])
        z = sb("z", [P, 2, D])
        y = sb("y", [P, 2, D])
        g = sb("g", [P, D])
        stat = sb("stat", [P, 2, 4])
        tps = [ctx.enter_context(nc.psum_tensor(f"{dst[0].tensor.name}_tps{b}", [P, KD, P], F32)) for b in range(2)]
        acc = [ctx.enter_context(nc.psum_tensor(f"{dst[0].tensor.name}_acc{b}", [P, 512], F32)) for b in range(3)]
        gain_in = sem("gain_in")
        loaded = [sem(f"loaded{b}") for b in range(2)]
        squares = [sem(f"squares{b}") for b in range(2)]
        means = [sem(f"means{b}") for b in range(2)]
        roots = [sem(f"roots{b}") for b in range(2)]
        inverses = [sem(f"inverses{b}") for b in range(2)]
        rows_ready = [sem(f"rows_ready{b}") for b in range(2)]
        turned = [sem(f"turned{b}") for b in range(2)]
        yT_written = [sem(f"yT_written{b}") for b in range(2)]
        y_high = [sem(f"y_high{b}") for b in range(2)]
        w_in, w_high, w_cut = sem("w_in"), sem("w_high"), sem("w_cut")
        w_used = sem("w_used")
        pad_zero = sem("pad_zero")
        res_in = [sem(f"res_in{b}") for b in range(3)]
        product = [sem(f"product{b}") for b in range(3)]
        evacuated = [sem(f"evacuated{b}") for b in range(3)]
        stored = [sem(f"stored{b}") for b in range(3)]
        n_loads = 1 if kind == "norm" else len(gates)

        def buffer_of(w_, i):
            return w_[:, :, bass.ds(i % 2, 1), :].rearrange("p k a c -> p k (a c)")

        def load_w(e, i):
            e.dma_start(w_raw[:, :, :], w[:, bass.ds(i * chunk, chunk)].rearrange("(k p) c -> p k c", p=P)).then_inc(w_in, 16)

        with nc.Block() as block:
            @block.sync
            def _(sp):
                for b in range(3):
                    sp.sem_inc(stored[b], 16)
                if kind == "norm":
                    sp.dma_start(g[:, :], gain.partition_broadcast(P)).then_inc(gain_in, 16)

                def rows(a, t, n):
                    return a[0][t * P:t * P + n, :] if t < NT else a[1]

                for t, n in gemm_tiles():
                    b = t % 2
                    sp.wait_ge(rows_ready[b], t // 2 + 1)
                    sp.dma_start(x[0:n, b, :], rows(src, t, n)).then_inc(loaded[b], 16)
                    if kind == "gate":
                        at = 0
                        for c0, c1 in gates[1:]:
                            sp.dma_start(z[0:n, b, at:at + c1 - c0], rows(gates[0], t, n)[:, c0:c1]).then_inc(loaded[b], 16)
                            at += c1 - c0

                def store(i, t, n):
                    k = i * 3 + t // 3
                    sp.wait_ge(evacuated[t % 3], k + 2)
                    to = dst[0][t * P:t * P + n, :] if t < NT else dst[1]
                    sp.dma_start(to[:, bass.ds(i * chunk, chunk)], outb[0:n, t % 3, :]).then_inc(stored[t % 3], 16)

                with sp.Fori(0, n_chunks - 1) as i:
                    sp.wait_ge(w_cut, i + 1)
                    load_w(sp, i + 1)
                    for t, n in gemm_tiles():
                        store(i, t, n)
                for t, n in gemm_tiles():
                    store(n_chunks - 1, t, n)
                for b in range(3):
                    sp.wait_ge(stored[b], 16 * (3 * n_chunks + 1))

            @block.scalar
            def _(act):
                def stats(t, n):
                    u, b = t // 2, t % 2
                    if kind == "gate":
                        act.wait_ge(loaded[b], (u + 1) * (16 * (len(gates))))
                        nc.scalar.activation(z[0:n, b, :], z[0:n, b, :], ACT.Silu).then_inc(squares[b], 1)
                    else:
                        act.wait_ge(loaded[b], (u + 1) * 16)
                        nc.scalar.activation(z[0:n, b, :], x[0:n, b, :], ACT.Square,
                                             accum_out=stat[0:n, b, 0:1]).then_inc(squares[b], 1)
                        act.wait_ge(means[b], u + 1)
                        nc.scalar.activation(stat[0:n, b, 2:3], stat[0:n, b, 1:2], ACT.Sqrt).then_inc(roots[b], 1)

                def evacuate(t, n):
                    b = t % 2
                    act.wait_ge(turned[b], t // 2 + 2)
                    nc.scalar.copy(y_hi[:, :, t * P:t * P + n], tps[b][:, :, 0:n]).then_inc(y_high[b], 1)

                def w_high_part(i):
                    act.wait_ge(w_in, (i + 1) * 16)
                    act.wait_ge(w_used, i + 1)
                    nc.scalar.copy(buffer_of(w_hi, i), w_raw[:, :, :]).then_inc(w_high, 1)

                def load_residual(i, t, n):
                    act.wait_ge(evacuated[t % 3], i * 3 + t // 3 + 1)
                    fr = residual[0][t * P:t * P + n, :] if t < NT else residual[1]
                    act.dma_start(res[0:n, t % 3, :], fr[:, bass.ds(i * chunk, chunk)]).then_inc(res_in[t % 3], 16)
                act.wait_ge(loaded[0], 16 * n_loads)
                load_w(act, 0)
                for b in range(2):
                    act.sem_inc(yT_written[b], 1)
                act.sem_inc(w_used, 1)
                tiles = gemm_tiles()
                for t, n in tiles:
                    stats(t, n)
                    if t:
                        evacuate(*tiles[t - 1])
                    if t == WEIGHT_AT:
                        w_high_part(0)
                    if residual is not None and t >= LAG:
                        load_residual(0, *tiles[t - LAG])
                evacuate(*tiles[NT])
                for t, n in tiles[NT + 1 - LAG:]:
                    if residual is not None:
                        load_residual(0, t, n)
                    if t == CUT_AFTER:
                        w_high_part(1)
                with act.Fori(1, n_chunks - 1) as i:
                    for t, n in tiles:
                        if residual is not None:
                            load_residual(i, t, n)
                        if t == CUT_AFTER:
                            w_high_part(i + 1)
                if residual is not None:
                    for t, n in gemm_tiles():
                        load_residual(n_chunks - 1, t, n)

            @block.vector
            def _(dve):
                if kind == "norm":
                    dve.wait_ge(gain_in, 16)

                def rows_of(t, n):
                    u, b = t // 2, t % 2
                    if kind == "gate":
                        dve.wait_ge(squares[b], u + 1)
                        dve.wait_ge(loaded[b], (u + 1) * (16 * (len(gates))))
                        dve.wait_ge(turned[b], u + 1)
                        nc.vector.tensor_tensor(y[0:n, b, :], x[0:n, b, :], z[0:n, b, :], ALU.mult).then_inc(rows_ready[b], 1)
                        return
                    dve.wait_ge(squares[b], u + 1)
                    nc.vector.tensor_scalar(stat[0:n, b, 1:2], stat[0:n, b, 0:1], 1.0 / D, EPS_RMS, ALU.mult, ALU.add).then_inc(means[b], 1)
                    dve.wait_ge(roots[b], u + 1)
                    nc.vector.reciprocal(stat[0:n, b, 3:4], stat[0:n, b, 2:3]).then_inc(inverses[b], 1)
                    dve.wait_ge(inverses[b], u + 1)
                    dve.wait_ge(turned[b], u + 1)
                    nc.vector.scalar_tensor_tensor(out=y[0:n, b, :], in0=x[0:n, b, :], scalar=stat[0:n, b, 3:4],
                                                   in1=g[0:n, :], op0=ALU.mult, op1=ALU.mult).then_inc(rows_ready[b], 1)
                for b in range(2):
                    dve.sem_inc(rows_ready[b], 1)
                for b in range(3):
                    dve.sem_inc(evacuated[b], 1)
                nc.vector.memset(y[:, 0, 0:KD * (P - NS)], 0.0).then_inc(pad_zero, 1)
                dve.wait_ge(pad_zero, 1)
                zeros = y[:, 0, 0:KD * (P - NS)].rearrange("p (k c) -> p k c", k=KD)
                nc.vector.tensor_copy(y_hi[:, :, ROWS:], zeros)
                nc.vector.tensor_copy(y_lo[:, :, ROWS:], zeros).then_inc(pad_zero, 1)
                dve.wait_ge(pad_zero, 2)

                def y_low_part(t, n):
                    b, col = t % 2, slice(t * P, t * P + n)
                    dve.wait_ge(y_high[b], t // 2 + 1)
                    nc.vector.tensor_tensor(y_lo[:, :, col], tps[b][:, :, 0:n], y_hi[:, :, col].bitcast(F32),
                                            ALU.subtract).then_inc(yT_written[b], 1)

                def w_low_part(i):
                    dve.wait_ge(w_high, i + 1)
                    nc.vector.tensor_tensor(buffer_of(w_lo, i), w_raw[:, :, :], buffer_of(w_hi, i).bitcast(F32),
                                            ALU.subtract).then_inc(w_cut, 1)

                def take_product(i, t, n):
                    k = i * 3 + t // 3
                    dve.wait_ge(product[t % 3], k + 1)
                    dve.wait_ge(stored[t % 3], (k + 1) * 16)
                    if residual is None:
                        nc.vector.tensor_copy(outb[0:n, t % 3, :], acc[t % 3][0:n, 0:chunk]).then_inc(evacuated[t % 3], 1)
                    else:
                        dve.wait_ge(res_in[t % 3], (k + 1) * 16)
                        nc.vector.tensor_tensor(outb[0:n, t % 3, :], acc[t % 3][0:n, 0:chunk], res[0:n, t % 3, :],
                                                ALU.add).then_inc(evacuated[t % 3], 1)
                tiles = gemm_tiles()
                for t, n in tiles:
                    rows_of(t, n)
                    if t:
                        y_low_part(*tiles[t - 1])
                    if t == WEIGHT_AT:
                        w_low_part(0)
                    if t > LAG:
                        take_product(0, *tiles[t - LAG - 1])
                y_low_part(*tiles[NT])
                for t, n in tiles[NT - LAG:]:
                    take_product(0, t, n)
                    if t == CUT_AFTER:
                        w_low_part(1)
                with dve.Fori(1, n_chunks - 1) as i:
                    for t, n in tiles:
                        take_product(i, t, n)
                        if t == CUT_AFTER:
                            w_low_part(i + 1)
                for t, n in gemm_tiles():
                    take_product(n_chunks - 1, t, n)

            @block.tensor
            def _(pe):
                for b in range(2):
                    pe.sem_inc(turned[b], 1)

                def turn(t, n):
                    u, b = t // 2, t % 2
                    pe.wait_ge(rows_ready[b], u + 2)
                    pe.wait_ge(yT_written[b], u + 1)
                    for k in range(KD):
                        last = nc.tensor.transpose(tps[b][:, k, 0:n], y[0:n, b, k * P:(k + 1) * P], ident[0:n, 0:n])
                    last.then_inc(turned[b], 1)

                def products(i, t, n):
                    pe.wait_ge(evacuated[t % 3], i * 3 + t // 3 + 1)
                    for k in range(KD):
                        for x, (rows, cols) in enumerate(((y_lo, w_hi), (y_hi, w_lo), (y_hi, w_hi))):
                            last = nc.tensor.matmul(acc[t % 3][:, 0:chunk], rows[:, k, t * P:(t + 1) * P],
                                                    cols[:, k, bass.ds(i % 2, 1), :].rearrange("p a c -> p (a c)"),
                                                    start=(k == 0 and x == 0), stop=(k == KD - 1 and x == 2))
                            if t == 1 and k == 0 and x == 0:
                                last.then_inc(w_used, 1)
                    last.then_inc(product[t % 3], 1)

                tiles = gemm_tiles()
                for t, n in tiles:
                    turn(t, n)
                    if t == LAG:
                        pe.wait_ge(w_cut, 1)
                        pe.wait_ge(pad_zero, 2)
                    if t >= LAG:
                        pe.wait_ge(yT_written[(t - LAG) % 2], (t - LAG) // 2 + 2)
                        products(0, *tiles[t - LAG])
                for t, n in tiles[NT + 1 - LAG:]:
                    pe.wait_ge(yT_written[t % 2], t // 2 + 2)
                    products(0, t, n)
                with pe.Fori(1, n_chunks) as i:
                    pe.wait_ge(w_cut, i + 1)
                    for t, n in tiles:
                        products(i, t, n)


def final_norm(nc, src, gain, dst):
    with Phase(nc) as ctx:
        x = ctx.enter_context(nc.sbuf_tensor("fn_x", [P, NT + 1, D], F32))
        sq = ctx.enter_context(nc.sbuf_tensor("fn_sq", [P, D], F32))
        g = ctx.enter_context(nc.sbuf_tensor("fn_g", [P, D], F32))
        stat = ctx.enter_context(nc.sbuf_tensor("fn_stat", [P, 4, NT + 1], F32))
        loaded = [ctx.semaphore(f"fn_loaded{t}") for t in range(NT + 1)]
        gain_in = ctx.semaphore("fn_gain_in")
        squares = ctx.semaphore("fn_squares")
        means = ctx.semaphore("fn_means")
        roots = ctx.semaphore("fn_roots")
        inverses = ctx.semaphore("fn_inverses")
        normed = ctx.semaphore("fn_normed")
        stored = ctx.semaphore("fn_stored")
        with nc.Block() as block:
            @block.sync
            def _(sp):
                sp.dma_start(g[:, :], gain.partition_broadcast(P)).then_inc(gain_in, 16)
                for t, n in gemm_tiles():
                    fr = src[0][t * P:t * P + n, :] if t < NT else src[1]
                    sp.dma_start(x[0:n, t, :], fr).then_inc(loaded[t], 16)
                for t, n in gemm_tiles():
                    sp.wait_ge(normed, t + 1)
                    to = dst[0][t * P:t * P + n, :] if t < NT else dst[1]
                    sp.dma_start(to, x[0:n, t, :]).then_inc(stored, 16)
                sp.wait_ge(stored, 16 * (NT + 1))

            @block.scalar
            def _(act):
                tiles = gemm_tiles()

                def root(t, n):
                    act.wait_ge(means, t + 1)
                    nc.scalar.activation(stat[0:n, 2, t:t + 1], stat[0:n, 1, t:t + 1], ACT.Sqrt).then_inc(roots, 1)
                for t, n in tiles:
                    act.wait_ge(loaded[t], 16)
                    if t:
                        act.wait_ge(squares, t)
                    nc.scalar.activation(sq[0:n, :], x[0:n, t, :], ACT.Square, accum_out=stat[0:n, 0, t:t + 1]).then_inc(squares, 1)
                    if t:
                        root(*tiles[t - 1])
                root(*tiles[NT])

            @block.vector
            def _(dve):
                tiles = gemm_tiles()

                def scale_rows(t, n):
                    dve.wait_ge(roots, t + 1)
                    nc.vector.reciprocal(stat[0:n, 3, t:t + 1], stat[0:n, 2, t:t + 1]).then_inc(inverses, 1)
                    dve.wait_ge(inverses, t + 1)
                    nc.vector.scalar_tensor_tensor(out=x[0:n, t, :], in0=x[0:n, t, :], scalar=stat[0:n, 3, t:t + 1],
                                                   in1=g[0:n, :], op0=ALU.mult, op1=ALU.mult).then_inc(normed, 1)
                dve.wait_ge(gain_in, 16)
                for t, n in tiles:
                    dve.wait_ge(squares, t + 1)
                    nc.vector.tensor_scalar(stat[0:n, 1, t:t + 1], stat[0:n, 0, t:t + 1], 1.0 / D, EPS_RMS, ALU.mult, ALU.add).then_inc(means, 1)
                    if t:
                        scale_rows(*tiles[t - 1])
                scale_rows(*tiles[NT])


def attend_prompt(nc, con, kind, h, mix, n_pairs, stores, kcmp=None, vcmp=None):
    sparse = kind == "sparse"
    NBR = 3 if sparse else 1
    n_rounds = n_pairs // 2
    with Phase(nc) as ctx:
        def sb(name, shape, dt=F32):
            return ctx.enter_context(nc.sbuf_tensor(f"{kind}_{name}", shape, dt))

        def sem(name):
            s = ctx.semaphore(f"{kind}_{name}")
            sems.append(s)
            return s
        sems = []
        q_in = sb("q_in", [P, NT, 2, 2, HD])
        k_in = sb("k_in", [P, NT, 2, 2, HD])
        q_ac = [sb(f"q_ac{b}", [P, 2, 2, T], BF16) for b in range(2)]
        k_abc = [sb(f"k_abc{b}", [P, 2, 3, T], BF16) for b in range(1 if sparse else 2)]
        rest = [sb(f"rest{b}", [P, 512]) for b in range(2)]
        v_sb = [sb(f"v{b}", [P, 2, NT, HD]) if sparse else sb(f"v{b}", [P, NT, P]) for b in range(1 if sparse else 2)]
        pr = [sb(f"pr{b}", [P, T]) for b in range(2)]
        prT = [sb(f"prT{b}", [P, 4 * P]) for b in range(4)]
        o_sb = [sb(f"o{b}", [P, NT, 2, HD]) for b in range(2)]
        nmax = sb("nmax", [P, 2, 2])
        lsum = sb("lsum", [P, 4, 2 * NBR])
        coef = sb("coef", [P, 2, 2 * NBR])
        part = sb("part", [P, 2 * NBR, HD])
        if sparse:
            k_all = sb("k_all", [P, 2, 2, 3, T], BF16)
            v_all = sb("v_all", [P, 2, NT, 2, HD])
            gl_in = sb("gl_in", [P, NT, 6])
            gate_e = sb("gate_e", [P, NT, 6])
            gate_den = [sb(f"gate_den{b}", [P, NT, 6]) for b in range(2)]
            kc_in = sb("kc_in", [P, 2, NCB])
            kc_rest = sb("kc_rest", [P, 2, NCB])
            kc_all = sb("kc_all", [P, 2, 3, NCB], BF16)
            kc = sb("kc", [P, 3, NCB], BF16)
            vc_all = sb("vc_all", [NCB, 2, HD])
            vc = sb("vc", [NCB, HD])
        ps_s = [ctx.enter_context(nc.psum_tensor(f"{kind}_ps_s{b}", [P, T], F32)) for b in range(2)]
        ps_t = [ctx.enter_context(nc.psum_tensor(f"{kind}_ps_t{b}", [P, 4 * P], F32)) for b in range(2)]
        ps_o = [ctx.enter_context(nc.psum_tensor(f"{kind}_ps_o{b}", [P, 512], F32)) for b in range(2)]
        q_loaded = [sem("q_loaded_first"), sem("q_loaded_second")]
        loaded = [sem("loaded_first"), sem("loaded_second")]
        k_loaded = [sem("k_loaded_sel"), sem("k_loaded_win")]
        copied_act, copied_dve, copied_pool = sem("copied_act"), sem("copied_dve"), sem("copied_pool")
        cut_first, cut_copied, cut_second, cut_done = sem("cut_first"), sem("cut_copied"), sem("cut_second"), sem("cut_done")
        gate_exp, gate_ready = sem("gate_exp"), sem("gate_ready")
        scores_ready, max_ready, probs_ready = sem("scores_ready"), sem("max_ready"), sem("probs_ready")
        turned = sem("turned")
        bank_free = [sem("bank_free0"), sem("bank_free1")]
        group_used, out_ready, stored, dve_step = sem("group_used"), sem("out_ready"), sem("stored"), sem("dve_step")
        kc_step, vc_loaded, rows_stored = sem("kc_step"), sem("vc_loaded"), sem("rows_stored")
        hp = h[0].rearrange("(t p) c -> p t c", p=P)

        def load_pair(sp, i, b, x):
            q0 = QC if sparse else QA
            rows = []
            for e in range(2):
                for dup in range(2):
                    sp.dma_start(q_in[:, :, e, dup, :], hp[:, :, bass.ds(i * P + (q0 + e * HD), HD)]).then_inc(q_loaded[x], 16)
                    if not sparse:
                        rows.append((k_in[:, :, e, dup, :], hp[:, :, bass.ds(i * P + (KA + e * HD), HD)]))
            if sparse:
                rows.append((gl_in[:, :, :], hp[:, :, bass.ds(i * 6 + GL, 6)]))
            else:
                rows.append((v_sb[b][:, :, :], hp[:, :, bass.ds(i * P + VA, P)]))
            for out, in_ in rows:
                sp.dma_start(out, in_).then_inc(loaded[x], 16)

        Q_LOADS, N_LOADS = 4, 1 if sparse else 5

        jobs = []
        for b in range(2):
            for t in range(NT):
                for e in range(2):
                    if sparse:
                        jobs.append((b, t, e, 1, list(range(t + 1))))
                        jobs.append((b, t, e, 2, list(range(max(0, t - 4), t + 1))))
                    else:
                        jobs.append((b, t, e, 0, list(range(t + 1))))
                if sparse:
                    jobs.append((b, t, None, 0, None))
        width = [2 * 64 if blocks is None else P * len(blocks) for *_, blocks in jobs]
        groups = []
        of_job = []
        for n, w in enumerate(width):
            of_job.append([])
            for c0 in range(0, w, 4 * P):
                of_job[n].append(len(groups))
                groups.append((n, c0, min(4 * P, w - c0)))
        last_group = {(j[0] * NT + j[1]): of_job[n][-1] for n, j in enumerate(jobs)}
        last_of_pair = [max(g for t, g in last_group.items() if t < NT), len(groups) - 1]

        by_act, busy_act, busy_dve = [], 0.0, 0.0
        for n, w in enumerate(width):
            busy_act += (2 if jobs[n][4] is None else 1) * 250 + w * 1.04
            busy_dve += 150 + w * 1.04 + (900 / (5 if sparse else 2))
            for g in of_job[n]:
                by_act.append(busy_act < busy_dve)
                if by_act[-1]:
                    busy_act += 200 + groups[g][2] * 0.9
                else:
                    busy_dve += 120 + groups[g][2] * 1.04

        units = [("q", e, x) for e in range(2) for x in range(2)]
        if not sparse:
            units += [("k", e, x) for e in range(2) for x in range(2)]

        steps = [("scores", 0), ("max", 0), ("exp", 0), ("scores", 1), ("max", 1)]
        per_pair = len(jobs) // 2
        start = per_pair // 4
        every = (per_pair - start - 2) // len(units)
        for n in range(len(jobs)):
            if n + 1 < len(jobs):
                steps.append(("exp", n + 1))
            for g in of_job[n]:
                steps += [("turn", g), ("take", g)]
            if n + 2 < len(jobs):
                steps += [("scores", n + 2), ("max", n + 2)]
            if n:
                steps += [("times_v", g) for g in of_job[n - 1]]
            if n >= 2 and jobs[n - 2][:2] != jobs[n - 1][:2]:
                steps.append(("finish", jobs[n - 2][0] * NT + jobs[n - 2][1]))
            k = n % per_pair
            if k >= start and (k - start) % every == 0 and (k - start) // every < len(units):
                steps.append(("cut", (n // per_pair, (k - start) // every)))
        steps += [("times_v", g) for g in of_job[-1]] + [("finish", 2 * NT - 1)]
        place, order = {}, 0
        for what, x in steps:
            if what in ("turn", "cut"):
                place[what, x] = order
                order += 1

        def bank(what, x):
            return place[what, x] % 2, place[what, x] // 2

        def parts_of(unit, b):
            what, e, x = unit
            cols = slice(x * 512, x * 512 + 512)
            if what == "q":
                return q_ac[b][:, e, 0, cols], None, q_ac[b][:, e, 1, cols]
            k = k_abc[b] if not sparse else k_all[:, b]
            return k[:, e, 0, cols], k[:, e, 1, cols], k[:, e, 2, cols]

        def cut_act(act, unit, b, src, n_turned, c):
            act.wait_ge(turned, n_turned)
            nc.scalar.activation(parts_of(unit, b)[0], src, ACT.Copy, scale=-SCALE if unit[0] == "q" else 1.0).then_inc(cut_first, 1)

        lo, hi = slice(0, HD), slice(HD, P)

        def cut_dve(dve, unit, b, src, c, free):
            dve.wait_ge(cut_first, c + 1)
            if c >= 2:
                dve.wait_ge(cut_done, c - 1)
            first, _, third = parts_of(unit, b)
            nc.vector.scalar_tensor_tensor(out=rest[c % 2][:, :], in0=src, scalar=-SCALE if unit[0] == "q" else 1.0,
                                           in1=first, op0=ALU.mult, op1=ALU.subtract).then_inc(free, 1)
            half = lo if unit[0] == "q" else hi
            nc.vector.tensor_copy(third[half], first[half]).then_inc(cut_copied, 1)

        def cut_second_part(eng, copy, unit, b, c, free, n_free):
            eng.wait_ge(free, n_free)
            if unit[0] == "q":
                copy(parts_of(unit, b)[0][hi], rest[c % 2][hi, :]).then_inc(cut_second, 1)
            else:
                copy(parts_of(unit, b)[1], rest[c % 2][:, :]).then_inc(cut_second, 1)

        def cut_third_part(pool, unit, b, c):
            pool.wait_ge(cut_second, c + 1)
            pool.wait_ge(cut_copied, c + 1)
            first, second, third = parts_of(unit, b)
            half, second = (hi, first) if unit[0] == "q" else (lo, second)
            nc.gpsimd.tensor_tensor(third[half], rest[c % 2][half, :], second[half], ALU.subtract).then_inc(cut_done, 1)
            pool.wait_ge(cut_done, c + 1)

        def cut_pe(pe, unit, to, src=None):
            what, e, x = unit
            src = (q_in if what == "q" else k_in) if src is None else src
            for m in range(4):
                last = nc.tensor.transpose(to[:, m * P:(m + 1) * P], src[:, 4 * x + m, e, :, :].rearrange("p a d -> p (a d)"),
                                           con("ident"))
            last.then_inc(turned, 1)

        first_cuts = [(u, 0) for u in units]
        if sparse:
            first_cuts += [(("k", m, x), g) for m in range(2) for g in range(2) for x in range(2)]
        with nc.Block() as block:
            @block.sync
            def _(sp):
                load_pair(sp, 0, 0, 0)
                if sparse:
                    for half in range(2):
                        for g in range(2):
                            sp.dma_start(kc_in[half * HD:(half + 1) * HD, g, :], kcmp[g * HD:(g + 1) * HD, :]).then_inc(vc_loaded, 16)
                    sp.dma_start(vc_all[:, :, :].rearrange("c g d -> c (g d)"), vcmp).then_inc(vc_loaded, 16)
                    for m, (kcol, vcol) in enumerate(((KS, VS), (KW, VW))):
                        if m == 1:
                            sp.wait_ge(turned, len(units) + 4)
                        for g in range(2):
                            for dup in range(2):
                                sp.dma_start(k_in[:, :, g, dup, :], hp[:, :, kcol + g * HD:kcol + (g + 1) * HD]).then_inc(k_loaded[m], 16)
                        sp.dma_start(v_all[:, m, :, :, :].rearrange("p t g d -> p t (g d)"), hp[:, :, vcol:vcol + P]).then_inc(k_loaded[m], 16)
                    sp.wait_ge(k_loaded[0], 80)
                    sp.wait_ge(k_loaded[1], 80)
                    sp.wait_ge(vc_loaded, 80)
                sp.wait_ge(q_loaded[0], 16 * Q_LOADS)
                sp.wait_ge(loaded[0], 16 * N_LOADS)
                sp.wait_ge(rows_stored, 16 * len(stores))

            @block.tensor
            def _(pe):
                pe.wait_ge(q_loaded[0], 16 * Q_LOADS)
                for c, (unit, b) in enumerate(first_cuts):
                    if c == 4:
                        pe.wait_ge(loaded[0], 16 * N_LOADS)
                    if c >= 2:
                        pe.wait_ge(bank_free[c % 2], c // 2)
                    if c >= len(units):
                        pe.wait_ge(k_loaded[unit[1]], 80)
                        what, m, x = unit
                        cut_pe(pe, (what, b, x), ps_t[c % 2])
                    else:
                        cut_pe(pe, unit, ps_t[c % 2])

            @block.scalar
            def _(act):
                act.wait_ge(loaded[0], 16 * N_LOADS)
                for to, fr in stores:
                    act.dma_start(to, fr).then_inc(rows_stored, 16)
                if sparse:
                    nc.scalar.activation(gate_e[:, :, :], gl_in[:, :, :], ACT.Exp, scale=-1.0).then_inc(gate_exp, 1)
                    act.wait_ge(vc_loaded, 80)
                    nc.scalar.copy(kc_all[:, :, 0, :], kc_in[:, :, :]).then_inc(kc_step, 1)
                for c, (unit, b) in enumerate(first_cuts):
                    cut_act(act, unit, b, ps_t[c % 2][:, :], c + 1, c)
                    if c:
                        cut_second_part(act, nc.scalar.copy, *first_cuts[c - 1], c - 1, bank_free[(c - 1) % 2], (c - 1) // 2 + 1)
                c = len(first_cuts) - 1
                cut_second_part(act, nc.scalar.copy, *first_cuts[c], c, bank_free[c % 2], c // 2 + 1)

            @block.vector
            def _(dve):
                if sparse:
                    dve.wait_ge(gate_exp, 1)
                    nc.vector.tensor_scalar(gate_den[0][:, :, :], gate_e[:, :, :], 1.0, None, ALU.add).then_inc(gate_ready, 1)
                    dve.wait_ge(gate_ready, 1)
                    dve.wait_ge(kc_step, 1)
                    nc.vector.tensor_tensor(kc_rest[:, :, :], kc_in[:, :, :], kc_all[:, :, 0, :], ALU.subtract).then_inc(kc_step, 1)
                    dve.wait_ge(kc_step, 2)
                    nc.vector.tensor_copy(kc_all[HD:P, :, 2, :], kc_all[HD:P, :, 0, :])
                    nc.vector.tensor_copy(kc_all[:, :, 1, :], kc_rest[:, :, :]).then_inc(kc_step, 1)
                    dve.wait_ge(kc_step, 3)
                    nc.vector.tensor_tensor(kc_all[0:HD, :, 2, :], kc_rest[0:HD, :, :], kc_all[0:HD, :, 1, :], ALU.subtract).then_inc(kc_step, 1)
                    dve.wait_ge(kc_step, 4)
                for c, (unit, b) in enumerate(first_cuts):
                    cut_dve(dve, unit, b, ps_t[c % 2][:, :], c, bank_free[c % 2])

            @block.gpsimd
            def _(pool):
                for c, (unit, b) in enumerate(first_cuts):
                    cut_third_part(pool, unit, b, c)
        next_round(nc, sems)

        with nc.Fori(0, n_rounds) as i:
            with nc.Block() as block:
                group_of_round = i // 2 if sparse else 0

                @block.sync
                def _(sp):
                    load_pair(sp, i * 2 + 1, 1, 0)
                    for tt in range(2 * NT):
                        if tt == NT:
                            sp.wait_ge(turned, place["cut", (0, len(units) - 1)] + 1)
                            sp.wait_ge(group_used, last_of_pair[0] + 1)
                            if sparse:
                                sp.wait_ge(gate_exp, 1)
                            load_pair(sp, (i * 2 + 2) % n_pairs, 0, 1)
                        sp.wait_ge(out_ready, tt + 1)
                        b, t = divmod(tt, NT)
                        sp.dma_start(mix[t * P:(t + 1) * P, bass.ds((i * 2 + b) * P, P)],
                                     o_sb[b][:, t, :, :].rearrange("p e d -> p (e d)")).then_inc(stored, 16)
                    for x in range(2):
                        sp.wait_ge(q_loaded[x], 16 * Q_LOADS)
                        sp.wait_ge(loaded[x], 16 * N_LOADS)
                    sp.wait_ge(stored, 16 * 2 * NT)

                def cut_of(x):
                    b, u = x
                    return units[u], 1 - b, b * len(units) + u

                @block.gpsimd
                def _(pool):
                    if sparse:
                        nc.gpsimd.tensor_copy(kc[:, :, :], kc_all[:, bass.ds(group_of_round, 1), :, :].rearrange("p g x c -> p (g x) c"))
                        nc.gpsimd.tensor_copy(vc[:, :], vc_all[:, bass.ds(group_of_round, 1), :].rearrange("p g d -> p (g d)")).then_inc(copied_pool, 1)
                    for what, x in steps:
                        if what == "cut":
                            unit, b, c = cut_of(x)
                            nb, nu = bank(what, x)
                            cut_second_part(pool, nc.gpsimd.tensor_copy, unit, b, c, bank_free[nb], nu + 1)
                            cut_third_part(pool, unit, b, c)

                def take(eng, copy, g):
                    n, _, w = groups[g]
                    nb, nu = bank("turn", g)
                    eng.wait_ge(turned, place["turn", g] + 1)
                    if g >= 4:
                        eng.wait_ge(group_used, g - 3)
                    rows = NCB if jobs[n][4] is None else P
                    w = 2 * P if jobs[n][4] is None else w
                    copy(prT[g % 4][0:rows, 0:w], ps_t[nb][0:rows, 0:w]).then_inc(bank_free[nb], 1)

                @block.scalar
                def _(act):
                    if sparse:
                        nc.scalar.copy(v_sb[0][:, 0, :, :], v_all[:, 0, :, bass.ds(group_of_round, 1), :].rearrange("p t g d -> p t (g d)"))
                        nc.scalar.copy(v_sb[0][:, 1, :, :], v_all[:, 1, :, bass.ds(group_of_round, 1), :].rearrange("p t g d -> p t (g d)")).then_inc(copied_act, 1)
                    for what, x in steps:
                        if what == "exp":
                            n = x
                            b, t, e, br, blocks = jobs[n]
                            tt = b * NT + t
                            act.wait_ge(max_ready, n + 1)
                            if n >= 2:
                                act.wait_ge(turned, place["turn", of_job[n - 2][-1]] + 1)
                            if tt >= 4:
                                act.wait_ge(out_ready, tt - 3)
                            if blocks is None:
                                for e in range(2):
                                    last = nc.scalar.activation(pr[n % 2][:, e * 64:e * 64 + NCB], ps_s[n % 2][:, e * 64:e * 64 + NCB], ACT.Exp,
                                                                scale=-1.0, bias=nmax[:, n % 2, e:e + 1],
                                                                accum_out=lsum[:, tt % 4, e * 3:e * 3 + 1])
                                last.then_inc(probs_ready, 1)
                            else:
                                src = ps_s[n % 2] if sparse else pr[n % 2]
                                nc.scalar.activation(pr[n % 2][:, 0:width[n]], src[:, 0:width[n]], ACT.Exp, scale=-1.0,
                                                     bias=nmax[:, n % 2, 0:1],
                                                     accum_out=lsum[:, tt % 4, e * NBR + br:e * NBR + br + 1]).then_inc(probs_ready, 1)
                        elif what == "take" and by_act[x]:
                            take(act, nc.scalar.copy, x)
                        elif what == "cut":
                            unit, b, c = cut_of(x)
                            cut_act(act, unit, b, ps_t[bank(what, x)[0]][:, :], place[what, x] + 1, c)
                            if sparse and x[1] == 0:
                                act.wait_ge(loaded[x[0]], 16 * N_LOADS)
                                if x[0] == 1:
                                    act.wait_ge(gate_ready, 1)
                                nc.scalar.activation(gate_e[:, :, :], gl_in[:, :, :], ACT.Exp, scale=-1.0).then_inc(gate_exp, 1)

                @block.vector
                def _(dve):
                    count = 0

                    def link(ins):
                        nonlocal count
                        count += 1
                        ins.then_inc(dve_step, 1)
                        dve.wait_ge(dve_step, count)

                    def maximum(n):
                        b, t, e, br, blocks = jobs[n]
                        dve.wait_ge(scores_ready, n + 1)
                        if n >= 2:
                            dve.wait_ge(probs_ready, n - 1)
                        s = ps_s[n % 2]
                        if blocks is None:
                            nc.vector.tensor_reduce(nmax[:, n % 2, :], s[:, 0:128].rearrange("p (e c) -> p e c", e=2)[:, :, 0:NCB], AX,
                                                    ALU.min).then_inc(max_ready, 1)
                        elif sparse:
                            nc.vector.tensor_reduce(nmax[:, n % 2, 0:1], s[:, 0:width[n]], AX, ALU.min).then_inc(max_ready, 1)
                        else:
                            if n >= 2:
                                dve.wait_ge(turned, place["turn", of_job[n - 2][-1]] + 1)
                            nc.vector.tensor_tensor_reduce(
                                out=pr[n % 2][:, 0:width[n]], in0=s[:, 0:width[n]],
                                in1=con("abias")[:, (NT - 1 - t) * P:], scale=1.0, scalar=3e38, op0=ALU.add, op1=ALU.min,
                                accum_out=nmax[:, n % 2, 0:1]).then_inc(max_ready, 1)

                    def finish(tt):
                        b, t = divmod(tt, NT)
                        dve.wait_ge(group_used, last_group[tt] + 1)
                        l, c = lsum[:, tt % 4, :], coef[:, tt % 2, :]
                        o = ps_o[tt % 2][:, 0:2 * NBR * HD].rearrange("p (s d) -> p s d", d=HD)
                        if sparse:
                            link(nc.vector.tensor_tensor(c, l, gate_den[b][:, t, :], ALU.mult))
                            link(nc.vector.reciprocal(c, c))
                            if t == 0:
                                cc = c.rearrange("p (e b) -> p e b", b=3)[:, :, 0]
                                link(nc.vector.tensor_scalar(cc, cc, con("valid"), None, ALU.mult))
                            link(nc.vector.tensor_tensor(part[:, :, :], o, c.unsqueeze(2).broadcast_to([P, 6, HD]), ALU.mult))
                            nc.vector.tensor_reduce(o_sb[b][:, t, :, :], part[:, :, :].rearrange("p (e b) d -> p e d b", b=3),
                                                    AX, ALU.add).then_inc(out_ready, 1)
                            dve.wait_ge(out_ready, tt + 1)
                        else:
                            link(nc.vector.reciprocal(c, l))
                            nc.vector.tensor_tensor(o_sb[b][:, t, :, :], o, c.unsqueeze(2).broadcast_to([P, 2, HD]),
                                                    ALU.mult).then_inc(out_ready, 1)
                    if sparse:
                        nc.vector.tensor_copy(k_abc[0][:, :, :, :], k_all[:, bass.ds(group_of_round, 1), :, :, :].rearrange(
                            "p g m x t -> p (g m) x t")).then_inc(copied_dve, 1)
                    for what, x in steps:
                        if what == "max":
                            maximum(x)
                        elif what == "take" and not by_act[x]:
                            take(dve, nc.vector.tensor_copy, x)
                        elif what == "finish":
                            finish(x)
                        elif what == "cut":
                            unit, b, c = cut_of(x)
                            cut_dve(dve, unit, b, ps_t[bank(what, x)[0]][:, :], c, bank_free[bank(what, x)[0]])
                            if sparse and x[1] == len(units) - 1:
                                dve.wait_ge(gate_exp, x[0] + 1)
                                nc.vector.tensor_scalar(gate_den[1 - x[0]][:, :, :], gate_e[:, :, :], 1.0, None, ALU.add).then_inc(gate_ready, 1)
                                dve.wait_ge(gate_ready, x[0] + 1)

                @block.tensor
                def _(pe):
                    if sparse:
                        pe.wait_ge(copied_dve, 1)
                        pe.wait_ge(copied_pool, 1)
                        pe.wait_ge(copied_act, 1)

                    def products(out, b, e, t, k3, first, last_):
                        for x in range(3):
                            q = q_ac[b][:, e, 1 if x == 2 else 0, t * P:(t + 1) * P]
                            ins = nc.tensor.matmul(out, q, k3(x), start=first and x == 0, stop=last_ and x == 2)
                        return ins

                    def scores(n):
                        b, t, e, br, blocks = jobs[n]
                        if n >= 2:
                            pe.wait_ge(probs_ready if sparse else max_ready, n - 1)
                        if n == per_pair:
                            pe.wait_ge(cut_done, len(units))
                            pe.wait_ge(loaded[0], 16 * N_LOADS)
                        s = ps_s[n % 2]
                        if blocks is None:
                            for e in range(2):
                                out = s[:, e * 64:e * 64 + NCB]
                                products(out, b, e, t, lambda x: kc[:, x, :], True, False)
                                last = nc.tensor.matmul(out, con.ident16, con.cmask16[:, t, :], start=False, stop=True)
                            last.then_inc(scores_ready, 1)
                            return
                        kb, ki = (k_abc[0], br - 1) if sparse else (k_abc[b], e)
                        for c0 in range(0, width[n], 512):
                            c1 = min(c0 + 512, width[n])
                            at = blocks[0] * P
                            masks = []
                            if sparse:
                                if width[n] - P >= c0 and width[n] <= c1:
                                    masks.append((width[n] - P, con.causal16))
                                if br == 2 and t >= 4 and c0 == 0:
                                    masks.append((0, con.edge16))
                            last = products(s[:, c0:c1], b, e, t, lambda x: kb[:, ki, x, at + c0:at + c1], True, not masks)
                            for x, (m0, mask) in enumerate(masks):
                                last = nc.tensor.matmul(s[:, m0:m0 + P], con.ident16, mask, start=False, stop=x == len(masks) - 1)
                        last.then_inc(scores_ready, 1)

                    def turn(g):
                        n, c0, w = groups[g]
                        if g == of_job[n][0]:
                            pe.wait_ge(probs_ready, n + 1)
                        to = enter("turn", g)
                        if jobs[n][4] is None:
                            for e in range(2):
                                last = nc.tensor.transpose(to[0:NCB, e * P:(e + 1) * P], pr[n % 2][:, e * 64:e * 64 + NCB], con("ident"))
                        else:
                            for c in range(0, w, P):
                                last = nc.tensor.transpose(to[:, c:c + P], pr[n % 2][:, c0 + c:c0 + c + P], con("ident"))
                        last.then_inc(turned, 1)

                    def enter(what, x):
                        nb, nu = bank(what, x)
                        if nu:
                            pe.wait_ge(bank_free[nb], nu)
                        return ps_t[nb]

                    def times_v(g):
                        n, c0, w = groups[g]
                        b, t, e, br, blocks = jobs[n]
                        tt = b * NT + t
                        nb, nu = bank("turn", g)
                        pe.wait_ge(bank_free[nb], nu + 1)
                        if tt >= 2 and (n == 0 or jobs[n - 1][:2] != jobs[n][:2]) and g == of_job[n][0]:
                            pe.wait_ge(out_ready, tt - 1)
                        if blocks is None:
                            for e in range(2):
                                last = nc.tensor.matmul(ps_o[tt % 2][:, e * 3 * HD:(e * 3 + 1) * HD], prT[g % 4][0:NCB, e * P:(e + 1) * P],
                                                        vc[:, :], start=True, stop=True)
                            last.then_inc(group_used, 1)
                            return
                        slot = (e * NBR + br) * HD
                        for c in range(0, w, P):
                            kb = blocks[(c0 + c) // P]
                            rhs = v_sb[0][:, br - 1, kb, :] if sparse else v_sb[b][:, kb, e * HD:(e + 1) * HD]
                            last = nc.tensor.matmul(ps_o[tt % 2][:, slot:slot + HD], prT[g % 4][:, c:c + P], rhs,
                                                    start=c0 + c == 0, stop=c0 + c + P >= width[n])
                        last.then_inc(group_used, 1)
                    for what, x in steps:
                        if what == "scores":
                            scores(x)
                        elif what == "turn":
                            turn(x)
                        elif what == "times_v":
                            times_v(x)
                        elif what == "cut":
                            if units[x[1]][0] == "q":
                                pe.wait_ge(q_loaded[x[0]], 16 * Q_LOADS)
                            else:
                                pe.wait_ge(loaded[x[0]], 16 * N_LOADS)
                            cut_pe(pe, units[x[1]], enter(what, x))
            next_round(nc, sems)


def retain(nc, con, h, mix, trig, state_out, state_in=None):
    sample = state_in is not None
    name = "ret_s" if sample else "ret"
    R = NS if sample else P
    n_rounds = 1 if sample else NT
    with Phase(nc) as ctx:
        def sb(nm, shape, dt=F32):
            return ctx.enter_context(nc.sbuf_tensor(f"{name}_{nm}", shape, dt))

        def sem(nm):
            s = ctx.semaphore(f"{name}_{nm}")
            sems.append(s)
            return s
        sems = []
        x = sb("x", [R, D])
        cs = sb("cs", [R, 2, 32])
        qk = sb("qk", [R, 8, 2, 32])
        m1 = sb("m1", [R, 8, 32])
        m2 = sb("m2", [R, 8, 32])
        qd = sb("qd", [R, BH, 2 if sample else 1, HD])
        kd = sb("kd", [R, BH, HD])
        kdm = sb("kdm", [NS, BH, NB, HD]) if sample else None
        n_t = 8 if sample else 6
        xT = sb("xT", [P, n_t, R])
        qdm = sb("qdm", [P, BH, NB // 2, NS]) if sample else None
        a = sb("a", [R, BH, R])
        st = sb("st", [P, NB // 2, BH, BDV]) if sample else sb("st", [P, 2, BDV])
        o = sb("o", [R, BH, BDV])
        sq = sb("sq", [R, BH, BDV])
        mean = sb("mean", [R, 4, BH])
        o_raw = None if sample else sb("o_raw", [R, BH, BDV])
        ps_t = ctx.enter_context(nc.psum_tensor(f"{name}_ps_t", [P, n_t, R], F32))
        ps_a = ctx.enter_context(nc.psum_tensor(f"{name}_ps_a", [P, 2, 512], F32))
        o_banks = 1 if sample else 2
        ps_o = ctx.enter_context(nc.psum_tensor(f"{name}_ps_o", [P, o_banks, 512], F32))
        ps_u = ctx.enter_context(nc.psum_tensor(f"{name}_ps_u", [P, 4 if sample else 1, 512], F32))

        def heads(ap, n, per):
            return ap[:, 0:per, 0:4 // per * n].rearrange("p e (m v) -> p m e v", v=n)
        first_load = ctx.semaphore(f"{name}_first_load")
        zeroed = ctx.semaphore(f"{name}_zeroed")
        v_moved = ctx.semaphore(f"{name}_v_moved")
        v_there, raw_used = sem("v_there"), sem("raw_used")
        loaded, rotated, decayed, turned, xT_ready, masked, a_raw, a_ready = (
            sem(n) for n in "loaded rotated decayed turned xT_ready masked a_raw a_ready".split())
        update_ready, o_acc, state_new, var_ready, root_ready, out_ready, stored, dve_step = (
            sem(n) for n in "update_ready o_acc state_new var_ready root_ready out_ready stored dve_step".split())

        def load(sp, i, s):
            if sample:
                sp.dma_start(x[:, :], h[1][:, QB:QB + D]).then_inc(s, 16)
                sp.dma_start(cs[:, :, :], trig[NT, 0:NS]).then_inc(s, 16)
                for e in range(2):
                    for m in range(NB // 2):
                        sp.dma_start(st[e * HD:(e + 1) * HD, m, :, :],
                                     state_in[2 * m + e].rearrange("h k v -> k h v")).then_inc(s, 16)
                return 2 + NB
            sp.dma_start(x[:, 0:512], h[0][bass.ds(i * P, P), QB:QB + 512]).then_inc(s, 16)
            sp.dma_start(cs[:, :, :].rearrange("p a f -> p (a f)"),
                         trig[bass.ds(i, 1)].rearrange("t p a f -> p (t a f)")).then_inc(s, 16)
            return 2

        def load_v(sp, i):
            sp.dma_start(x[:, 512:D], h[0][bass.ds(i * P, P), QB + 512:QB + D]).then_inc(v_moved, 16)

        with nc.Block() as block:
            @block.sync
            def _(sp):
                n = load(sp, 0, first_load)
                if not sample:
                    load_v(sp, 0)
                    sp.sem_inc(v_moved, 16)
                sp.wait_ge(first_load, 16 * n)

            if not sample:
                @block.vector
                def _(dve):
                    nc.vector.memset(o_raw[:, :, :], 0.0)
                    nc.vector.memset(st[:, :, :], 0.0).then_inc(zeroed, 1)
                    dve.wait_ge(zeroed, 1)

        def store_chunk(sp, i):
            sp.dma_start(mix[bass.ds(i * P, P), 512:D], o[:, :, :].rearrange("p h e -> p (h e)")).then_inc(v_moved, 16)

        def norm_means(link, raw):
            link(nc.vector.tensor_reduce(mean[:, 0, :], raw, AX, ALU.add))
            link(nc.vector.tensor_scalar(mean[:, 0, :], mean[:, 0, :], 1.0 / BDV, None, ALU.mult))

        def norm_rest(link, dve, raw):
            nc.vector.tensor_tensor(o[:, :, :], raw, mean[:, 0, :].unsqueeze(2).broadcast_to([R, BH, BDV]),
                                    ALU.subtract).then_inc(raw_used, 1)
            dve.wait_ge(raw_used, 1)
            link(nc.vector.tensor_tensor(sq[:, :, :], o[:, :, :], o[:, :, :], ALU.mult))
            link(nc.vector.tensor_reduce(mean[:, 1, :], sq[:, :, :], AX, ALU.add))
            nc.vector.tensor_scalar(mean[:, 1, :], mean[:, 1, :], 1.0 / BDV, EPS_GN, ALU.mult, ALU.add).then_inc(var_ready, 1)
            dve.wait_ge(root_ready, 1)
            link(nc.vector.reciprocal(mean[:, 3, :], mean[:, 2, :]))
            nc.vector.tensor_tensor(o[:, :, :], o[:, :, :], mean[:, 3, :].unsqueeze(2).broadcast_to([R, BH, BDV]),
                                    ALU.mult).then_inc(out_ready, 1)

        def norm_root(act):
            act.wait_ge(var_ready, 1)
            nc.scalar.activation(mean[:, 2, :], mean[:, 1, :], ACT.Sqrt).then_inc(root_ready, 1)

        def round_(i):
            with nc.Block() as block:
                @block.sync
                def _(sp):
                    if sample:
                        sp.wait_ge(out_ready, 1)
                        sp.dma_start(mix[T:ROWS, 512:D], o[:, :, :].rearrange("p h e -> p (h e)")).then_inc(stored, 16)
                        sp.wait_ge(stored, 16)
                    else:
                        sp.wait_ge(v_moved, (i + 1) * 32)
                        sp.sem_inc(v_there, 1)
                        sp.wait_ge(rotated, 1)
                        load(sp, (i + 1) % n_rounds, loaded)
                        sp.wait_ge(out_ready, 1)
                        store_chunk(sp, (i + n_rounds - 1) % n_rounds)
                        sp.wait_ge(update_ready, 1)
                        load_v(sp, (i + 1) % n_rounds)
                        sp.wait_ge(loaded, 32)

                @block.vector
                def _(dve):
                    steps = 0

                    def link(ins):
                        nonlocal steps
                        steps += 1
                        ins.then_inc(dve_step, 1)
                        dve.wait_ge(dve_step, steps)
                    v4 = x[:, 0:512].rearrange("p (h a f) -> p h a f", h=8, a=2)
                    x1, x2 = v4[:, :, 0, :], v4[:, :, 1, :]
                    cos = cs[:, 0, :].unsqueeze(1).broadcast_to([R, 8, 32])
                    sin = cs[:, 1, :].unsqueeze(1).broadcast_to([R, 8, 32])
                    nc.vector.tensor_tensor(m1[:, :, :], x1, cos, ALU.mult)
                    link(nc.vector.tensor_tensor(m2[:, :, :], x2, sin, ALU.mult))
                    link(nc.vector.tensor_tensor(qk[:, :, 0, :], m1[:, :, :], m2[:, :, :], ALU.subtract))
                    nc.vector.tensor_tensor(m1[:, :, :], x1, sin, ALU.mult)
                    link(nc.vector.tensor_tensor(m2[:, :, :], x2, cos, ALU.mult))
                    nc.vector.tensor_tensor(qk[:, :, 1, :], m1[:, :, :], m2[:, :, :], ALU.add).then_inc(rotated, 1)
                    dve.wait_ge(rotated, 1)
                    flat = qk[:, :, :, :].rearrange("p h a f -> p h (a f)")
                    qdec = con("qdec_s" if sample else "qdec").unsqueeze(2).broadcast_to([R, BH, HD])
                    kdec = con("kdec_s" if sample else "kdec").unsqueeze(2).broadcast_to([R, BH, HD])
                    nc.vector.tensor_tensor(qd[:, :, 0, :], flat[:, 0:4, :], qdec, ALU.mult)
                    if sample:
                        nc.vector.tensor_tensor(qd[:, :, 1, :], flat[:, 0:4, :], qdec, ALU.mult)
                    nc.vector.tensor_tensor(kd[:, :, :], flat[:, 4:8, :], kdec, ALU.mult).then_inc(decayed, 1)
                    if sample:
                        dve.wait_ge(decayed, 1)
                        for hh in range(BH):
                            last = nc.vector.tensor_tensor(kdm[:, hh, :, :], kd[:, hh, :].unsqueeze(1).broadcast_to([NS, NB, HD]),
                                                           con("kmask_s").unsqueeze(2).broadcast_to([NS, NB, HD]), ALU.mult)
                        last.then_inc(decayed, 1)
                    if not sample:
                        norm_means(link, o_raw[:, :, :])
                    dve.wait_ge(turned, 1)
                    nc.vector.tensor_copy(xT[:, :, :], ps_t[:, 0:n_t, 0:R]).then_inc(xT_ready, 1)
                    if sample:
                        dve.wait_ge(xT_ready, 1)
                        for hh in range(BH):
                            last = nc.vector.tensor_tensor(qdm[:, hh, :, :], xT[:, 4 + hh, :].unsqueeze(1).broadcast_to([P, NB // 2, NS]),
                                                           con("qmask_s").rearrange("p (m t) -> p m t", t=NS), ALU.mult)
                        last.then_inc(masked, 1)
                    dve.wait_ge(a_raw, 1)
                    intra = con("intra_s" if sample else "intra").rearrange("p (h q) -> p h q", h=BH)
                    nc.vector.tensor_tensor(a[:, :, :].rearrange("p (m e) q -> p m e q", e=2), heads(ps_a[0:R, :, :], R, 2),
                                            intra.rearrange("p (m e) q -> p m e q", e=2), ALU.mult).then_inc(a_ready, 1)
                    if not sample:
                        dve.wait_ge(v_there, 1)
                        norm_rest(link, dve, o_raw[:, :, :])
                    dve.wait_ge(o_acc, 1)
                    dve.wait_ge(update_ready, 1)
                    for hh in range(BH):
                        if sample:
                            u = ps_u[:, hh, :].rearrange("p (m v) -> p m v", v=BDV)
                            last = nc.vector.scalar_tensor_tensor(out=st[:, :, hh, :], in0=st[:, :, hh, :],
                                                                  scalar=float(np.exp(LOG_G[hh] * NJ)), in1=u,
                                                                  op0=ALU.mult, op1=ALU.add)
                        else:
                            half, m = slice(hh % 2 * HD, hh % 2 * HD + HD), hh // 2
                            last = nc.vector.scalar_tensor_tensor(out=st[half, m, :], in0=st[half, m, :],
                                                                  scalar=float(np.exp(LOG_G[hh] * P)),
                                                                  in1=ps_u[half, 0, m * BDV:(m + 1) * BDV],
                                                                  op0=ALU.mult, op1=ALU.add)
                    last.then_inc(state_new, 1)
                    if sample:
                        po = ps_o[0:R, 0, :].rearrange("p (h v) -> p h v", h=BH)
                        norm_means(link, po)
                        norm_rest(link, dve, po)

                @block.scalar
                def _(act):
                    norm_root(act)
                    if not sample:
                        act.wait_ge(raw_used, 1)
                        act.wait_ge(o_acc, 1)
                        nc.scalar.copy(o_raw[:, :, :].rearrange("p (m e) v -> p m e v", e=2), heads(ps_o[:, :, :], BDV, 2))

                @block.tensor
                def _(pe):
                    pe.wait_ge(decayed, 2 if sample else 1)
                    flat = qk[:, :, :, :].rearrange("p h a f -> p (h a f)")
                    qdf = qd[:, :, :, :].rearrange("p h e f -> p (h e f)")
                    for m in range(4):
                        nc.tensor.transpose(ps_t[:, m, 0:R], flat[:, m * P:(m + 1) * P], con("ident")[0:R, 0:R])
                    for m in range(n_t - 4):
                        src = qdf[:, m * P:(m + 1) * P]
                        last = nc.tensor.transpose(ps_t[:, 4 + m, 0:R], src, con("ident")[0:R, 0:R])
                    last.then_inc(turned, 1)
                    pe.wait_ge(xT_ready, 1)
                    for hh in range(BH):
                        half, m = slice(hh % 2 * HD, hh % 2 * HD + HD), hh // 2
                        last = nc.tensor.matmul(ps_a[0:R, hh % 2, m * R:(m + 1) * R], xT[half, 2 + m, :], xT[half, m, :],
                                                start=True, stop=True)
                    last.then_inc(a_raw, 1)
                    v = x[:, 512:D].rearrange("p (h v) -> p h v", h=BH)
                    pe.wait_ge(a_ready, 1)
                    pe.wait_ge(masked if sample else v_there, 1)
                    for hh in range(BH):
                        half, m = slice(hh % 2 * HD, hh % 2 * HD + HD), hh // 2
                        acc = ps_o[0:R, 0, hh * BDV:(hh + 1) * BDV] if sample else ps_o[:, hh % 2, m * BDV:(m + 1) * BDV]
                        nc.tensor.matmul(acc, a[:, hh, :], v[:, hh, :], start=True, stop=False)
                        if sample:
                            for q in range(NB // 2):
                                last = nc.tensor.matmul(acc, qdm[:, hh, q, :], st[:, q, hh, :], start=False, stop=q == NB // 2 - 1)
                        else:
                            last = nc.tensor.matmul(acc, xT[half, 4 + m, :], st[half, m, :], start=False, stop=True)
                    last.then_inc(o_acc, 1)
                    for hh in range(BH):
                        half, m = slice(hh % 2 * HD, hh % 2 * HD + HD), hh // 2
                        if sample:
                            for q in range(NB // 2):
                                last = nc.tensor.matmul(ps_u[:, hh, q * BDV:(q + 1) * BDV],
                                                        kdm[:, hh, 2 * q:2 * q + 2, :].rearrange("p n k -> p (n k)"),
                                                        v[:, hh, :], start=True, stop=True)
                        else:
                            last = nc.tensor.matmul(ps_u[half, 0, m * BDV:(m + 1) * BDV], kd[:, hh, :], v[:, hh, :],
                                                    start=True, stop=True)
                    last.then_inc(update_ready, 1)
        if sample:
            round_(0)
        else:
            with nc.Fori(0, n_rounds) as i:
                round_(i)
                next_round(nc, sems)
        state_stored = ctx.semaphore(f"{name}_state_stored")
        with nc.Block() as block:
            @block.sync
            def _(sp):
                n = 0
                if sample:
                    for e in range(2):
                        for m in range(NB // 2):
                            sp.dma_start(state_out[2 * m + e].rearrange("h k v -> k h v"),
                                         st[e * HD:(e + 1) * HD, m, :, :]).then_inc(state_stored, 16)
                            n += 1
                else:
                    for hh in range(BH):
                        sp.dma_start(state_out[hh], st[hh % 2 * HD:hh % 2 * HD + HD, hh // 2, :]).then_inc(state_stored, 16)
                        n += 1
                    sp.wait_ge(v_moved, (n_rounds + 1) * 32)
                    sp.sem_inc(v_there, 1)
                    sp.wait_ge(out_ready, 1)
                    store_chunk(sp, n_rounds - 1)
                    sp.wait_ge(v_moved, (n_rounds + 1) * 32 + 16)
                sp.wait_ge(state_stored, 16 * n)

            if not sample:
                @block.scalar
                def _(act):
                    norm_root(act)

                @block.vector
                def _(dve):
                    steps = 0

                    def link(ins):
                        nonlocal steps
                        steps += 1
                        ins.then_inc(dve_step, 1)
                        dve.wait_ge(dve_step, steps)
                    norm_means(link, o_raw[:, :, :])
                    dve.wait_ge(v_there, 1)
                    norm_rest(link, dve, o_raw[:, :, :])


def attend_samples_dilated(nc, con, h_s, cache_k, cache_v, rows, mix):
    with Phase(nc) as ctx:
        def sb(nm, shape, dt=F32):
            return ctx.enter_context(nc.sbuf_tensor(f"ds_{nm}", shape, dt))

        def sem(nm):
            s = ctx.semaphore(f"ds_{nm}")
            sems.append(s)
            return s
        sems = []
        placed = ctx.semaphore("ds_placed")
        NP = 4
        q_in = sb("q_in", [NS, 512])
        q_all = sb("q_all", [P, NB, NP * 32])
        q_cur = sb("q_cur", [P, NP * 32])
        kw, ks, kn = sb("kw", [P, 4, 512]), sb("ks", [STR, 4, 512]), sb("kn", [NJ, 512])
        vw, vs, vn = sb("vw", [P, 4, 512]), sb("vs", [STR, 4, 512]), sb("vn", [NJ, 512])
        kT = sb("kT", [P, NP, AK])
        pr = sb("pr", [32, AK])
        pw, pst, pn = sb("pw", [P, 4, 32]), sb("pst", [STR, 4, 32]), sb("pn", [NJ, 32])
        stat = sb("stat", [32, 3])
        part = sb("part", [32, 8, HD])
        o = sb("o", [32, HD])
        ps_t = [ctx.enter_context(nc.psum_tensor(f"ds_ps_t{b}", [P, 512], F32)) for b in range(2)]
        ps_s = ctx.enter_context(nc.psum_tensor("ds_ps_s", [32, 1024], F32))
        ps_p = ctx.enter_context(nc.psum_tensor("ds_ps_p", [P, 9, 32], F32))
        ps_o = ctx.enter_context(nc.psum_tensor("ds_ps_o", [32, 512], F32))
        q_loaded, q_zero, q_turned, q_placed = (
            ctx.semaphore(f"ds_{n}") for n in "q_loaded q_zero q_turned q_placed".split())
        k_in, v_moved = ctx.semaphore("ds_k_in"), ctx.semaphore("ds_v_moved")
        k_there, v_there, q_ready, turned, copied_act, copied_dve, scores_ready, max_ready, probs_ready = (
            sem(n) for n in "k_there v_there q_ready turned copied_act copied_dve scores_ready max_ready probs_ready".split())
        probs_turned, probsT_ready, o_ready, inverse, part_ready, out_ready = (
            sem(n) for n in "probs_turned probsT_ready o_ready inverse part_ready out_ready".split())
        copied = [copied_act, copied_dve]

        def load(sp, n, cache, w, st, new, col, s):
            c = cache[bass.ds(n, 1)].rearrange("n r c -> (n r) c")
            sp.dma_start(w[:, :, :].rearrange("p s c -> p (s c)"),
                         c[PAST - 512:PAST, :].rearrange("(p s) c -> p (s c)", s=4)).then_inc(s, 16)
            sp.dma_start(st[:, :, :].rearrange("p s c -> p (s c)"),
                         c[0:PAST - 512, :].rearrange("(p s) c -> p (s c)", s=16)[:, 0:4 * 512]).then_inc(s, 16)
            sp.dma_start(new[:, :], h_s[bass.ds(n * NJ, NJ), col:col + 512]).then_inc(s, 16)

        with nc.Block() as block:
            @block.sync
            def _(sp):
                sp.dma_start(q_in[:, :], h_s[:, QA:QA + 512]).then_inc(q_loaded, 16)
                load(sp, 0, cache_k, kw, ks, kn, KA, k_in)
                load(sp, 0, cache_v, vw, vs, vn, VA, v_moved)
                sp.sem_inc(v_moved, 16)

            @block.tensor
            def _(pe):
                pe.wait_ge(q_loaded, 16)
                for m in range(NP):
                    last = nc.tensor.transpose(ps_t[0][:, m * NS:(m + 1) * NS], q_in[:, m * P:(m + 1) * P], con("ident")[0:NS, 0:NS])
                last.then_inc(q_turned, 1)

            @block.vector
            def _(dve):
                for w in (pw[:, :, :], pst[:, :, :], pn[:, :], stat[:, 2:3]):
                    nc.vector.memset(w, 0.0)
                nc.vector.memset(q_all[:, :, :], 0.0).then_inc(q_zero, 1)
                dve.wait_ge(q_zero, 1)
                dve.wait_ge(q_turned, 1)
                to = q_all[:, :, :].rearrange("p n (m h j) -> p n m h j", m=NP, h=8)
                for hh in range(8):
                    half = slice(hh % 2 * HD, hh % 2 * HD + HD)
                    src = ps_t[0][half, (hh // 2) * NS:(hh // 2 + 1) * NS].rearrange("p (n j) -> p n j", j=NJ)
                    last = nc.vector.tensor_scalar(to[half, :, hh // 2, hh, :], src, -SCALE, None, ALU.mult)
                last.then_inc(q_placed, 1)
                dve.wait_ge(q_placed, 1)

        def o_product(pe):
            pe.wait_ge(v_there, 1)
            for g in range(9):
                lhs = pw[:, g, :] if g < 4 else pst[:, g - 4, :] if g < 8 else pn[:, :]
                rhs = vw[:, g, :] if g < 4 else vs[:, g - 4, :] if g < 8 else vn[:, :]
                last = nc.tensor.matmul(ps_o[:, :], lhs, rhs, start=g == 0, stop=g == 8)
            last.then_inc(o_ready, 1)

        def finish_out(dve):
            dve.wait_ge(o_ready, 1)
            nc.vector.scalar_tensor_tensor(out=part[:, :, :].rearrange("p h d -> p (h d)"), in0=ps_o[:, :], scalar=stat[:, 2:3],
                                           in1=con("adiag"), op0=ALU.mult, op1=ALU.mult).then_inc(part_ready, 1)
            dve.wait_ge(part_ready, 1)
            dve.wait_ge(v_there, 1)
            nc.vector.tensor_reduce(o[:, :], part[:, :, :].rearrange("p h d -> p d h"), AX, ALU.add).then_inc(out_ready, 1)

        def store_out(sp, n):
            sp.dma_start(rows[bass.ds(n * 32, 32), :], o[:, :]).then_inc(v_moved, 16)

        widths = [P] * 4 + [STR] * 4 + [NJ]
        with nc.Fori(0, NB) as n:
            with nc.Block() as block:
                @block.sync
                def _(sp):
                    sp.wait_ge(v_moved, (n + 1) * 64)
                    sp.sem_inc(v_there, 1)
                    sp.wait_ge(turned, 9)
                    load(sp, (n + 1) % NB, cache_k, kw, ks, kn, KA, k_in)
                    sp.wait_ge(o_ready, 1)
                    load(sp, n, cache_v, vw, vs, vn, VA, v_moved)
                    sp.wait_ge(out_ready, 1)
                    store_out(sp, (n + NB - 1) % NB)

                def copy_group(eng, copy, g):
                    eng.wait_ge(turned, g + 1)
                    c0 = sum(widths[:g])
                    copy(kT[:, :, c0:c0 + widths[g]],
                         ps_t[g % 2][:, :].rearrange("p (m c) -> p m c", m=NP)[:, :, 0:widths[g]]).then_inc(copied[g % 2], 1)

                @block.tensor
                def _(pe):
                    pe.wait_ge(k_there, 1)
                    for g in range(9):
                        if g >= 2:
                            pe.wait_ge(copied[g % 2], g // 2)
                        src = kw[:, g, :] if g < 4 else ks[:, g - 4, :] if g < 8 else kn[:, :]
                        w = widths[g]
                        for m in range(NP):
                            last = nc.tensor.transpose(ps_t[g % 2][:, m * P:m * P + w], src[:, m * P:(m + 1) * P], con("ident")[0:w, 0:w])
                        last.then_inc(turned, 1)
                    pe.wait_ge(q_ready, 1)
                    pe.wait_ge(copied[0], 5)
                    pe.wait_ge(copied[1], 4)
                    for c0, c1 in ((0, 512), (512, AK)):
                        for m in range(NP):
                            last = nc.tensor.matmul(ps_s[:, c0:c1], q_cur[:, m * 32:(m + 1) * 32], kT[:, m, c0:c1],
                                                    start=m == 0, stop=m == NP - 1)
                    last.then_inc(scores_ready, 1)
                    o_product(pe)
                    pe.wait_ge(probs_ready, 1)
                    for g in range(9):
                        c0, w = sum(widths[:g]), widths[g]
                        last = nc.tensor.transpose(ps_p[0:w, g, :], pr[:, c0:c0 + w], con("ident")[0:32, 0:32])
                    last.then_inc(probs_turned, 1)

                @block.scalar
                def _(act):
                    act.wait_ge(k_in, (n + 1) * 48)
                    act.sem_inc(k_there, 1)
                    for g in range(0, 9, 2):
                        copy_group(act, nc.scalar.copy, g)
                    act.wait_ge(max_ready, 1)
                    nc.scalar.activation(pr[:, :], pr[:, :], ACT.Exp, scale=-1.0, bias=stat[:, 0:1],
                                         accum_out=stat[:, 1:2]).then_inc(probs_ready, 1)

                @block.vector
                def _(dve):
                    nc.vector.tensor_copy(q_cur[:, :], q_all[:, bass.ds(n, 1), :].rearrange("p n c -> p (n c)")).then_inc(q_ready, 1)
                    for g in range(1, 9, 2):
                        copy_group(dve, nc.vector.tensor_copy, g)
                    dve.wait_ge(scores_ready, 1)
                    nc.vector.tensor_tensor_reduce(out=pr[:, :], in0=ps_s[:, 0:AK], in1=con("asbias"), scale=1.0, scalar=3e38,
                                                   op0=ALU.add, op1=ALU.min, accum_out=stat[:, 0:1]).then_inc(max_ready, 1)
                    finish_out(dve)
                    dve.wait_ge(probs_turned, 1)
                    nc.vector.tensor_copy(pw[:, :, :], ps_p[:, 0:4, :])
                    nc.vector.tensor_copy(pst[:, :, :], ps_p[0:STR, 4:8, :])
                    nc.vector.tensor_copy(pn[:, :], ps_p[0:NJ, 8, :]).then_inc(probsT_ready, 1)
                    nc.vector.reciprocal(stat[:, 2:3], stat[:, 1:2]).then_inc(inverse, 1)
                    dve.wait_ge(inverse, 1)
            next_round(nc, sems)

        with nc.Block() as block:
            @block.tensor
            def _(pe):
                o_product(pe)

            @block.vector
            def _(dve):
                finish_out(dve)

            @block.sync
            def _(sp):
                sp.wait_ge(v_moved, (NB + 1) * 64)
                sp.sem_inc(v_there, 1)
                sp.wait_ge(out_ready, 1)
                store_out(sp, NB - 1)
                sp.wait_ge(k_in, (NB + 1) * 48)
                sp.wait_ge(v_moved, (NB + 1) * 64 + 16)
                for n in range(NB):
                    sp.dma_start(mix[T + n * NJ:T + (n + 1) * NJ, 0:512].rearrange("j (h d) -> j h d", d=HD),
                                 rows[n * 32:(n + 1) * 32, :].rearrange("(h j) d -> j h d", j=NJ)).then_inc(placed, 16)
                sp.wait_ge(placed, 16 * NB)


class Compressor:

    def __init__(self, nc, ctx, con):
        self.nc, self.con = nc, con
        self.w1 = [ctx.enter_context(nc.sbuf_tensor(f"cmp_w1_{m}", [P, 16, CH], F32)) for m in range(2)]
        self.w2k = ctx.enter_context(nc.sbuf_tensor("cmp_w2k", [P, 2, 2, P], F32))
        self.w2v = ctx.enter_context(nc.sbuf_tensor("cmp_w2v", [P, 2, HD], F32))
        self.bias = ctx.enter_context(nc.sbuf_tensor("cmp_bias", [P, 2, 2], F32))

    def setup(self, w1, w2, pos):
        nc = self.nc
        with Phase(nc) as ctx:
            pos_in = ctx.enter_context(nc.sbuf_tensor("cmp_pos_in", [16, 2, P], F32))
            pe_in = ctx.enter_context(nc.sbuf_tensor("cmp_pos", [P, 2, 16], F32))
            ps = ctx.enter_context(nc.psum_tensor("cmp_ps", [P, 4], F32))
            ps_pos = ctx.enter_context(nc.psum_tensor("cmp_ps_pos", [P, 2, 16], F32))
            w1_in = [ctx.semaphore(f"cmp_w1_in{m}") for m in range(2)]
            pos_loaded, turned, copied = (ctx.semaphore(f"cmp_{n}") for n in "pos_loaded turned copied".split())
            loaded, zeroed, product, done = (ctx.semaphore(f"cmp_{n}") for n in "loaded zeroed product done".split())
            with nc.Block() as block:
                @block.sync
                def _(sp):
                    for m in range(2):
                        sp.dma_start(pos_in[:, m, :], pos[m].rearrange("(l a) d -> l (a d)", a=2)).then_inc(pos_loaded, 16)
                    for m in range(2):
                        sp.dma_start(self.w1[m][:, :, :], w1[m].rearrange("(l p) f -> p l f", p=P)).then_inc(w1_in[m], 16)
                    sp.dma_start(self.w2v[:, :, :], w2[1].rearrange("(c f) d -> f c d", f=P)).then_inc(loaded, 16)
                    sp.wait_ge(zeroed, 1)
                    for g in range(2):
                        sp.dma_start(self.w2k[:, :, g, g * HD:(g + 1) * HD],
                                     w2[0].rearrange("(c f) d -> f c d", f=P)).then_inc(loaded, 16)
                    sp.wait_ge(loaded, 16 * 3)

                @block.tensor
                def _(pe):
                    pe.wait_ge(pos_loaded, 32)
                    for m in range(2):
                        last = nc.tensor.transpose(ps_pos[:, m, :], pos_in[:, m, :], self.con("ident")[0:16, 0:16])
                    last.then_inc(turned, 1)
                    pe.wait_ge(copied, 1)
                    for m in range(2):
                        pe.wait_ge(w1_in[m], 16)
                        for c in range(2):
                            for l in range(16):
                                last = nc.tensor.matmul(ps[:, 2 * m + c:2 * m + c + 1], self.w1[m][:, l, c * P:(c + 1) * P],
                                                        pe_in[:, m, l:l + 1], start=l == 0, stop=l == 15)
                    last.then_inc(product, 1)

                @block.vector
                def _(dve):
                    nc.vector.memset(self.w2k[:, :, :, :], 0.0).then_inc(zeroed, 1)
                    dve.wait_ge(turned, 1)
                    nc.vector.tensor_copy(pe_in[:, :, :], ps_pos[:, :, :]).then_inc(copied, 1)
                    dve.wait_ge(product, 1)
                    nc.vector.tensor_copy(self.bias[:, :, :].rearrange("p m c -> p (m c)"), ps[:, :]).then_inc(done, 1)
                    dve.wait_ge(done, 1)

    def turn(self, x, q, pieces, out):
        for c in range(4):
            g, l = divmod(4 * q + c, 8)
            src = x[:, g, 2 * l:2 * l + 2, :].rearrange("p s d -> p (s d)")
            last = self.nc.tensor.transpose(out[:, c * P:c * P + pieces], src, self.con("ident")[0:pieces, 0:pieces])
        return last

    def hidden(self, m, xT, blocks, out, c):
        for l in range(16):
            s = 0 if l < 8 else 1
            last = self.nc.tensor.matmul(out[:, c * 256:c * 256 + 2 * blocks], self.w1[m][:, l, c * P:(c + 1) * P],
                                         xT[:, :, l % 8, s:s + blocks], start=l == 0, stop=l == 15)
        return last

    def down_k(self, hid, blocks, out):
        for x, (c, g) in enumerate([(c, g) for c in range(2) for g in range(2)]):
            last = self.nc.tensor.matmul(out, self.w2k[:, c, g, :], hid[:, c, g, :], start=x == 0, stop=x == 3)
        return last

    def down_v(self, hid, blocks, out):
        for g in range(2):
            for c in range(2):
                last = self.nc.tensor.matmul(out[:, g * HD:(g + 1) * HD], hid[:, c, g, :], self.w2v[:, c, :],
                                             start=c == 0, stop=c == 1)
        return last


def compress_prompt(nc, con, comp, h, kcmp, vcmp):
    with Phase(nc) as ctx:
        def sem(nm):
            return ctx.semaphore(f"cp_{nm}")
        x = [ctx.enter_context(nc.sbuf_tensor(f"cp_x{m}", [NPC, 2, 16, HD], F32)) for m in range(2)]
        xT = [ctx.enter_context(nc.sbuf_tensor(f"cp_xT{m}", [P, 2, 8, NPC], F32)) for m in range(2)]
        hid = [ctx.enter_context(nc.sbuf_tensor(f"cp_hid{m}", [P, 2, 2, NCB], F32)) for m in range(2)]
        kc = ctx.enter_context(nc.sbuf_tensor("cp_kc", [P, NCB], F32))
        vc = ctx.enter_context(nc.sbuf_tensor("cp_vc", [NCB, P], F32))
        ps_t = [ctx.enter_context(nc.psum_tensor(f"cp_t{b}", [P, 512], F32)) for b in range(2)]
        ps_h = [ctx.enter_context(nc.psum_tensor(f"cp_h{b}", [P, 512], F32)) for b in range(2)]
        ps_c = ctx.enter_context(nc.psum_tensor("cp_c", [P, 2, P], F32))
        loaded, turned, copied, hidden, active, products, ready, stored = (
            sem(n) for n in "loaded turned copied hidden active products ready stored".split())
        with nc.Block() as block:
            @block.sync
            def _(sp):
                for m, col in enumerate((KC, VC)):
                    for g in range(2):
                        sp.dma_start(x[m][:, g, :, :], h[0][:, col + g * HD:col + (g + 1) * HD].rearrange("(p s) c -> p s c", s=16)).then_inc(loaded, 16)
                sp.wait_ge(ready, 2)
                sp.dma_start(kcmp, kc[:, :]).then_inc(stored, 16)
                sp.dma_start(vcmp, vc[:, :]).then_inc(stored, 16)
                sp.wait_ge(stored, 32)

            @block.tensor
            def _(pe):
                pe.wait_ge(loaded, 64)
                for m in range(2):
                    for q in range(4):
                        g = 4 * m + q
                        if g >= 2:
                            pe.wait_ge(copied, g - 1)
                        comp.turn(x[m], q, NPC, ps_t[g % 2]).then_inc(turned, 1)
                for m in range(2):
                    pe.wait_ge(copied, 4 * (m + 1))
                    for c in range(2):
                        comp.hidden(m, xT[m], NCB, ps_h[m], c).then_inc(hidden, 1)
                pe.wait_ge(active, 4)
                comp.down_k(hid[0], NCB, ps_c[:, 0, 0:NCB])
                comp.down_v(hid[1], NCB, ps_c[0:NCB, 1, :]).then_inc(products, 1)

            @block.scalar
            def _(act):
                for m in range(2):
                    for c in range(2):
                        act.wait_ge(hidden, 2 * m + 2)
                        nc.scalar.activation(hid[m][:, c, :, :],
                                             ps_h[m][:, c * 256:c * 256 + 2 * NCB].rearrange("p (g b) -> p g b", g=2),
                                             ACT.Silu, bias=comp.bias[:, m, c:c + 1]).then_inc(active, 1)

            @block.vector
            def _(dve):
                for m in range(2):
                    for q in range(4):
                        dve.wait_ge(turned, 4 * m + q + 1)
                        nc.vector.tensor_copy(xT[m][:, q // 2, (q % 2) * 4:(q % 2) * 4 + 4, :],
                                              ps_t[q % 2][:, :].rearrange("p (l c) -> p l c", c=P)[:, :, 0:NPC]).then_inc(copied, 1)
                dve.wait_ge(products, 1)
                nc.vector.tensor_copy(kc[:, :], ps_c[:, 0, 0:NCB]).then_inc(ready, 1)
                nc.vector.tensor_copy(vc[:, :], ps_c[0:NCB, 1, :]).then_inc(ready, 1)


def attend_samples_sparse(nc, con, comp, h_s, pools, wins, page_table, branches, gathers):
    with Phase(nc) as ctx:
        def sb(nm, shape, dt=F32):
            return ctx.enter_context(nc.sbuf_tensor(f"ss_{nm}", shape, dt))

        def sem(nm):
            s = ctx.semaphore(f"ss_{nm}")
            sems.append(s)
            return s
        sems = []
        NKEY = PAST + NJ
        q_in = sb("q_in", [NS, 8, 2, HD])
        q_all = sb("q_all", [P, NB, 64])
        q_cur = sb("q_cur", [P, 64])
        pages = sb("pages", [P, NB + 1], I32)
        rows = sb("rows", [P, NB + 1], I32)
        pages_f, rows_f = sb("pages_f", [P, NB + 1]), sb("rows_f", [P, NB + 1])
        row_cur = sb("row_cur", [P, 1], I32)
        row_now = sb("row_now", [P, 1], I32)
        kc_in, vc_in, ks_in, vs_in = (sb(n, [P, 16, P]) for n in "kc_in vc_in ks_in vs_in".split())
        kc_p, vc_p = sb("kc_p", [P, 2, 16, HD]), sb("vc_p", [P, 2, 16, HD])
        kw_in, vw_in = sb("kw_in", [P, 4, P]), sb("vw_in", [P, 4, P])
        new_in = sb("new_in", [NJ, 4, P])
        xT = sb("xT", [P, 2, 8, P])
        hid = sb("hid", [P, 2, 2, NCS])
        kc, vc = sb("kc", [P, NCS]), sb("vc", [NCS, P])
        ksT, kwT, newT = sb("ksT", [P, PAST]), sb("kwT", [P, 512]), sb("newT", [P, 2, NJ])
        pc, pcT = sb("pc", [64, NCS]), sb("pcT", [NCS, 64])
        share, score, score2, top = sb("share", [64, NSL]), sb("score", [64, NSL]), sb("score2", [64, NSL]), sb("top", [64, 8])
        bias_b, bias = sb("bias_b", [64, NSL]), sb("bias", [64, 32, 4])
        psel, pwin = sb("psel", [64, NKEY]), sb("pwin", [64, 512 + NJ])
        pselT, pselnT = sb("pselT", [P, 16, 64]), sb("pselnT", [NJ, 64])
        pwinT, pwinnT = sb("pwinT", [P, 4, 64]), sb("pwinnT", [NJ, 64])
        mins, stat = sb("mins", [64, 8]), sb("stat", [64, 3, 3])
        o = sb("o", [64, 3, HD])
        ps_t = [ctx.enter_context(nc.psum_tensor(f"ss_ps_t{b}", [P, 512], F32)) for b in range(2)]
        ps_s = ctx.enter_context(nc.psum_tensor("ss_ps_s", [64, 4, 512], F32))
        ps_h = ctx.enter_context(nc.psum_tensor("ss_ps_h", [P, 512], F32))
        ps_m = ctx.enter_context(nc.psum_tensor("ss_ps_m", [P, 512], F32))
        M_KC, M_CS, M_SH, M_SUM, M_NEW, M_O = (slice(0, P), slice(128, 128 + NCS), slice(256, 256 + NSL), slice(290, 290 + NSL),
                                               slice(324, 332), slice(384, 512))
        pre = {n: ctx.semaphore(f"ss_{n}") for n in
               "table_in index_step index_ready q_loaded q_zero q_turned q_placed".split()}
        win_in, stored = ctx.semaphore("ss_win_in"), ctx.semaphore("ss_stored")
        s = {n: sem(n) for n in
             ("rows_in windows_in row_ready pieces_k pieces_v new_read sum_read q_ready turned copied_act copied_dve hid_k act_k prod_k kc_ready "
              "cmp_scores cmp_max cmp_probs cmp_norm share_raw share_ready sum_raw bias_ready sel_scores sel_max sel_probs "
              "hid_v act_v prod_v vc_ready cmp_o cmp_o_ready win_max win_probs sel_o sel_o_ready win_o win_o_ready "
              "dve_step").split()}
        copied = [s["copied_act"], s["copied_dve"]]

        def gather(pool, to, m, which, row=row_cur):
            return pool.indirect_dma_start(out=to[:, :, :].rearrange("p s c -> p (s c)"), out_offset=None,
                                           in_=pools[m], in_offset=bass.IndirectOffsetOnAxis(ap=row[:, 0:1], axis=0)
                                           ).then_inc(which, 16)

        def load_windows(sp, n, which):
            for to, fr in ((kw_in, wins[0]), (vw_in, wins[1])):
                sp.dma_start(to[:, :, :].rearrange("p s c -> p (s c)"),
                             fr[bass.ds(n, 1)].rearrange("n (p s) c -> p (n s c)", s=4)).then_inc(which, 16)
            sp.dma_start(new_in[:, :, :].rearrange("j m c -> j (m c)"), h_s[bass.ds(n * NJ, NJ), KS:KS + 512]).then_inc(which, 16)

        with nc.Block() as block:
            @block.sync
            def _(sp):
                for g in range(2):
                    sp.dma_start(q_in[:, :, g, :], h_s[:, QC + g * 512:QC + (g + 1) * 512].rearrange("t (r d) -> t r d", d=HD)
                                 ).then_inc(pre["q_loaded"], 16)
                for pg in range(PAST // PAGE):
                    for col, n0, n in ((0, 0, NB), (NB, 0, 1)):
                        sp.dma_start(pages[pg * 8:(pg + 1) * 8, col:col + n],
                                     page_table[n0:n0 + n, pg:pg + 1].rearrange("n a -> a n").broadcast_to([8, n]),
                                     allow_slow_non_contiguous=True).then_inc(pre["table_in"], 16)
                load_windows(sp, 0, win_in)
                sp.sem_inc(stored, 48)

            @block.gpsimd
            def _(pool):
                pool.wait_ge(pre["index_ready"], 1)
                for m, to in enumerate((kc_in, vc_in, ks_in)):
                    gather(pool, to, m, gathers[("kc", "vc", "ks")[m]])

            @block.tensor
            def _(pe):
                pe.wait_ge(pre["q_loaded"], 32)
                for r in range(8):
                    last = nc.tensor.transpose(ps_t[0][:, r * NS:(r + 1) * NS], q_in[:, r, :, :].rearrange("t g d -> t (g d)"), con("ident")[0:NS, 0:NS])
                last.then_inc(pre["q_turned"], 1)

            @block.vector
            def _(dve):
                count = 0

                def link(ins):
                    nonlocal count
                    count += 1
                    ins.then_inc(pre["index_step"], 1)
                    dve.wait_ge(pre["index_step"], count)
                dve.wait_ge(pre["table_in"], 16 * 2 * (PAST // PAGE))
                link(nc.vector.tensor_copy(pages_f[:, :], pages[:, :]))
                link(nc.vector.tensor_scalar(rows_f[:, :], pages_f[:, :], 8.0, con("sub"), ALU.mult, ALU.add))
                link(nc.vector.tensor_copy(rows[:, :], rows_f[:, :]))
                nc.vector.tensor_copy(row_cur[:, :], rows[:, 0:1]).then_inc(pre["index_ready"], 1)
                nc.vector.memset(q_all[:, :, :], 0.0).then_inc(pre["q_zero"], 1)
                dve.wait_ge(pre["q_zero"], 1)
                dve.wait_ge(pre["q_turned"], 1)
                to = q_all[:, :, :].rearrange("p n (g r j) -> p n g r j", g=2, r=8)
                for g in range(2):
                    half = slice(g * HD, (g + 1) * HD)
                    src = ps_t[0][half, 0:256].rearrange("p (r n j) -> p n r j", r=8, n=NB)
                    last = nc.vector.tensor_scalar(to[half, :, g, :, :], src, -SCALE, None, ALU.mult)
                last.then_inc(pre["q_placed"], 1)
                dve.wait_ge(pre["q_placed"], 1)

        def v4(ap):
            return ap.rearrange("p (c k) -> p c k", c=4)
        G_SEL, G_CK, G_WIN, G_NEW, G_CV, G_PC, G_WS, G_PS, G_PW = 0, 4, 8, 9, 10, 14, 15, 16, 18

        with nc.Fori(0, NB) as n:
            with nc.Block() as block:
                @block.sync
                def _(sp):
                    sp.wait_ge(win_in, (n + 1) * 48)
                    sp.wait_ge(stored, (n + 1) * 48)
                    sp.sem_inc(s["windows_in"], 1)
                    for b, ready in enumerate(("cmp_o_ready", "sel_o_ready", "win_o_ready")):
                        sp.wait_ge(s[ready], 1)
                        if b == 2:
                            load_windows(sp, (n + 1) % NB, win_in)
                        sp.dma_start(branches[b, bass.ds(n * 64, 64), :], o[:, b, :]).then_inc(stored, 16)

                @block.gpsimd
                def _(pool):
                    for which in ("ks", "kc", "vc"):
                        pool.wait_ge(gathers[which], (n + 1) * 16)
                        pool.sem_inc(s["rows_in"], 1)
                    nc.gpsimd.tensor_copy(row_now[:, :], rows[:, bass.ds(n, 1)])
                    nc.gpsimd.tensor_copy(row_cur[:, :], rows[:, bass.ds(n + 1, 1)]).then_inc(s["row_ready"], 1)
                    pool.wait_ge(s["row_ready"], 1)
                    gather(pool, vs_in, 3, gathers["vs"], row_now)
                    nc.gpsimd.tensor_copy(vc_p[:, :, :, :], vc_in[:, :, :].rearrange("p s (g d) -> p g s d", g=2)).then_inc(s["pieces_v"], 1)
                    pool.wait_ge(s["pieces_v"], 1)
                    gather(pool, vc_in, 1, gathers["vc"])
                    pool.wait_ge(s["pieces_k"], 2)
                    gather(pool, kc_in, 0, gathers["kc"])
                    pool.wait_ge(s["turned"], G_SEL + 4)
                    gather(pool, ks_in, 2, gathers["ks"])
                    pool.wait_ge(gathers["vs"], (n + 1) * 16)
                    pool.sem_inc(s["rows_in"], 1)

                def copy_pieces_k(eng, copy, g):
                    eng.wait_ge(s["rows_in"], 2)
                    copy(kc_p[:, g, :, :], kc_in[:, :, g * HD:(g + 1) * HD]).then_inc(s["pieces_k"], 1)

                def copy_group(eng, copy, g):
                    eng.wait_ge(s["turned"], g + 1)
                    src = ps_t[g % 2]
                    done = copied[g % 2]
                    if g < G_CK:
                        copy(ksT[:, g * 512:(g + 1) * 512], src[:, :]).then_inc(done, 1)
                    elif g < G_WIN or G_CV <= g < G_PC:
                        if g in (G_CV, G_CV + 1):
                            eng.wait_ge(s["hid_k"], 2)
                        q = g - G_CK if g < G_WIN else g - G_CV
                        copy(xT[:, q // 2, (q % 2) * 4:(q % 2) * 4 + 4, :], v4(src[:, :])).then_inc(done, 1)
                    elif g == G_WIN:
                        copy(kwT[:, :], src[:, :]).then_inc(done, 1)
                    elif g == G_NEW:
                        copy(newT[:, :, :], src[:, 0:2 * NJ].rearrange("p (m j) -> p m j", j=NJ)).then_inc(done, 1)
                    elif g == G_PC:
                        copy(pcT[:, :], src[0:NCS, 0:64]).then_inc(done, 1)
                    elif g < G_PW:
                        x = g - G_PS
                        copy(pselT[:, 8 * x:8 * x + 8, :], src[:, :].rearrange("p (c k) -> p c k", c=8)).then_inc(done, 1)
                    else:
                        copy(pwinT[:, :, :], src[:, 0:256].rearrange("p (c k) -> p c k", c=4))
                        copy(pselnT[:, :], src[0:NJ, 256:320])
                        copy(pwinnT[:, :], src[0:NJ, 320:384]).then_inc(done, 1)

                @block.tensor
                def _(pe):
                    id64 = con("ident")[0:64, 0:64]

                    def bank(g):
                        if g >= 2:
                            pe.wait_ge(copied[g % 2], g // 2)
                        return ps_t[g % 2]

                    def all_copied(g):
                        pe.wait_ge(copied[0], g // 2 + 1)
                        pe.wait_ge(copied[1], (g + 1) // 2)
                    pe.wait_ge(s["rows_in"], 1)
                    for g in range(G_SEL, G_SEL + 4):
                        to = bank(g)
                        for c in range(4):
                            last = nc.tensor.transpose(to[:, c * P:(c + 1) * P], ks_in[:, 4 * g + c, :], con("ident"))
                        last.then_inc(s["turned"], 1)
                    pe.wait_ge(s["pieces_k"], 2)
                    for q in range(4):
                        comp.turn(kc_p, q, P, bank(G_CK + q)).then_inc(s["turned"], 1)
                    pe.wait_ge(s["windows_in"], 1)
                    to = bank(G_WIN)
                    for c in range(4):
                        last = nc.tensor.transpose(to[:, c * P:(c + 1) * P], kw_in[:, c, :], con("ident"))
                    last.then_inc(s["turned"], 1)
                    to = bank(G_NEW)
                    for c in range(2):
                        last = nc.tensor.transpose(to[:, c * NJ:(c + 1) * NJ], new_in[:, 2 * c, :], con("ident")[0:NJ, 0:NJ])
                    last.then_inc(s["turned"], 1)
                    all_copied(G_NEW)
                    pe.wait_ge(s["q_ready"], 1)
                    for c in range(2):
                        comp.hidden(0, xT, NCS, ps_h, c).then_inc(s["hid_k"], 1)
                    for c in range(4):
                        nc.tensor.matmul(ps_s[:, c, :], q_cur[:, :], ksT[:, c * 512:(c + 1) * 512], start=True, stop=True)
                    nc.tensor.matmul(ps_m[0:64, M_NEW.start:M_NEW.start + NJ], q_cur[:, :], newT[:, 0, :], start=True, stop=True)
                    nc.tensor.matmul(ps_m[0:64, M_NEW.start + NJ:M_NEW.stop], q_cur[:, :], newT[:, 1, :], start=True,
                                     stop=True).then_inc(s["sel_scores"], 1)
                    pe.wait_ge(s["act_k"], 2)
                    pe.wait_ge(s["new_read"], 1)
                    comp.down_k(hid, NCS, ps_m[:, 0:NCS]).then_inc(s["prod_k"], 1)
                    pe.wait_ge(s["pieces_v"], 1)
                    for q in range(4):
                        comp.turn(vc_p, q, P, bank(G_CV + q)).then_inc(s["turned"], 1)
                    pe.wait_ge(s["kc_ready"], 1)
                    nc.tensor.matmul(ps_m[0:64, M_CS], q_cur[:, :], kc[:, :], start=True, stop=True).then_inc(s["cmp_scores"], 1)
                    all_copied(G_CV + 3)
                    comp.hidden(1, xT, NCS, ps_h, 0).then_inc(s["hid_v"], 1)
                    pe.wait_ge(s["cmp_norm"], 1)
                    to = bank(G_PC)
                    nc.tensor.transpose(to[0:NCS, 0:64], pc[:, :], id64).then_inc(s["turned"], 1)
                    nc.tensor.matmul(bank(G_WS)[0:64, :], q_cur[:, :], kwT[:, :], start=True, stop=True).then_inc(s["turned"], 1)
                    all_copied(G_PC)
                    nc.tensor.matmul(ps_m[0:64, M_SH], pcT[:, :], con("overlap"), start=True, stop=True).then_inc(s["share_raw"], 1)
                    pe.wait_ge(s["share_ready"], 1)
                    nc.tensor.matmul(ps_m[0:64, M_SUM], con("same"), share[:, :], start=True, stop=True).then_inc(s["sum_raw"], 1)
                    comp.hidden(1, xT, NCS, ps_h, 1).then_inc(s["hid_v"], 1)
                    pe.wait_ge(s["sel_probs"], 1)
                    for g in (G_PS, G_PS + 1):
                        to = bank(g)
                        for c in range(8):
                            k0 = (8 * (g - G_PS) + c) * P
                            last = nc.tensor.transpose(to[:, c * 64:(c + 1) * 64], psel[:, k0:k0 + P], id64)
                        last.then_inc(s["turned"], 1)
                    pe.wait_ge(s["act_v"], 2)
                    pe.wait_ge(s["sum_read"], 1)
                    comp.down_v(hid, NCS, ps_m[0:NCS, M_KC]).then_inc(s["prod_v"], 1)
                    pe.wait_ge(s["vc_ready"], 1)
                    nc.tensor.matmul(ps_m[0:64, M_O], pcT[:, :], vc[:, :], start=True, stop=True).then_inc(s["cmp_o"], 1)
                    pe.wait_ge(s["win_probs"], 1)
                    to = bank(G_PW)
                    for c in range(4):
                        nc.tensor.transpose(to[:, c * 64:(c + 1) * 64], pwin[:, c * P:(c + 1) * P], id64)
                    nc.tensor.transpose(to[0:NJ, 256:320], psel[:, PAST:NKEY], id64)
                    nc.tensor.transpose(to[0:NJ, 320:384], pwin[:, 512:512 + NJ], id64).then_inc(s["turned"], 1)
                    all_copied(G_PW)
                    pe.wait_ge(s["cmp_o_ready"], 1)
                    pe.wait_ge(s["rows_in"], 4)
                    for c in range(16):
                        nc.tensor.matmul(ps_m[0:64, M_O], pselT[:, c, :], vs_in[:, c, :], start=c == 0, stop=False)
                    nc.tensor.matmul(ps_m[0:64, M_O], pselnT[:, :], new_in[:, 1, :], start=False, stop=True).then_inc(s["sel_o"], 1)
                    pe.wait_ge(s["sel_o_ready"], 1)
                    for c in range(4):
                        nc.tensor.matmul(ps_m[0:64, M_O], pwinT[:, c, :], vw_in[:, c, :], start=c == 0, stop=False)
                    nc.tensor.matmul(ps_m[0:64, M_O], pwinnT[:, :], new_in[:, 3, :], start=False, stop=True).then_inc(s["win_o"], 1)

                @block.scalar
                def _(act):
                    def silu(m, done, hidden):
                        act.wait_ge(s[hidden], 2)
                        if m == 1:
                            act.wait_ge(s["prod_k"], 1)
                        for c in range(2):
                            nc.scalar.activation(hid[:, c, :, :],
                                                 ps_h[:, c * 256:c * 256 + 2 * NCS].rearrange("p (g b) -> p g b", g=2),
                                                 ACT.Silu, bias=comp.bias[:, m, c:c + 1]).then_inc(s[done], 1)
                    copy_group(act, nc.scalar.copy, 0)
                    copy_pieces_k(act, nc.scalar.copy, 0)
                    for g in range(2, G_CV, 2):
                        copy_group(act, nc.scalar.copy, g)
                    silu(0, "act_k", "hid_k")
                    copy_group(act, nc.scalar.copy, G_CV)
                    copy_group(act, nc.scalar.copy, G_CV + 2)
                    act.wait_ge(s["cmp_max"], 1)
                    nc.scalar.activation(pc[:, :], ps_m[0:64, M_CS], ACT.Exp, scale=-1.0, bias=stat[:, 0, 0:1],
                                         accum_out=stat[:, 0, 1:2]).then_inc(s["cmp_probs"], 1)
                    copy_group(act, nc.scalar.copy, G_PC)
                    act.wait_ge(s["sel_max"], 1)
                    nc.scalar.activation(psel[:, :], psel[:, :], ACT.Exp, scale=-1.0, bias=stat[:, 1, 0:1],
                                         accum_out=stat[:, 1, 1:2]).then_inc(s["sel_probs"], 1)
                    act.wait_ge(s["win_max"], 1)
                    nc.scalar.activation(pwin[:, :], pwin[:, :], ACT.Exp, scale=-1.0, bias=stat[:, 2, 0:1],
                                         accum_out=stat[:, 2, 1:2]).then_inc(s["win_probs"], 1)
                    silu(1, "act_v", "hid_v")
                    copy_group(act, nc.scalar.copy, G_PS)
                    copy_group(act, nc.scalar.copy, G_PW)

                @block.vector
                def _(dve):
                    count = 0

                    def link(ins):
                        nonlocal count
                        count += 1
                        ins.then_inc(s["dve_step"], 1)
                        dve.wait_ge(s["dve_step"], count)

                    def write_out(b, done, ready):
                        if b == 0:
                            dve.wait_ge(s["windows_in"], 1)
                        dve.wait_ge(s[done], 1)
                        for g in range(2):
                            r = slice(32 * g, 32 * g + 32)
                            src = ps_m[r, M_O.start + g * HD:M_O.start + (g + 1) * HD]
                            if b == 0:
                                last = nc.vector.tensor_copy(o[r, b, :], src)
                            else:
                                last = nc.vector.tensor_scalar(o[r, b, :], src, stat[r, b, 2:3], None, ALU.mult)
                        last.then_inc(s[ready], 1)
                    nc.vector.tensor_copy(q_cur[:, :], q_all[:, bass.ds(n, 1), :].rearrange("p n c -> p (n c)")).then_inc(s["q_ready"], 1)
                    copy_pieces_k(dve, nc.vector.tensor_copy, 1)
                    for g in range(1, G_CV, 2):
                        copy_group(dve, nc.vector.tensor_copy, g)
                    dve.wait_ge(s["sel_scores"], 1)
                    for x, dst in enumerate((psel[:, PAST:NKEY], pwin[:, 512:512 + NJ])):
                        last = nc.vector.tensor_tensor_reduce(out=dst, in0=ps_m[0:64, M_NEW.start + x * NJ:M_NEW.start + (x + 1) * NJ],
                                                              in1=con("newmask"), scale=1.0, scalar=3e38, op0=ALU.add,
                                                              op1=ALU.min, accum_out=mins[:, 4 + x:5 + x])
                    last.then_inc(s["new_read"], 1)
                    dve.wait_ge(s["prod_k"], 1)
                    nc.vector.tensor_copy(kc[:, :], ps_m[:, 0:NCS]).then_inc(s["kc_ready"], 1)
                    copy_group(dve, nc.vector.tensor_copy, G_CV + 1)
                    dve.wait_ge(s["cmp_scores"], 1)
                    nc.vector.tensor_reduce(stat[:, 0, 0:1], ps_m[0:64, M_CS], AX, ALU.min).then_inc(s["cmp_max"], 1)
                    copy_group(dve, nc.vector.tensor_copy, G_CV + 3)
                    dve.wait_ge(s["cmp_probs"], 1)
                    link(nc.vector.reciprocal(stat[:, 0, 2:3], stat[:, 0, 1:2]))
                    nc.vector.tensor_scalar(pc[:, :], pc[:, :], stat[:, 0, 2:3], None, ALU.mult).then_inc(s["cmp_norm"], 1)
                    dve.wait_ge(s["share_raw"], 1)
                    nc.vector.tensor_copy(share[:, :], ps_m[0:64, M_SH]).then_inc(s["share_ready"], 1)
                    dve.wait_ge(s["turned"], G_WS + 1)
                    nc.vector.tensor_tensor_reduce(out=pwin[:, 0:512], in0=ps_t[G_WS % 2][0:64, :], in1=con("winmask"), scale=1.0,
                                                   scalar=3e38, op0=ALU.add, op1=ALU.min,
                                                   accum_out=mins[:, 6:7]).then_inc(copied[G_WS % 2], 1)
                    dve.wait_ge(copied[G_WS % 2], G_WS // 2 + 1)
                    nc.vector.tensor_reduce(stat[:, 2, 0:1], mins[:, 5:7], AX, ALU.min).then_inc(s["win_max"], 1)
                    dve.wait_ge(s["sum_raw"], 1)
                    nc.vector.tensor_copy(score[:, :], ps_m[0:64, M_SUM]).then_inc(s["sum_read"], 1)
                    dve.wait_ge(s["sum_read"], 1)
                    nc.vector.memset(score[:, 0:1], 1e9)
                    link(nc.vector.memset(score[:, 31:33], 1e9))
                    link(nc.vector.max(top[:, :], score[:, :]))
                    link(nc.vector.match_replace(score2[:, :], top[:, :], score[:, :], -3e38))
                    link(nc.vector.max(top[:, :], score2[:, :]))
                    link(nc.vector.match_replace(score[:, :], top[:, :], score2[:, :], -3e38))
                    link(nc.vector.tensor_scalar(bias_b[:, :], score[:, :], -1e37, BIG, ALU.is_gt, ALU.mult))
                    link(nc.vector.tensor_copy(bias[:, :, :], bias_b[:, 0:32].unsqueeze(2).broadcast_to([64, 32, 4])))
                    dve.wait_ge(s["sel_scores"], 1)
                    fb = bias[:, :, :].rearrange("p b s -> p (b s)").unsqueeze(1).broadcast_to([64, 4, P])
                    for c in range(4):
                        last = nc.vector.tensor_tensor_reduce(out=psel[:, c * 512:(c + 1) * 512].rearrange("p (s k) -> p s k", s=4),
                                                       in0=ps_s[:, c, :].rearrange("p (s k) -> p s k", s=4), in1=fb,
                                                       scale=1.0, scalar=3e38, op0=ALU.add, op1=ALU.min,
                                                       accum_out=mins[:, c:c + 1])
                        last.then_inc(s["dve_step"], 1)
                        count += 1
                    dve.wait_ge(s["dve_step"], count)
                    nc.vector.tensor_reduce(stat[:, 1, 0:1], mins[:, 0:5], AX, ALU.min).then_inc(s["sel_max"], 1)
                    copy_group(dve, nc.vector.tensor_copy, G_PS + 1)
                    dve.wait_ge(s["prod_v"], 1)
                    nc.vector.tensor_copy(vc[:, :], ps_m[0:NCS, M_KC]).then_inc(s["vc_ready"], 1)
                    write_out(0, "cmp_o", "cmp_o_ready")
                    dve.wait_ge(s["sel_probs"], 1)
                    dve.wait_ge(s["win_probs"], 1)
                    link(nc.vector.reciprocal(stat[:, 1:3, 2], stat[:, 1:3, 1]))
                    write_out(1, "sel_o", "sel_o_ready")
                    write_out(2, "win_o", "win_o_ready")
            next_round(nc, sems)

        with nc.Block() as block:
            @block.sync
            def _(sp):
                sp.wait_ge(stored, (NB + 1) * 48)
                sp.wait_ge(win_in, (NB + 1) * 48)

            @block.gpsimd
            def _(pool):
                for which in ("ks", "kc", "vc"):
                    pool.wait_ge(gathers[which], (NB + 1) * 16)


def mix_sample_branches(nc, h_s, branches, mix_s):
    with Phase(nc) as ctx:
        b = ctx.enter_context(nc.sbuf_tensor("mb_b", [NS, 3, D], F32))
        gl = ctx.enter_context(nc.sbuf_tensor("mb_gl", [NS, 48], F32))
        out = ctx.enter_context(nc.sbuf_tensor("mb_out", [NS, D], F32))
        loaded, gates, step, ready, stored = (ctx.semaphore(f"mb_{n}") for n in "loaded gates step ready stored".split())
        n_loads = 1 + 3 * NB

        def load(eng, samples):
            for n in samples:
                for x in range(3):
                    eng.dma_start(b[n * NJ:(n + 1) * NJ, x, :].rearrange("j (h d) -> j h d", d=HD),
                                  branches[x, n * 64:(n + 1) * 64, :].rearrange("(h j) d -> j h d", j=NJ)).then_inc(loaded, 16)
        with nc.Block() as block:
            @block.sync
            def _(sp):
                sp.dma_start(gl[:, :], h_s[:, GL:GL + 48]).then_inc(loaded, 16)
                load(sp, range(0, NB, 2))
                sp.wait_ge(ready, 1)
                sp.dma_start(mix_s, out[:, :]).then_inc(stored, 16)
                sp.wait_ge(stored, 16)

            @block.scalar
            def _(act):
                load(act, range(1, NB, 2))
                act.wait_ge(loaded, 16 * n_loads)
                nc.scalar.activation(gl[:, :], gl[:, :], ACT.Sigmoid).then_inc(gates, 1)

            @block.vector
            def _(dve):
                dve.wait_ge(loaded, 16 * n_loads)
                dve.wait_ge(gates, 1)
                for x in range(3):
                    v = b[:, x, :].rearrange("t (h d) -> t h d", d=HD)
                    g = gl[:, :].rearrange("t (h x) -> t h x", x=3)[:, :, x].unsqueeze(2).broadcast_to([NS, 16, HD])
                    last = nc.vector.tensor_tensor(v, v, g, ALU.mult)
                last.then_inc(step, 1)
                dve.wait_ge(step, 1)
                nc.vector.tensor_tensor(out[:, :], b[:, 0, :], b[:, 1, :], ALU.add).then_inc(step, 1)
                dve.wait_ge(step, 2)
                nc.vector.tensor_tensor(out[:, :], out[:, :], b[:, 2, :], ALU.add).then_inc(ready, 1)


class Constants:

    def __init__(self, nc, ctx, dram):
        self.all = ctx.enter_context(nc.sbuf_tensor("constants", [P, CONST.shape[1]], F32))
        t16 = ctx.enter_context(nc.sbuf_tensor("constants16", [P, 3 * P + NT * NCB], BF16))
        self.ident16, self.causal16, self.edge16 = (t16[:, k * P:(k + 1) * P] for k in range(3))
        self.cmask16 = t16[:, 3 * P:].rearrange("p (t c) -> p t c", t=NT)
        self.rows = {n: P for n in COLS}
        self.rows.update(asbias=32, adiag=32, newmask=64, winmask=64, same=64, overlap=NCS, intra_s=NS, qdec_s=NS,
                         kdec_s=NS, kmask_s=NS)
        with Phase(nc) as phase, nc.Block() as block:
            loaded, cast = phase.semaphore("constants_in"), phase.semaphore("constants_cast")

            @block.sync
            def _(sp):
                sp.dma_start(self.all[:, :], dram).then_inc(loaded, 16)

            @block.vector
            def _(dve):
                dve.wait_ge(loaded, 16)
                for to, name in ((self.ident16, "ident"), (self.causal16, "causal"), (self.edge16, "edge"), (t16[:, 3 * P:], "cmask")):
                    last = nc.vector.tensor_copy(to, self(name))
                last.then_inc(cast, 1)
                dve.wait_ge(cast, 1)

    def __call__(self, name):
        a, b = COLS[name]
        return self.all[0:self.rows[name], a:b]


def build(nc, i, o):
    h0 = nc.dram_tensor("h0", [ROWS, E_COLS], F32, kind="Internal").ap()
    h1 = nc.dram_tensor("h1", [ROWS, O_COLS], F32, kind="Internal").ap()
    mix0 = nc.dram_tensor("mix0", [ROWS, D], F32, kind="Internal").ap()
    mix1 = nc.dram_tensor("mix1", [ROWS, D], F32, kind="Internal").ap()
    x1 = nc.dram_tensor("x1", [ROWS, D], F32, kind="Internal").ap()
    x2 = nc.dram_tensor("x2", [ROWS, D], F32, kind="Internal").ap()
    kcmp = nc.dram_tensor("kcmp", [P, NCB], F32, kind="Internal").ap()
    vcmp = nc.dram_tensor("vcmp", [NCB, P], F32, kind="Internal").ap()
    rows_s = nc.dram_tensor("rows_s", [NB * 32, HD], F32, kind="Internal").ap()
    branches = nc.dram_tensor("branches", [3, NB * 64, HD], F32, kind="Internal").ap()

    def both(a):
        return a[0:T, :], a[T:ROWS, :]
    with ExitStack() as ctx:
        con = Constants(nc, ctx, i["const"])
        gathers = {n: ctx.enter_context(nc.semaphore("gathered_" + n)) for n in ("kc", "vc", "ks", "vs")}
        ident = con("ident")
        x0 = (i["x_prompt"], i["x_sample"])
        project(nc, ident, "norm", x0, i["even_w_in"], E_COLS, both(h0), gain=i["even_norm"])
        stores = [(o["a_k_p"], h0[0:T, KA:KA + 512]), (o["a_k_s"], h0[T:, KA:KA + 512]),
                  (o["a_v_p"], h0[0:T, VA:VA + 512]), (o["a_v_s"], h0[T:, VA:VA + 512])]
        attend_prompt(nc, con, "dilated", both(h0), mix0, 4, stores)
        retain(nc, con, both(h0), mix0, i["trig"], o["ret_p"])
        retain(nc, con, both(h0), mix0, i["trig"], o["ret_s"], state_in=i["state_ret"])
        attend_samples_dilated(nc, con, h0[T:ROWS, :], i["cache_a_k"], i["cache_a_v"], rows_s, mix0)
        project(nc, ident, "gate", both(mix0), i["even_w_out"], D, both(x1),
                gates=(both(h0), (ZA, ZA + 512), (ZB, ZB + 512)), residual=x0)
        project(nc, ident, "norm", both(x1), i["odd_w_in"], O_COLS, both(h1), gain=i["odd_norm"])
        pairs = []
        for name, col in (("kc", KC), ("vc", VC), ("ks", KS), ("vs", VS), ("kw", KW), ("vw", VW)):
            first = T - 512 if name in ("kw", "vw") else 0
            pairs.append((o[name + "_p"], h1[first:T, col:col + P]))
            pairs.append((o[name + "_s"], h1[T:, col:col + P]))
        with ExitStack() as inner:
            comp = Compressor(nc, inner, con)
            comp.setup((i["cmp_w1_k"], i["cmp_w1_v"]), (i["cmp_w2_k"], i["cmp_w2_v"]), (i["cmp_pos_k"], i["cmp_pos_v"]))
            compress_prompt(nc, con, comp, both(h1), kcmp, vcmp)
            attend_samples_sparse(nc, con, comp, h1[T:ROWS, :], [i["pool_" + n] for n in ("kc", "vc", "ks", "vs")],
                                  (i["cache_c_kwin"], i["cache_c_vwin"]), i["page_table"], branches, gathers)
        mix_sample_branches(nc, h1[T:ROWS, :], branches, mix1[T:ROWS, :])
        attend_prompt(nc, con, "sparse", both(h1), mix1, 8, pairs, kcmp, vcmp)
        project(nc, ident, "gate", both(mix1), i["odd_w_out"], D, both(x2), gates=(both(h1), (ZC, ZC + D)), residual=both(x1))
        final_norm(nc, both(x2), i["final_norm"], (o["y_p"], o["y_s"]))


_IN = {"x_prompt": (T, D), "x_sample": (NS, D), "cache_a_k": (NB, PAST, 512), "cache_a_v": (NB, PAST, 512),
       "state_ret": (NB, BH, HD, BDV), "cache_c_kcmp": (NPOOL * 8, 2048), "cache_c_vcmp": (NPOOL * 8, 2048),
       "cache_c_ksel": (NPOOL * 8, 2048), "cache_c_vsel": (NPOOL * 8, 2048), "cache_c_kwin": (NB, 512, P),
       "cache_c_vwin": (NB, 512, P), "page_table": (NB, PAST // PAGE), "even_norm": (D,), "even_w_in": (D, E_COLS),
       "even_w_out": (D, D), "odd_norm": (D,), "odd_w_in": (D, O_COLS), "odd_w_out": (D, D), "cmp_pos_k": (32, HD),
       "cmp_w1_k": (2048, CH), "cmp_w2_k": (CH, HD), "cmp_pos_v": (32, HD), "cmp_w1_v": (2048, CH), "cmp_w2_v": (CH, HD),
       "final_norm": (D,)}
_OUT = [("y_p", (1, T, D)), ("y_s", (NB, NJ, D)), ("a_k_p", (1, 1, T, 8, HD)), ("a_k_s", (1, NB, NJ, 8, HD)),
        ("a_v_p", (1, 1, T, 8, HD)), ("a_v_s", (1, NB, NJ, 8, HD)), ("ret_p", (1, 1, BH, HD, BDV)),
        ("ret_s", (1, NB, BH, HD, BDV))] + [
    (f"{n}_{w}", ((1, 1, T // (2 if n in ("kw", "vw") else 1), 2, HD) if w == "p" else (1, NB, NJ, 2, HD)))
    for n in ("kc", "vc", "ks", "vs", "kw", "vw") for w in ("p", "s")]


def kernel(**inputs):
    import concourse.bacc as _bacc
    from concourse.bass_utils import run_bass_kernel_spmd as _run

    nc = _bacc.Bacc("TRN2", target_bir_lowering=False, num_devices=1)
    arrays, ins, outs = {}, {}, {}
    laid = {n: np.ascontiguousarray(inputs[n]).reshape(shape) for n, shape in _IN.items()}
    laid["const"], laid["trig"] = CONST, TRIG
    for name, a in laid.items():
        arrays["in_" + name] = a
        ins[name] = nc.dram_tensor("in_" + name, a.shape, mybir.dt.from_np(a.dtype), kind="ExternalInput").ap()
    for short, full in (("kc", "kcmp"), ("vc", "vcmp"), ("ks", "ksel"), ("vs", "vsel")):
        ins["pool_" + short] = ins["cache_c_" + full]
    flat = {"y_p": (T, D), "y_s": (NS, D), "ret_p": (BH, HD, BDV), "ret_s": (NB, BH, HD, BDV)}
    for name, shape in _OUT:
        cols = 512 if name[:2] == "a_" else P
        s2 = flat.get(name, (int(np.prod(shape)) // cols, cols))
        outs[name] = nc.dram_tensor("out_" + name, s2, F32, kind="ExternalOutput").ap()
    build(nc, ins, outs)
    r = _run(nc, [arrays], core_ids=[0])
    return tuple(r.results[0]["out_" + name].reshape(shape) for name, shape in _OUT)
```
